# Optimizing a Trainium2 kernel written in Bass

```python
import jax
import jax.numpy as jnp
from jax import lax
import numpy as np

D_MODEL = 1024
BATCH = 1
SEQ = 1024
DEPTH = 2

PLE_DIM = 256
HEAD_DIM = 128
A_HEADS = D_MODEL // HEAD_DIM
A_WIDTH = A_HEADS * HEAD_DIM
B_HEADS = D_MODEL // HEAD_DIM
B_WIDTH = B_HEADS * HEAD_DIM
MIX_HEADS = A_HEADS + B_HEADS
EVEN_WIDTH = A_WIDTH + B_WIDTH
EVEN_IN = 3 * A_WIDTH + 3 * B_WIDTH + 2 * B_HEADS + EVEN_WIDTH
LRU_WIDTH = 2 * D_MODEL
LRU_BLOCKS = 16
LRU_BLOCK = LRU_WIDTH // LRU_BLOCKS
LRU_C = 8.0
CONV_WIDTH = 4
CHUNK = 64
N_EVEN = (DEPTH + 1) // 2
N_ODD = DEPTH // 2
EPS = 1e-6

kernel_name = "hybrid_hgrn2_gdn_rglru_trunk"

def rmsnorm(x, g):
    xf = x.astype(jnp.float32)
    y = xf * lax.rsqrt(jnp.mean(xf * xf, axis=-1, keepdims=True) + EPS)
    return (y * g.astype(jnp.float32)).astype(x.dtype)

def head_rmsnorm(o, g):
    h, d = o.shape[-2], o.shape[-1]
    y = o * lax.rsqrt(jnp.mean(o * o, axis=-1, keepdims=True) + EPS)
    return y * g.astype(jnp.float32).reshape(h, d)

def l2norm(t):
    return t * lax.rsqrt(jnp.sum(t * t, axis=-1, keepdims=True) + EPS)

def causal_dwconv(x, w):
    return lax.conv_general_dilated(
        x, w.astype(jnp.float32)[:, None, :], window_strides=(1,),
        padding=((CONV_WIDTH - 1, 0),), dimension_numbers=("NWC", "WIO", "NWC"),
        feature_group_count=x.shape[-1])

def to_chunks(t):
    b, s, h = t.shape[:3]
    t = t.reshape((b, s // CHUNK, CHUNK, h) + t.shape[3:])
    return jnp.moveaxis(t, (1, 2, 3), (0, 3, 2))

def from_chunks(o):
    o = jnp.moveaxis(o, (0, 2, 3), (1, 3, 2))
    b, n, c, h, d = o.shape
    return o.reshape(b, n * c, h, d)

def hgrn2_chunked(q, k, v, log_f):
    b, _, h, dk = q.shape
    dv = v.shape[-1]
    tri = jnp.tril(jnp.ones((CHUNK, CHUNK), dtype=bool))

    def step(state, xs):
        q_c, k_c, v_c, g_c = xs
        cum = jnp.cumsum(g_c, axis=-2)
        rel = jnp.where(tri[:, :, None], cum[..., :, None, :] - cum[..., None, :, :], -jnp.inf)
        attn = jnp.einsum("bhtd,bhsd,bhtsd->bhts", q_c, k_c, jnp.exp(rel))
        o = (jnp.einsum("bhts,bhse->bhte", attn, v_c)
             + jnp.einsum("bhtd,bhde->bhte", q_c * jnp.exp(cum), state))
        last = cum[..., -1:, :]
        state = (jnp.exp(last[..., 0, :])[..., None] * state
                 + jnp.einsum("bhsd,bhse->bhde", k_c * jnp.exp(last - cum), v_c))
        return state, o

    s0 = jnp.zeros((b, h, dk, dv), jnp.float32)
    _, o = lax.scan(step, s0, (to_chunks(q), to_chunks(k), to_chunks(v), to_chunks(log_f)))
    return from_chunks(o)

def gated_delta_chunked(q, k, v, g, beta):
    b, _, h, dk = q.shape
    dv = v.shape[-1]
    qc, kc, vc = to_chunks(q), to_chunks(k), to_chunks(v)
    gcum = jnp.cumsum(to_chunks(g), axis=-1)
    bc = to_chunks(beta)
    tri = jnp.tril(jnp.ones((CHUNK, CHUNK), dtype=bool))
    strict = jnp.tril(jnp.ones((CHUNK, CHUNK), dtype=bool), -1)
    decay = jnp.exp(jnp.where(tri, gcum[..., :, None] - gcum[..., None, :], -jnp.inf))
    kb = kc * bc[..., None]
    vb = vc * bc[..., None]
    a_strict = jnp.where(strict, jnp.einsum("nbhtd,nbhsd->nbhts", kb, kc) * decay, 0.0)
    m = a_strict + jnp.eye(CHUNK, dtype=jnp.float32)
    u = lax.linalg.triangular_solve(m, vb, left_side=True, lower=True, unit_diagonal=True)
    w = lax.linalg.triangular_solve(m, kb * jnp.exp(gcum)[..., None], left_side=True,
                                    lower=True, unit_diagonal=True)
    qk = jnp.einsum("nbhtd,nbhsd->nbhts", qc, kc) * decay

    def step(state, xs):
        q_c, k_c, u_c, w_c, qk_c, g_c = xs
        v_new = u_c - jnp.einsum("bhtd,bhde->bhte", w_c, state)
        o = (jnp.einsum("bhtd,bhde->bhte", q_c * jnp.exp(g_c)[..., None], state)
             + jnp.einsum("bhts,bhse->bhte", qk_c, v_new))
        last = g_c[..., -1:]
        state = (state * jnp.exp(last)[..., None]
                 + jnp.einsum("bhsd,bhse->bhde", k_c * jnp.exp(last - g_c)[..., None], v_new))
        return state, o

    s0 = jnp.zeros((b, h, dk, dv), jnp.float32)
    _, o = lax.scan(step, s0, (qc, kc, u, w, qk, gcum))
    return from_chunks(o)

def even_layer(x, norm_g, w_in, lb, conv_w, a_log, dt_bias, head_g, w_out):
    bsz, s, _ = x.shape
    z = (rmsnorm(x, norm_g) @ w_in).astype(jnp.float32)
    o1 = A_WIDTH
    o2 = 2 * A_WIDTH
    o3 = 3 * A_WIDTH
    o4 = o3 + 3 * B_WIDTH
    o5 = o4 + B_HEADS
    o6 = o5 + B_HEADS
    a_q, a_f, a_i = z[..., :o1], z[..., o1:o2], z[..., o2:o3]
    b_qkv, b_a, b_b, gate = z[..., o3:o4], z[..., o4:o5], z[..., o5:o6], z[..., o6:]

    lb = lb.astype(jnp.float32)
    log_f = jnp.logaddexp(jnp.log(lb), jnp.log1p(-lb) + jax.nn.log_sigmoid(a_f))
    a_k = (1.0 - lb) * jax.nn.sigmoid(-a_f)
    hd = (bsz, s, A_HEADS, HEAD_DIM)
    o_a = hgrn2_chunked(a_q.reshape(hd), a_k.reshape(hd), a_i.reshape(hd), log_f.reshape(hd))

    qkv = jax.nn.silu(causal_dwconv(b_qkv, conv_w))
    hb = (bsz, s, B_HEADS, HEAD_DIM)
    q = l2norm(qkv[..., :B_WIDTH].reshape(hb)) * (HEAD_DIM ** -0.5)
    k = l2norm(qkv[..., B_WIDTH:2 * B_WIDTH].reshape(hb))
    v = qkv[..., 2 * B_WIDTH:].reshape(hb)
    beta = jax.nn.sigmoid(b_b)
    g = -jnp.exp(a_log.astype(jnp.float32)) * jax.nn.softplus(b_a + dt_bias.astype(jnp.float32))
    o_b = gated_delta_chunked(q, k, v, g, beta)

    o = head_rmsnorm(jnp.concatenate([o_a, o_b], axis=2), head_g)
    y = o.reshape(bsz, s, EVEN_WIDTH) * jax.nn.silu(gate)
    return y.astype(x.dtype) @ w_out

def _lin_combine(c1, c2):
    a1, b1 = c1
    a2, b2 = c2
    return a1 * a2, a2 * b1 + b2

def odd_layer(x, norm_g, w_in, conv_w, conv_b, w_a, b_a, w_x, b_x, lam, w_out):
    bsz, s, _ = x.shape
    z = (rmsnorm(x, norm_g) @ w_in).astype(jnp.float32)
    xb, gate = z[..., :LRU_WIDTH], z[..., LRU_WIDTH:]
    xc = causal_dwconv(xb, conv_w) + conv_b.astype(jnp.float32)
    xh = xc.reshape(bsz, s, LRU_BLOCKS, LRU_BLOCK)
    r = jax.nn.sigmoid(jnp.einsum("bsgi,gij->bsgj", xh, w_a.astype(jnp.float32)).reshape(bsz, s, LRU_WIDTH)
                       + b_a.astype(jnp.float32))
    i = jax.nn.sigmoid(jnp.einsum("bsgi,gij->bsgj", xh, w_x.astype(jnp.float32)).reshape(bsz, s, LRU_WIDTH)
                       + b_x.astype(jnp.float32))
    log_a = -LRU_C * r * jax.nn.softplus(-lam.astype(jnp.float32))
    a = jnp.exp(log_a)
    mult = jnp.sqrt(-jnp.expm1(2.0 * log_a))
    mult = jnp.where(jnp.arange(s)[None, :, None] == 0, 1.0, mult)
    _, h = lax.associative_scan(_lin_combine, (a, xc * i * mult), axis=1)
    y = h * jax.nn.silu(gate)
    return y.astype(x.dtype) @ w_out

def setup_inputs(seed: int = 0) -> dict:
    key = jax.random.key(seed)
    ks = jax.random.split(key, 24)
    f32 = jnp.float32
    nrm = lambda k, shp: jax.random.normal(k, shp, f32)
    dt = jnp.exp(jax.random.uniform(ks[7], (N_EVEN, B_HEADS), f32,
                                    minval=float(np.log(1e-3)), maxval=float(np.log(1e-1))))
    a_base = jax.random.uniform(ks[18], (N_ODD, LRU_WIDTH), f32, minval=0.9, maxval=0.999)
    sig = a_base ** (1.0 / LRU_C)
    return {
        "x": nrm(ks[0], (BATCH, SEQ, D_MODEL)),
        "p": nrm(ks[1], (DEPTH, BATCH, SEQ, PLE_DIM)),
        "even_norm": 1.0 + 0.02 * nrm(ks[2], (N_EVEN, D_MODEL)),
        "even_w_in": nrm(ks[3], (N_EVEN, D_MODEL, EVEN_IN)) * D_MODEL ** -0.5,
        "hgrn_lb_logits": 0.5 * nrm(ks[4], (N_EVEN, A_WIDTH)),
        "gdn_conv_w": nrm(ks[5], (N_EVEN, CONV_WIDTH, 3 * B_WIDTH)) * CONV_WIDTH ** -0.5,
        "gdn_a_log": jnp.log(jax.random.uniform(ks[6], (N_EVEN, B_HEADS), f32, minval=1.0, maxval=16.0)),
        "gdn_dt_bias": dt + jnp.log(-jnp.expm1(-dt)),
        "even_head_norm": 1.0 + 0.02 * nrm(ks[8], (N_EVEN, EVEN_WIDTH)),
        "even_w_out": nrm(ks[9], (N_EVEN, EVEN_WIDTH, D_MODEL)) * EVEN_WIDTH ** -0.5,
        "odd_norm": 1.0 + 0.02 * nrm(ks[10], (N_ODD, D_MODEL)),
        "odd_w_in": nrm(ks[11], (N_ODD, D_MODEL, 2 * LRU_WIDTH)) * D_MODEL ** -0.5,
        "lru_conv_w": nrm(ks[12], (N_ODD, CONV_WIDTH, LRU_WIDTH)) * CONV_WIDTH ** -0.5,
        "lru_conv_b": 0.01 * nrm(ks[13], (N_ODD, LRU_WIDTH)),
        "lru_w_a": nrm(ks[14], (N_ODD, LRU_BLOCKS, LRU_BLOCK, LRU_BLOCK)) * LRU_BLOCK ** -0.5,
        "lru_b_a": 0.01 * nrm(ks[15], (N_ODD, LRU_WIDTH)),
        "lru_w_x": nrm(ks[16], (N_ODD, LRU_BLOCKS, LRU_BLOCK, LRU_BLOCK)) * LRU_BLOCK ** -0.5,
        "lru_b_x": 0.01 * nrm(ks[17], (N_ODD, LRU_WIDTH)),
        "lru_lambda": jnp.log(sig) - jnp.log1p(-sig),
        "odd_w_out": nrm(ks[19], (N_ODD, LRU_WIDTH, D_MODEL)) * LRU_WIDTH ** -0.5,
        "ple_norm": 1.0 + 0.02 * nrm(ks[20], (DEPTH, D_MODEL)),
        "ple_gate_w": nrm(ks[21], (DEPTH, D_MODEL, D_MODEL)) * D_MODEL ** -0.5,
        "ple_proj_w": nrm(ks[22], (DEPTH, PLE_DIM, D_MODEL)) * (0.5 * PLE_DIM ** -0.5),
        "final_norm": 1.0 + 0.02 * nrm(ks[23], (D_MODEL,)),
    }

def reference(x, p, even_norm, even_w_in, hgrn_lb_logits, gdn_conv_w, gdn_a_log, gdn_dt_bias,
              even_head_norm, even_w_out, odd_norm, odd_w_in, lru_conv_w, lru_conv_b, lru_w_a,
              lru_b_a, lru_w_x, lru_b_x, lru_lambda, odd_w_out, ple_norm, ple_gate_w, ple_proj_w,
              final_norm):
    lb_cum = jnp.cumsum(jax.nn.softmax(hgrn_lb_logits.astype(jnp.float32), axis=0), axis=0)
    lower_bounds = lb_cum - lb_cum[0]
    for i in range(DEPTH):
        j = i // 2
        if i % 2 == 0:
            x = x + even_layer(x, even_norm[j], even_w_in[j], lower_bounds[j], gdn_conv_w[j],
                               gdn_a_log[j], gdn_dt_bias[j], even_head_norm[j], even_w_out[j])
        else:
            x = x + odd_layer(x, odd_norm[j], odd_w_in[j], lru_conv_w[j], lru_conv_b[j], lru_w_a[j],
                              lru_b_a[j], lru_w_x[j], lru_b_x[j], lru_lambda[j], odd_w_out[j])
        ple_gate = jax.nn.sigmoid(rmsnorm(x, ple_norm[i]) @ ple_gate_w[i])
        x = x + ple_gate * (p[i] @ ple_proj_w[i])
    return rmsnorm(x, final_norm)


_drawn_inputs = setup_inputs


def setup_inputs(seed=0):
    import zlib

    import numpy as np

    out = dict(_drawn_inputs(seed))
    spreads = {}
    factors = {'even_norm': 2.706,
     'even_head_norm': 5.336,
     'odd_norm': 6.074,
     'lru_b_a': 64.0,
     'lru_b_x': 45.023,
     'ple_norm': 64.0,
     'final_norm': 8.466,
     'lru_conv_b': 8.0}
    for name, (base, spread) in spreads.items():
        noise = np.random.default_rng([zlib.crc32(name.encode()), seed]).standard_normal(out[name].shape)
        drawn = base * np.exp(spread * noise) if base else spread * noise
        out[name] = jnp.asarray(drawn.astype(out[name].dtype))
    for name, factor in factors.items():
        out[name] = (out[name] * factor).astype(out[name].dtype)
    return out
```

```python
from contextlib import ExitStack

import concourse.bass as bass
from concourse import mybir

F32 = mybir.dt.float32
F32R = mybir.dt.float32r
U8 = mybir.dt.uint8
ACT = mybir.ActivationFunctionType
ALU = mybir.AluOpType

P = 128
HALF = 512
CHUNK = 128
LEVELS = 7
EPS = 1e-6
TAPS = 4
PAD = TAPS - 1


class Step:

    def __init__(self, sem, per_turn):
        self.sem, self.per_turn = sem, per_turn

    def at(self, turn, n):
        return turn * self.per_turn + n


def after(eng, step, turn, n):
    eng.wait_ge(step.sem, step.at(turn, n))


def spread(pieces, points):
    return [pieces * (n + 1) // points for n in range(points)]


def build_trunk(nc, x_in, p_in, even_norm, even_w_in, lb_logits, gdn_conv_w, gdn_a_log, gdn_dt_bias,
                even_head_norm, even_w_out, odd_norm, odd_w_in, lru_conv_w, lru_conv_b, lru_w_a,
                lru_b_a, lru_w_x, lru_b_x, lru_lambda, odd_w_out, ple_norm, ple_gate_w, ple_proj_w,
                final_norm, out):
    _, T, D = x_in.shape
    KD = D // P
    NC = T // CHUNK
    HC = NC // 2
    HEADS = D // P
    BLOCKS = lru_w_a.shape[1]
    KP = p_in.shape[3] // P
    AW = HEADS * P
    GATE0 = 6 * AW + 2 * HEADS
    assert T == 2 * HALF and KD == 8 and NC == 8 and HEADS == 8 and BLOCKS == 2 * HEADS and KP == 2

    with ExitStack() as ctx:
        def sb(name, shape, dt=F32):
            return ctx.enter_context(nc.sbuf_tensor(name, shape, dt))

        def sem(name):
            return ctx.enter_context(nc.semaphore(name))

        def step(name, per_turn):
            return Step(sem(name), per_turn)

        x = sb("x", [P, KD, T])
        xh = sb("xh", [P, KD, T], F32R)
        xl = sb("xl", [P, KD, T], F32R)
        yh = sb("yh", [P, 2, T], F32R)
        yl = sb("yl", [P, 2, T], F32R)
        w_stage = sb("w_stage", [P, T])
        w_high = sb("w_high", [P, 2, T], F32R)
        w_low = sb("w_low", [P, 2, T], F32R)
        za = sb("za", [P, 5, T])
        zb = sb("zb", [P, 3, PAD + T + 1])
        zg = sb("zg", [P, T])
        cv = sb("cv", [P, 3, T])
        w1 = sb("w1", [P, T])
        w2 = sb("w2", [P, T])
        w3 = sb("w3", [P, T])
        rows = sb("rows", [64, T])
        cols = sb("cols", [P, 2 * P + 32])
        lows = sb("lows", [P, 4, HEADS])
        unit_cols = sb("unit_cols", [P, 2, 16])
        gcols = sb("gcols", [P, 2, NC, HEADS])
        head_cols = sb("head_cols", [P, 6, NC])
        state = sb("state", [P, 2, P])
        ident = sb("ident", [P, P])
        upper = sb("upper", [P, P])
        ones = sb("ones", [P, P])
        masks = sb("masks", [P, 2 * LEVELS + 1, P], U8)
        tiny = sb("tiny", [P, 4])

        dense = [ctx.enter_context(nc.psum_tensor(f"dense{i}", [P, HALF], F32)) for i in range(4)]
        work = [ctx.enter_context(nc.psum_tensor(f"work{i}", [P, HALF], F32)) for i in range(4)]

        def half(t, h):
            return t[:, h * HALF:(h + 1) * HALF]

        def chunk(t, c):
            return t[:, c * CHUNK:(c + 1) * CHUNK]

        def in_half(bank, c):
            return bank[:, (c % HC) * CHUNK:(c % HC + 1) * CHUNK]

        q_a, f_a, v_a, gate_a, k_a = (za[:, n, :] for n in range(5))
        q_b, k_b, v_b = (cv[:, n, :] for n in range(3))
        raw = [zb[:, n, PAD:PAD + T] for n in range(3)]
        tiles8 = [za[:, n, :] for n in range(5)] + [cv[:, n, :] for n in range(3)]

        C_CONV, C_HEAD, C_NORM, C_LB = 0, TAPS * 3 * HEADS, TAPS * 3 * HEADS + 2 * HEADS, P - HEADS
        C_ODD = P
        C_TAIL = 2 * P
        NORMS = [C_NORM, C_TAIL + 8, C_TAIL, C_TAIL + 16, C_TAIL + 24]

        def pairs(i):
            return head_cols[:, :, :].rearrange("p a c -> p (a c)")[:, i * BLOCKS:(i + 1) * BLOCKS]

        def gate_tile(n):
            return za[:, n, :] if n < 5 else (w1, w2, zg)[n - 5][:, :]

        MADE = 6 + 6 * LEVELS + 2

        made = step("constants_made", 0)
        cleared = step("padding_cleared", 0)
        small_in = step("small_inputs_loaded", 0)
        vec_in = step("vectors_loaded", 0)
        vec_turned = step("vectors_turned", 0)
        vec_kept = step("vectors_kept", 0)
        vec_ready = step("vector_work_done", 0)
        x_loaded = step("x_loaded", 0)
        x_turned = step("x_turned", 0)
        x_kept = step("x_kept", 0)
        masks_ready = step("masks_ready", 0)
        split_begun = step("split_begun", 0)
        select_begun = step("select_begun", 0)
        w_in = step("weights_loaded", 0)
        w_split_high = step("weights_split_high", 0)
        w_split = step("weights_split", 0)
        dense_ready = step("dense_ready", 0)
        taken = [step(f"dense_taken{n}", 0) for n in range(2)]
        norm_squared = step("norm_squared", KD)
        norm_summed = step("norm_summed", KD)
        norm_rooted = step("norm_rooted", 2)
        norm_inverse = step("norm_inverse", 2)
        norm_scaled = step("norm_scaled", KD)
        norm_high = step("norm_high", KD)
        norm_low = step("norm_low", KD)
        row_step = step("row_step_scalar", 0)
        row_vec = step("row_step_vector", 0)
        row_turned = step("rows_turned", 0)
        row_cols = step("row_columns_kept", 0)
        z_ready = [step("unit_a_projected", 4), step("unit_b_projected", 4)]
        a_gates = step("hgrn_gates", 3)
        a_cols = step("hgrn_columns", 1)
        a_bounded = step("hgrn_bounded", 3)
        a_scores = step("hgrn_scores", 1 + LEVELS)
        a_kept = step("hgrn_scores_kept", 2 + LEVELS)
        a_scaled = step("hgrn_scaled", 1 + 3 * LEVELS)
        a_turned = step("hgrn_turned", 4)
        a_values = step("hgrn_values_turned", 2)
        a_keys = step("hgrn_keys_turned", 2)
        a_kv = step("hgrn_key_values", 2)
        a_state = step("hgrn_states", NC - 1)
        mixed = [step("hgrn_mixed", 2), step("gdn_mixed", 2)]
        o_kept = [step("hgrn_output_kept", 4), step("gdn_output_kept", 4)]
        o_summed = [step("hgrn_output_summed", 2), step("gdn_output_summed", 2)]
        o_rooted = [step("hgrn_output_rooted", 2), step("gdn_output_rooted", 2)]
        o_scaled = [step("hgrn_output_scaled", 3), step("gdn_output_scaled", 3)]
        y_high = [step("hgrn_y_high", 1), step("gdn_y_high", 1)]
        y_ready = [step("hgrn_y_ready", 1), step("gdn_y_ready", 1)]
        b_cols = step("gdn_columns", 5)
        b_conv = step("gdn_convolved", 3 * TAPS)
        b_silu = step("gdn_silu", 4)
        b_squared = step("gdn_squared", 2)
        b_summed = step("gdn_summed", 4)
        b_rooted = step("gdn_rooted", 4)
        b_normed = step("gdn_normed", 4)
        b_rows = step("gdn_rows_picked", 2)
        b_spread = step("gdn_rows_spread", 2)
        b_decay = step("gdn_decay_rows", 2)
        b_keyed = step("gdn_keys_scaled", 2)
        b_diff = step("gdn_decay_differences", NC + 2)
        b_exp = step("gdn_decay_exponentials", 3)
        b_masked = step("gdn_decays_masked", 1)
        b_prod = step("gdn_products", 4)
        b_scores = step("gdn_scores", 4)
        b_qdec = step("gdn_queries_decayed", 1)
        b_turned = step("gdn_turned", 4)
        b_vk = step("gdn_values_and_keys_turned", 4)
        b_ident = step("inverse_started", 2)
        b_u = step("inverse_right_factor", 2 * LEVELS)
        b_ukept = step("inverse_right_factor_kept", 2 * (LEVELS - 1))
        b_y = step("inverse_products", 2 * (2 * (LEVELS - 1)) - 2)
        b_inv = step("inverse_grown", 4 * LEVELS - 2)
        c_ks = step("chain_read_state", NC - 1)
        c_r = step("chain_residue", NC - 1)
        c_v = step("chain_value", NC)
        c_vn = step("chain_value_kept", NC)
        c_kv = step("chain_state_change", NC - 1)
        c_state = step("chain_state", NC - 1)
        l_in = [step(f"lru{u}_weights_loaded", 32) for u in range(2)]
        l_cols = [step(f"lru{u}_columns", 1) for u in range(2)]
        l_silu = [step(f"lru{u}_gate_silu", 1) for u in range(2)]
        l_conv = [step(f"lru{u}_convolved", TAPS) for u in range(2)]
        l_gates = [step(f"lru{u}_gate_products", 2) for u in range(2)]
        l_sig = [step(f"lru{u}_gates", 4) for u in range(2)]
        l_exp = [step(f"lru{u}_decays", 2) for u in range(2)]
        l_vec = [step(f"lru{u}_vector_steps", 7) for u in range(2)]
        l_root = [step(f"lru{u}_rooted", 1) for u in range(2)]
        l_high = [step(f"lru{u}_y_high", 1) for u in range(2)]
        l_y = [step(f"lru{u}_y_ready", 1) for u in range(2)]
        lz_ready = [step(f"lru{u}_projected", 2) for u in range(2)]
        l_lam = step("lambda_steps", 0)
        p_loaded = step("ple_input_loaded", 0)
        p_turned = step("ple_input_turned", 4)
        p_high = step("ple_input_high", 4)
        p_low = step("ple_input_low", 4)
        p_gate = step("ple_gates", KD)
        p_prod = step("ple_gated", 2 * KD)
        p_added = step("ple_added", KD)
        f_scaled = step("final_scaled", KD)
        f_turned = step("final_turned", 2 * NC)
        f_kept = step("final_kept", 2 * NC)
        stored = [step(f"output{n}_stored", 0) for n in range(2)]

        def proj(u, n):
            return [("P", u, i) for i in range(n)]

        def outp(u):
            return [("O", u, n) for n in range(KD)]

        def turn_steps(n, last):
            return [proj(1, n), outp(0) + ([] if last else proj(0, n)), outp(1)]

        def n_steps(n):
            return sum(len(w) for w in turn_steps(n, False))

        class Place:

            def __init__(self, step0, tile0, steps=0, tiles=0, turn=0):
                self.step0, self.tile0, self.steps, self.tiles, self.turn = step0, tile0, steps, tiles, turn

            def ready(self, local):
                return self.turn * self.steps + (self.step0 + local + 1)

            def pair(self, local):
                return (self.step0 + local) % 2

            def taken(self, local):
                s = self.step0 + local
                return self.turn * (self.steps // 2) + (s - s % 2) // 2 + 1

            def split(self, local):
                return self.turn * self.tiles + (self.tile0 + local + 1)

            def slot(self, local):
                return (self.tile0 + local) % 2

        def tile_of(steps, local):
            t = -1
            for kind, _, n in steps[:local + 1]:
                t += kind in "PG" or n == 0
            return t

        EVEN_N, ODD_N = 4, 2
        PRE_EVEN = Place(0, 0)
        EVEN = lambda turn: Place(1 + EVEN_N, 1 + EVEN_N, n_steps(EVEN_N), 2 * EVEN_N + 2, turn)
        after_even = (1 + HEADS * n_steps(EVEN_N), 1 + HEADS * (2 * EVEN_N + 2))
        PLE_STEPS = [("G", 0, n) for n in range(KD)] + [("J", 0, n) for n in range(KD)]
        PLE_TILES = KD + KP
        PLE0 = Place(*after_even)
        after_ple0 = (after_even[0] + 2 * KD, after_even[1] + PLE_TILES)
        PRE_ODD = Place(*after_ple0)
        ODD = lambda turn: Place(after_ple0[0] + ODD_N, after_ple0[1] + ODD_N, n_steps(ODD_N), 2 * ODD_N + 2, turn)
        TURNS = BLOCKS // 2
        after_odd = (after_ple0[0] + TURNS * n_steps(ODD_N), after_ple0[1] + TURNS * (2 * ODD_N + 2))
        PLE1 = Place(*after_odd)
        TILES = after_odd[1] + PLE_TILES

        def turns(eng, count, body):
            with eng.Fori(0, count - 1) as turn:
                body(turn, False)
            body(count - 1, True)

        FILLS_A, FILLS_B, FILLS_L = 13, 24, 5

        class Filler:

            def __init__(self, window, local0, place, steps, points, piece, done):
                self.pieces = [(i, k) for i, s in enumerate(window) for k in range(KD if s[0] == "P" else 1)]
                self.upto = spread(len(self.pieces), points)
                self.at = self.point = 0
                self.window, self.local0, self.place, self.steps = window, local0, place, steps
                self.piece, self.done = piece, done

            def __call__(self):
                while self.at < self.upto[self.point]:
                    i, k = self.pieces[self.at]
                    last = k == (KD - 1 if self.window[i][0] == "P" else 0)
                    if self.piece:
                        self.piece(self.window[i], self.local0 + i, k, last, self.place, self.steps)
                    if self.done and last:
                        self.done(self.window[i], self.local0 + i, self.place)
                    self.at += 1
                self.point += 1

            def finish(self):
                assert self.point == len(self.upto) and self.at == len(self.pieces)

        block = ctx.enter_context(nc.Block())

        @block.sync
        def _(sp):
            def load_rows(src, slot, at):
                n = src.shape[0]
                sp.dma_start(w1[at:at + n, slot * P:(slot + 1) * P], src).then_inc(vec_in.sem, 16)

            load_rows(gdn_conv_w[0].rearrange("t (m q) -> (t m) q", q=P), 0, C_CONV)
            load_rows(even_head_norm[0].rearrange("(m q) -> m q", q=P), 0, C_HEAD)
            load_rows(even_norm[0].rearrange("(m q) -> m q", q=P), 0, C_NORM)
            load_rows(lb_logits[0].rearrange("(m q) -> m q", q=P), 0, C_LB)
            load_rows(lru_conv_w[0].rearrange("t (m q) -> (t m) q", q=P), 1, 0)
            for i, v in enumerate((lru_conv_b, lru_b_a, lru_b_x, lru_lambda)):
                load_rows(v[0].rearrange("(m q) -> m q", q=P), 1, (TAPS + i) * BLOCKS)
            load_rows(odd_norm[0].rearrange("(m q) -> m q", q=P), 2, 0)
            load_rows(ple_norm.rearrange("d (m q) -> (d m) q", q=P), 2, 8)
            load_rows(final_norm.rearrange("(m q) -> m q", q=P), 2, 24)
            for c in range(NC):
                sp.dma_start(tiles8[c], x_in[0, c * P:(c + 1) * P, :]).then_inc(x_loaded.sem, 16)
            sp.dma_start(tiny[0:HEADS, 1:2], gdn_a_log.rearrange("a (h b) -> (a h) b", b=1)).then_inc(small_in.sem, 16)
            sp.dma_start(tiny[0:HEADS, 2:3], gdn_dt_bias.rearrange("a (h b) -> (a h) b", b=1)).then_inc(small_in.sem, 16)

            def load(src, before, width=P):
                if before is not None:
                    sp.wait_ge(w_split.sem, before)
                dst = w_stage[:, :] if len(src.shape) == 2 else w_stage[:, :].rearrange("p (k n) -> p k n", n=P)
                sp.dma_start(dst, src).then_inc(w_in.sem, 16)

            def columns(w, at):
                return w[:, at].rearrange("(k p) n -> p k n", p=P)

            w_even = even_w_in[0]
            sp.wait_ge(cleared.sem, 1)
            stage3 = w_stage[:, :].rearrange("p (k n) -> p k n", n=P)
            for i, at in enumerate((0, 32)):
                sp.dma_start(stage3[:, :, at:at + HEADS],
                             w_even[:, 6 * AW + i * HEADS:6 * AW + (i + 1) * HEADS].rearrange("(k p) n -> p k n", p=P))\
                    .then_inc(w_in.sem, 16)
            starts = ([0, AW, 2 * AW, GATE0], [3 * AW, 4 * AW, 5 * AW, GATE0 + AW])

            def even_columns(u, n, head):
                return w_even[:, bass.ds(starts[u][n] + head * P, P)].rearrange("(k p) n -> p k n", p=P)

            def odd_columns(u, n, turn):
                at = n * BLOCKS * P + u * P
                return odd_w_in[0][:, bass.ds(at + turn * (2 * P), P)].rearrange("(k p) n -> p k n", p=P)

            for n in range(EVEN_N):
                load(even_columns(0, n, 0), 1 + n)

            def even_turn(turn, last):
                place, tile = EVEN(turn), 0
                for kind, u, n in sum(turn_steps(EVEN_N, last), []):
                    if kind == "P":
                        load(even_columns(u, n, turn + 1 if u == 0 else turn), place.split(tile - 1))
                        tile += 1
                    elif n == 0:
                        load(even_w_out[0][bass.ds(turn * P + u * AW, P), :], place.split(tile - 1))
                        tile += 1

            turns(sp, HEADS, even_turn)

            def load_ple(i, place):
                sp.dma_start(cv[:, 0:2, :].rearrange("p a b -> p (a b)").rearrange("p (c q) -> p c q", q=KP * P),
                             p_in[i, 0].rearrange("(c t) q -> t c q", t=P)).then_inc(p_loaded.sem, 16)
                for n in range(KD):
                    load(ple_gate_w[i][:, n * P:(n + 1) * P].rearrange("(k p) n -> p k n", p=P), place.split(n - 1))
                for n in range(KP):
                    load(ple_proj_w[i][n * P:(n + 1) * P, :], place.split(KD + n - 1))

            sp.wait_ge(y_ready[1].sem, HEADS)
            load_ple(0, PLE0)

            def load_gates(turn, u):
                sp.dma_start(w1[:, :].rearrange("p (a b) -> p a b", b=P)[:, 2 * u, :],
                             lru_w_a[0][bass.ds(turn * 2 + u, 1)].rearrange("g i j -> i (g j)")).then_inc(l_in[u].sem, 16)
                sp.dma_start(w1[:, :].rearrange("p (a b) -> p a b", b=P)[:, 2 * u + 1, :],
                             lru_w_x[0][bass.ds(turn * 2 + u, 1)].rearrange("g i j -> i (g j)")).then_inc(l_in[u].sem, 16)

            for n in range(ODD_N):
                load(odd_columns(0, n, 0), PRE_ODD.split(n - 1))
            after(sp, norm_low, 2, KD)
            for u in range(2):
                load_gates(0, u)

            def odd_turn(turn, last):
                place, tile = ODD(turn), 0
                for kind, u, n in sum(turn_steps(ODD_N, last), []):
                    if kind == "P":
                        load(odd_columns(u, n, turn + 1 if u == 0 else turn), place.split(tile - 1))
                        tile += 1
                    elif n == 0:
                        load(odd_w_out[0][bass.ds(turn * 2 * P + u * P, P), :], place.split(tile - 1))
                        tile += 1
                        if not last:
                            after(sp, l_y[u], turn, 1)
                            load_gates(turn + 1, u)

            turns(sp, TURNS, odd_turn)
            sp.wait_ge(l_y[1].sem, TURNS)
            load_ple(1, PLE1)

            for c in range(NC):
                sp.wait_ge(f_kept.sem, 2 * c + 2)
                sp.dma_start(out[0, c * P:(c + 1) * P, :], (w1, w2)[c % 2][:, :]).then_inc(stored[c % 2].sem, 16)
            for n in range(2):
                sp.wait_ge(stored[n].sem, 16 * NC // 2)

        @block.gpsimd
        def _(pool):
            build = zb[:, :, :].rearrange("p a b -> p (a b)")[:, 0:(2 * LEVELS + 1) * P].rearrange("p (a b) -> p a b", b=P)
            count = [0]

            def link(ins):
                count[0] += 1
                ins.then_inc(made.sem, 1)
                pool.wait_ge(made.sem, count[0])

            pool.memset(w_stage[:, :], 0.0).then_inc(cleared.sem, 1)
            link(pool.memset(ones[:, :], 1.0))
            link(pool.memset(ident[:, :], 0.0))
            link(pool.affine_select(out=ident[:, :], in_=ident[:, :], compare_op=ALU.not_equal, fill=1.0,
                                    base=0, pattern=[[-1, P]], channel_multiplier=1))
            link(pool.memset(upper[:, :], 1.0))
            link(pool.affine_select(out=upper[:, :], in_=upper[:, :], compare_op=ALU.is_ge, fill=0.0,
                                    base=0, pattern=[[1, P]], channel_multiplier=-1))
            link(pool.memset(build[:, :, :], 0.0))
            for l in range(LEVELS):
                b = 1 << l
                n = P // (2 * b)
                right = build[:, l, :].rearrange("p (n two b) -> p n two b", two=2, b=b)[:, :, 1, :]
                left = build[:, LEVELS + l, :].rearrange("p (n two b) -> p n two b", two=2, b=b)[:, :, 0, :]
                for v, off in ((right, 0), (left, b)):
                    link(pool.memset(v, 1.0))
                    link(pool.affine_select(out=v, in_=v, compare_op=ALU.is_ge, fill=0.0, base=-off,
                                            pattern=[[-2 * b, n], [0, b]], channel_multiplier=1))
                    link(pool.affine_select(out=v, in_=v, compare_op=ALU.is_ge, fill=0.0, base=off + b - 1,
                                            pattern=[[2 * b, n], [0, b]], channel_multiplier=-1))
            link(pool.tensor_copy(build[:, 2 * LEVELS, :], ident[:, :]))
            pool.memset(tiny[:, 0:1], EPS).then_inc(made.sem, 1)
            assert count[0] + 1 == MADE

            def split(slot, loaded, used):
                pool.wait_ge(w_in.sem, loaded)
                if used is not None:
                    pool.wait_ge(dense_ready.sem, used)
                pool.sem_inc(split_begun.sem, 1)
                pool.tensor_copy(w_high[:, slot, :], w_stage[:, :]).then_inc(w_split_high.sem, 1)

            def rest(slot, n):
                pool.wait_ge(w_split_high.sem, n)
                pool.tensor_tensor(w_low[:, slot, :], w_stage[:, :], w_high[:, slot, :].bitcast(F32),
                                   ALU.subtract).then_inc(w_split.sem, 1)

            def tile(place, local, used):
                slot = place.slot(local)
                n = place.split(local)
                split(slot, place.turn * (16 * place.tiles) + 16 * (place.tile0 + local + 2), used)
                rest(slot, n)

            tile(PRE_EVEN, 0, None)
            tile(PRE_EVEN, 1, None)
            for n in range(1, EVEN_N):
                tile(PRE_EVEN, 1 + n, n)

            def turn_tiles(place, n_cols, last):
                steps = sum(turn_steps(n_cols, last), [])
                final = [max(i for i in range(len(steps)) if tile_of(steps, i) == t)
                         for t in range(tile_of(steps, len(steps) - 1) + 1)]
                for t in range(len(final)):
                    if t >= 2:
                        used = place.ready(final[t - 2])
                    elif t == 1:
                        used = place.ready(-1)
                    else:
                        used = place.ready(-2)
                    tile(place, t, used)

            turns(pool, HEADS, lambda turn, last: turn_tiles(EVEN(turn), EVEN_N, last))

            def ple_tiles(place):
                for n in range(KD + KP):
                    if n >= 2:
                        used = place.ready(n - 2)
                    else:
                        used = place.ready((-9, -1)[n])
                    tile(place, n, used)

            ple_tiles(PLE0)
            for n in range(ODD_N):
                tile(PRE_ODD, n, PRE_ODD.ready(-1))
            turns(pool, TURNS, lambda turn, last: turn_tiles(ODD(turn), ODD_N, last))
            ple_tiles(PLE1)

        @block.tensor
        def _(pe):
            def three(out_, wh, wl, xh_, xl_, first, last):
                pe.matmul(out_, wh, xh_, start=first, stop=False)
                pe.matmul(out_, wh, xl_, start=False, stop=False)
                return pe.matmul(out_, wl, xh_, start=False, stop=last)

            def piece(what, local, k, last, place, steps):
                kind, u, n = what
                pair = place.pair(local)
                slot = place.slot(tile_of(steps, local))
                if k == 0:
                    pe.wait_ge(w_split.sem, place.split(tile_of(steps, local)))
                    if not (isinstance(place.turn, int) and place.taken(local) < 2):
                        pe.wait_ge(taken[pair].sem, place.taken(local) - 1)
                    if kind == "O":
                        y = y_ready if place.steps == n_steps(EVEN_N) else l_y
                        if n == 0:
                            after(pe, y[u], place.turn, 1)
                for h in range(2):
                    bank = dense[2 * pair + h]
                    if kind in "PG":
                        w = slice(k * P, (k + 1) * P)
                        r = three(bank[:, :], w_high[:, slot, w], w_low[:, slot, w],
                                  half(xh[:, k, :], h), half(xl[:, k, :], h), k == 0, last)
                    else:
                        w = slice(n * P, (n + 1) * P)
                        r = three(bank[:, :], w_high[:, slot, w], w_low[:, slot, w],
                                  half(yh[:, u, :], h), half(yl[:, u, :], h), True, True)
                if last:
                    r.then_inc(dense_ready.sem, 1)

            def norm(n):
                for k in range(KD):
                    after(pe, norm_squared, n, k + 1)
                    sq = (w1, w2)[k % 2]
                    for h in range(2):
                        r = pe.matmul(work[h][:, :], ones[:, :], half(sq, h), start=k == 0, stop=k == KD - 1)
                    r.then_inc(norm_summed.sem, 1)

            def turn_all(src, banks, st):
                for c in range(NC):
                    r = pe.transpose(in_half(banks[c // HC], c), chunk(src, c), ident[:, :])
                    if c % HC == HC - 1:
                        r.then_inc(st.sem, 1)

            pe.wait_ge(vec_in.sem, 16 * 12)
            pe.wait_ge(made.sem, MADE)
            for i, n in enumerate((P, P, 32)):
                r = pe.transpose(work[0][:, i * P:i * P + n], w1[0:n, i * P:(i + 1) * P], ident[0:n, 0:n])
            r.then_inc(vec_turned.sem, 1)
            pe.wait_ge(x_loaded.sem, 16 * NC)
            for k in range(KD):
                for h in range(2):
                    i = 2 * k + h
                    bank = work[i % 4]
                    if i == 0:
                        pe.wait_ge(vec_kept.sem, 1)
                    if i >= 4:
                        pe.wait_ge(x_kept.sem, i - 3)
                    for c in range(HC):
                        r = pe.transpose(in_half(bank, c), tiles8[h * HC + c][:, k * P:(k + 1) * P], ident[:, :])
                    r.then_inc(x_turned.sem, 1)
            pe.wait_ge(x_kept.sem, 2 * KD)
            norm(0)

            pe.wait_ge(w_split.sem, 1)
            for k in range(KD):
                after(pe, norm_low, 0, k + 1)
                for h in range(2):
                    r = three(dense[h][0:64, :], w_high[:, 0, k * P:k * P + 64], w_low[:, 0, k * P:k * P + 64],
                              half(xh[:, k, :], h), half(xl[:, k, :], h), k == 0, k == KD - 1)
            r.then_inc(dense_ready.sem, 1)
            for n in range(EVEN_N):
                for k in range(KD):
                    piece(("P", 0, n), 1 + n, k, k == KD - 1, PRE_EVEN, [("P", 0, 0)] + proj(0, EVEN_N))
            pe.wait_ge(row_vec.sem, 5)
            after(pe, norm_rooted, 0, 2)
            for i in range(2):
                for c in range(NC):
                    at = 32 * i
                    r = pe.transpose(work[i][:, c * HEADS:(c + 1) * HEADS],
                                     rows[at:at + HEADS, c * CHUNK:(c + 1) * CHUNK],
                                     ident[at:at + HEADS, at:at + HEADS])
                r.then_inc(row_turned.sem, 1)

            def head_sum(u, turn, sq):
                for h in range(2):
                    after(pe, o_kept[u], turn, 2 * h + 2)
                    pe.matmul(work[2 + h][:, :], ones[:, :], half(sq, h), start=True, stop=True)\
                        .then_inc(o_summed[u].sem, 1)

            def hgrn(turn, fill):
                after(pe, a_bounded, turn, 3)
                for c in range(NC):
                    r = pe.matmul(in_half(work[c // HC], c), chunk(k_a, c), chunk(q_a, c), start=True, stop=True)
                r.then_inc(a_scores.sem, 1)
                fill()
                for l in range(LEVELS):
                    b = 1 << l
                    after(pe, a_scaled, turn, 1 + 3 * l)
                    if l >= 2:
                        after(pe, a_kept, turn, 2 + l - 1)
                    for c in range(NC):
                        right = chunk(q_a, c).rearrange("p (n two b) -> p n two b", two=2, b=b)[:, :, 1, :]
                        r = pe.matmul(work[2 + l % 2][:, c * 64:(c + 1) * 64], chunk(k_a, c), right,
                                      start=True, stop=True)
                    r.then_inc(a_scores.sem, 1)
                    if l == 0:
                        after(pe, a_kept, turn, 2)
                        turn_all(v_a, work[0:2], a_turned)
                    fill()
                after(pe, a_values, turn, 2)
                after(pe, a_scaled, turn, 1 + 3 * LEVELS)
                turn_all(k_a, work[0:2], a_turned)
                fill()
                for h in range(2):
                    after(pe, a_keys, turn, h + 1)
                    after(pe, a_kept, turn, 2 + LEVELS)
                    for c in range(h * HC, min((h + 1) * HC, NC - 1)):
                        r = pe.matmul(in_half(work[2 + h], c), chunk(k_a, c), chunk(v_a, c), start=True, stop=True)
                    r.then_inc(a_kv.sem, 1)
                fill()
                for h in range(2):
                    for c in range(h * HC, (h + 1) * HC):
                        o = in_half(work[h], c)
                        r = pe.matmul(o, chunk(v_a, c), chunk(w1, c), start=True, stop=c == 0)
                        if c:
                            after(pe, a_state, turn, c)
                            r = pe.matmul(o, w2[:, (c - 1) * P:c * P], chunk(q_a, c), start=False, stop=True)
                    r.then_inc(mixed[0].sem, 1)
                fill()
                after(pe, a_state, turn, NC - 1)
                head_sum(0, turn, f_a)
                fill()
                fill()

            def gdn(turn, fill):
                for i in range(2):
                    after(pe, b_squared, turn, i + 1)
                    for h in range(2):
                        pe.matmul(work[2 * i + h][:, :], ones[:, :], half(raw[i], h), start=True, stop=True)\
                            .then_inc(b_summed.sem, 1)
                fill()
                for i in range(2):
                    after(pe, b_rooted, turn, 2 * i + 2)
                    after(pe, b_rows, turn, 2)
                    at = 32 * i
                    for h in range(2):
                        r = pe.matmul(work[2 * i + h][:, :], ones[at:at + HEADS, :],
                                      w2[at:at + HEADS, h * HALF:(h + 1) * HALF], start=True, stop=True)
                    r.then_inc(b_spread.sem, 1)
                fill()
                after(pe, b_normed, turn, 4)
                after(pe, b_diff, turn, NC + 2)
                after(pe, b_keyed, turn, 2)
                for i, other in enumerate((raw[1], q_b)):
                    for c in range(NC):
                        r = pe.matmul(in_half(work[2 * i + c // HC], c), chunk(k_b, c), chunk(other, c),
                                      start=True, stop=True)
                        if c % HC == HC - 1:
                            r.then_inc(b_prod.sem, 1)
                fill()
                after(pe, b_scores, turn, 2)
                after(pe, b_silu, turn, 3)
                turn_all(v_b, work[0:2], b_turned)
                after(pe, b_scores, turn, 4)
                turn_all(k_b, work[2:4], b_turned)
                fill()
                after(pe, b_ident, turn, 2)
                for l in range(LEVELS):
                    for h in range(2):
                        right = work[2 * h]
                        if l == 0:
                            after(pe, b_vk, turn, 4)
                        else:
                            after(pe, b_inv, turn, 4 * l if h else 4 * l - 2)
                        for c in range(h * HC, (h + 1) * HC):
                            r = pe.matmul(in_half(right, c), chunk(raw[1], c),
                                          ident[:, :] if l == 0 else chunk(w1, c), start=True, stop=True)
                        r.then_inc(b_u.sem, 1)
                    if l:
                        fill()
                        for h in range(2):
                            after(pe, b_ukept, turn, 2 * (l - 1) + h + 1)
                            if l < LEVELS - 1:
                                for c in range(h * HC, (h + 1) * HC):
                                    r = pe.matmul(in_half(work[2 * h + 1], c), chunk(w3, c), chunk(w2, c),
                                                  start=True, stop=True)
                                r.then_inc(b_y.sem, 1)
                            for c in range(h * HC, (h + 1) * HC):
                                r = pe.matmul(in_half(work[2 * h], c), chunk(w2, c), chunk(w3, c),
                                              start=True, stop=True)
                            r.then_inc(b_y.sem, 1)
                    fill()
                for c in range(NC):
                    before = state[:, c % 2, :]
                    if c == 0:
                        after(pe, b_inv, turn, 4 * LEVELS - 2)
                    else:
                        after(pe, c_state, turn, c)
                        pe.matmul(work[0][:, 0:P], chunk(k_b, c), before, start=True, stop=True).then_inc(c_ks.sem, 1)
                        after(pe, c_r, turn, c)
                    pe.matmul(work[1][:, 0:P], chunk(w3, c), chunk(v_b, c), start=True, stop=True).then_inc(c_v.sem, 1)
                    after(pe, c_vn, turn, c + 1)
                    if c < NC - 1:
                        pe.matmul(work[0][:, 0:P], chunk(raw[0], c), chunk(w2, c), start=True, stop=True)\
                            .then_inc(c_kv.sem, 1)
                    o = in_half(work[2 + c // HC], c)
                    if c:
                        pe.matmul(o, before, chunk(q_b, c), start=True, stop=False)
                    r = pe.matmul(o, chunk(w2, c), chunk(raw[2], c), start=c == 0, stop=True)
                    if c % HC == HC - 1:
                        r.then_inc(mixed[1].sem, 1)
                    if c % 2:
                        fill()
                after(pe, o_kept[1], turn, 4)
                head_sum(1, turn, raw[0])
                fill()
                fill()
                fill()

            def lru(u, turn, fill):
                after(pe, l_in[u], turn, 32)
                after(pe, l_conv[u], turn, TAPS)
                blocks = w1[:, :].rearrange("p (a b) -> p a b", b=P)
                for i in range(2):
                    for h in range(2):
                        r = pe.matmul(work[2 * i + h][:, :], blocks[:, 2 * u + i, :], half(cv[:, 0, :], h),
                                      start=True, stop=True)
                    r.then_inc(l_gates[u].sem, 1)
                for _ in range(FILLS_L):
                    fill()

            def even_turn(turn, last):
                place = EVEN(turn)
                w = turn_steps(EVEN_N, last)
                steps = sum(w, [])
                f = Filler(w[0], 0, place, steps, FILLS_A, piece, None)
                hgrn(turn, f)
                f.finish()
                f = Filler(w[1], len(w[0]), place, steps, FILLS_B, piece, None)
                gdn(turn, f)
                f.finish()
                f = Filler(w[2], len(w[0]) + len(w[1]), place, steps, 1, piece, None)
                f()

            turns(pe, HEADS, even_turn)

            def ple(i, place, n_norm):
                norm(n_norm)
                after(pe, norm_low, n_norm, KD)
                for n in range(KD):
                    for k in range(KD):
                        piece(("G", 0, n), n, k, k == KD - 1, place, PLE_STEPS)
                pe.wait_ge(p_loaded.sem, 16 * (i + 1))
                after(pe, norm_rooted, n_norm, 2)
                src = cv[:, 0:2, :].rearrange("p a b -> p (a b)").rearrange("p (c q) -> p c q", q=KP * P)
                for k in range(KP):
                    for h in range(2):
                        for c in range(HC):
                            r = pe.transpose(in_half(work[2 * k + h], c), src[:, h * HC + c, k * P:(k + 1) * P],
                                             ident[:, :])
                        r.then_inc(p_turned.sem, 1)
                pe.wait_ge(w_split.sem, place.split(KD + KP - 1))
                after(pe, p_low, i, 4)
                for n in range(KD):
                    local = KD + n
                    pair = place.pair(local)
                    pe.wait_ge(taken[pair].sem, place.taken(local) - 1)
                    for k in range(KP):
                        slot = place.slot(KD + k)
                        w = slice(n * P, (n + 1) * P)
                        for h in range(2):
                            r = three(dense[2 * pair + h][:, :], w_high[:, slot, w], w_low[:, slot, w],
                                      half(yh[:, k, :], h), half(yl[:, k, :], h), k == 0, k == KP - 1)
                    r.then_inc(dense_ready.sem, 1)

            ple(0, PLE0, 1)
            norm(2)
            after(pe, norm_low, 2, KD)
            for n in range(ODD_N):
                for k in range(KD):
                    piece(("P", 0, n), n, k, k == KD - 1, PRE_ODD, proj(0, ODD_N))

            def odd_turn(turn, last):
                place = ODD(turn)
                w = turn_steps(ODD_N, last)
                steps = sum(w, [])
                f = Filler(w[0], 0, place, steps, FILLS_L, piece, None)
                lru(0, turn, f)
                f = Filler(w[1], len(w[0]), place, steps, FILLS_L, piece, None)
                lru(1, turn, f)
                f = Filler(w[2], len(w[0]) + len(w[1]), place, steps, 1, piece, None)
                f()

            turns(pe, TURNS, odd_turn)
            ple(1, PLE1, 3)
            norm(4)
            after(pe, f_scaled, 0, KD)
            after(pe, norm_rooted, 4, 2)
            for c in range(NC):
                for h in range(2):
                    i = 2 * c + h
                    if i >= 4:
                        pe.wait_ge(f_kept.sem, i - 3)
                    for k in range(KD // 2):
                        r = pe.transpose(in_half(work[i % 4], k), chunk(tiles8[h * (KD // 2) + k], c), ident[:, :])
                    r.then_inc(f_turned.sem, 1)

        @block.scalar
        def _(act):
            eps = tiny[:, 0:1]

            def evac(what, local, place):
                kind, u, n = what
                if kind != "P":
                    return
                pair = place.pair(local)
                odd = place.steps == n_steps(ODD_N) or place is PRE_ODD
                if odd:
                    dst = raw[u] if n == 0 else za[:, u, :]
                elif u == 0:
                    dst = za[:, n, :]
                else:
                    dst = raw[n] if n < 3 else zg[:, :]
                act.wait_ge(dense_ready.sem, place.ready(local))
                act.activation(half(dst, 0), dense[2 * pair][:, :], ACT.Copy)\
                    .then_inc((lz_ready if odd else z_ready)[u].sem, 1)
                act.activation(half(dst, 1), dense[2 * pair + 1][:, :], ACT.Copy).then_inc(taken[pair].sem, 1)

            def norm_root(n):
                for h in range(2):
                    after(act, norm_summed, n, KD)
                    act.activation(half(w3, h), work[h][:, :], ACT.Sqrt, bias=eps, scale=1.0 / D)\
                        .then_inc(norm_rooted.sem, 1)

            def norm(n, split=True):
                for k in range(KD):
                    if k >= 2:
                        after(act, norm_summed, n, k - 1)
                    act.activation((w1, w2)[k % 2][:, :], x[:, k, :], ACT.Square).then_inc(norm_squared.sem, 1)
                norm_root(n)
                if split:
                    for k in range(KD):
                        after(act, norm_scaled, n, k + 1)
                        act.activation(xh[:, k, :], (w1, w2)[k % 2][:, :], ACT.Copy).then_inc(norm_high.sem, 1)

            act.wait_ge(vec_turned.sem, 1)
            act.activation(cols[:, :], work[0][:, 0:2 * P + 32], ACT.Copy).then_inc(vec_kept.sem, 1)
            for i in range(2 * KD):
                act.wait_ge(x_turned.sem, i + 1)
                act.activation(half(x[:, i // 2, :], i % 2), work[i % 4][:, :], ACT.Copy).then_inc(x_kept.sem, 1)
            act.wait_ge(vec_ready.sem, 1)
            act.activation(lows[:, 1, :], lows[:, 0, :], ACT.Exp).then_inc(l_lam.sem, 1)
            lam = cols[:, C_ODD + 7 * BLOCKS:C_ODD + 8 * BLOCKS]
            t0, t1 = pairs(0), pairs(1)
            act.wait_ge(vec_kept.sem, 1)
            act.activation(t0, lam, ACT.Abs).then_inc(l_lam.sem, 1)
            act.wait_ge(l_lam.sem, 2)
            act.activation(t1, t0, ACT.Exp, scale=-1.0).then_inc(l_lam.sem, 1)
            act.wait_ge(l_lam.sem, 3)
            act.activation(t0, t1, ACT.Ln, bias=1.0).then_inc(l_lam.sem, 1)
            act.activation(unit_cols[:, 0, :], lam, ACT.Relu, scale=-1.0).then_inc(l_lam.sem, 1)
            act.wait_ge(small_in.sem, 32)
            act.activation(tiny[0:HEADS, 3:4], tiny[0:HEADS, 1:2], ACT.Exp).then_inc(l_lam.sem, 1)
            act.wait_ge(x_kept.sem, 2 * KD)
            norm(0)

            act.wait_ge(dense_ready.sem, 1)
            dt = tiny[0:HEADS, 2:3]
            for h in range(2):
                act.activation(rows[32:32 + HEADS, h * HALF:(h + 1) * HALF], dense[h][32:32 + HEADS, :], ACT.Sigmoid)\
                    .then_inc(row_step.sem, 1)
            for h in range(2):
                act.activation(w1[0:HEADS, h * HALF:(h + 1) * HALF], dense[h][0:HEADS, :], ACT.Abs, bias=dt)\
                    .then_inc(row_step.sem, 1)
                act.activation(w2[0:HEADS, h * HALF:(h + 1) * HALF], dense[h][0:HEADS, :], ACT.Relu, bias=dt)\
                    .then_inc(row_step.sem if h == 0 else taken[0].sem, 1)
            act.wait_ge(row_step.sem, 5)
            act.activation(w1[0:HEADS, :], w1[0:HEADS, :], ACT.Exp, scale=-1.0).then_inc(row_step.sem, 1)
            act.wait_ge(row_step.sem, 6)
            act.activation(w1[0:HEADS, :], w1[0:HEADS, :], ACT.Ln, bias=1.0).then_inc(row_step.sem, 1)
            for n in range(EVEN_N):
                evac(("P", 0, n), 1 + n, PRE_EVEN)
            for i in range(2):
                act.wait_ge(row_turned.sem, i + 1)
                act.activation(gcols[:, i, :, :].rearrange("p c h -> p (c h)"), work[i][:, 0:NC * HEADS], ACT.Copy)\
                    .then_inc(row_cols.sem, 1)

            def head_out(u, turn, o, sq):
                for h in range(2):
                    after(act, mixed[u], turn, h + 1)
                    bank = work[(0, 2)[u] + h]
                    act.activation(half(o, h), bank[:, :], ACT.Copy).then_inc(o_kept[u].sem, 1)
                    act.activation(half(sq, h), bank[:, :], ACT.Square).then_inc(o_kept[u].sem, 1)
                for h in range(2):
                    after(act, o_summed[u], turn, h + 1)
                    act.activation(half(sq, h), work[2 + h][:, :], ACT.Sqrt, bias=eps, scale=1.0 / P)\
                        .then_inc(o_rooted[u].sem, 1)

            def round_y(u, turn, o, st, high):
                after(act, st, turn, st.per_turn)
                act.activation(yh[:, u, :], o, ACT.Copy).then_inc(high.sem, 1)

            def hgrn(turn, fill):
                after(act, z_ready[0], turn, 4)
                act.activation(k_a, f_a, ACT.Sigmoid, scale=-1.0).then_inc(a_gates.sem, 1)
                after(act, a_gates, turn, 1)
                act.activation(f_a, f_a, ACT.Sigmoid).then_inc(a_gates.sem, 1)
                act.activation(gate_a, gate_a, ACT.Silu).then_inc(a_gates.sem, 1)
                fill()
                for l in range(LEVELS):
                    if l == 0:
                        for h in range(2):
                            after(act, a_turned, turn, h + 1)
                            act.activation(half(v_a, h), work[h][:, :], ACT.Copy).then_inc(a_values.sem, 1)
                    fill()
                for h in range(2):
                    after(act, a_turned, turn, 2 + h + 1)
                    act.activation(half(k_a, h), work[h][:, :], ACT.Copy).then_inc(a_keys.sem, 1)
                fill()
                fill()
                fill()
                after(act, a_state, turn, HC)
                head_out(0, turn, q_a, f_a)
                fill()
                round_y(0, turn, q_a, o_scaled[0], y_high[0])
                fill()

            def gdn(turn, fill):
                for m in range(3):
                    after(act, b_conv, turn, 3 * (TAPS - 1) + m + 1)
                    act.activation(cv[:, m, :], cv[:, m, :], ACT.Silu).then_inc(b_silu.sem, 1)
                after(act, b_silu, turn, 1)
                act.activation(zg[:, :], zg[:, :], ACT.Silu).then_inc(b_silu.sem, 1)
                for m in range(2):
                    after(act, b_silu, turn, m + 1)
                    act.activation(raw[m], cv[:, m, :], ACT.Square).then_inc(b_squared.sem, 1)
                for i in range(2):
                    for h in range(2):
                        after(act, b_summed, turn, 2 * i + h + 1)
                        act.activation(half(raw[i], h), work[2 * i + h][:, :], ACT.Sqrt, bias=eps)\
                            .then_inc(b_rooted.sem, 1)
                fill()
                after(act, b_normed, turn, 4)
                after(act, b_spread, turn, 1)
                for h in range(2):
                    act.activation(half(raw[0], h), work[h][:, :], ACT.Exp).then_inc(b_decay.sem, 1)
                act.activation(w1[:, :].rearrange("p (c t) -> p c t", t=P), wide(ident, NC), ACT.Copy)\
                    .then_inc(b_ident.sem, 1)
                act.activation(w3[:, :].rearrange("p (c t) -> p c t", t=P), wide(ident, NC), ACT.Copy)\
                    .then_inc(b_ident.sem, 1)
                fill()
                after(act, b_diff, turn, NC + 2)
                act.activation(raw[2], raw[2], ACT.Exp).then_inc(b_exp.sem, 1)
                act.activation(head_cols[:, 2, :], head_cols[:, 0, :], ACT.Exp).then_inc(b_exp.sem, 1)
                act.activation(head_cols[:, 3, :], head_cols[:, 3, :], ACT.Exp).then_inc(b_exp.sem, 1)
                fill()
                fill()
                for l in range(LEVELS):
                    if l:
                        for h in range(2):
                            after(act, b_u, turn, 2 * l + h + 1)
                            act.activation(half(w2, h), work[2 * h][:, :], ACT.Copy).then_inc(b_ukept.sem, 1)
                        fill()
                    fill()
                for c in range(NC):
                    after(act, c_v, turn, c + 1)
                    act.activation(chunk(w2, c), work[1][:, 0:P], ACT.Copy).then_inc(c_vn.sem, 1)
                    if c % 2:
                        fill()
                head_out(1, turn, q_b, raw[0])
                fill()
                round_y(1, turn, q_b, o_scaled[1], y_high[1])
                fill()
                fill()

            def even_turn(turn, last):
                place = EVEN(turn)
                w = turn_steps(EVEN_N, last)
                steps = sum(w, [])
                hgrn(turn, Filler(w[0], 0, place, steps, FILLS_A, None, evac))
                gdn(turn, Filler(w[1], len(w[0]), place, steps, FILLS_B, None, evac))

            def wide(t, n):
                a = t[:, :]
                return bass.AP(a.tensor, a.offset, [list(a.ap[0]), [0, n], [1, P]])

            turns(act, HEADS, even_turn)

            def ple(i, place, n_norm):
                added = place.taken
                act.wait_ge(taken[place.pair(-1)].sem, added(-1))
                act.wait_ge(taken[place.pair(-2)].sem, added(-2))
                norm(n_norm)
                for n in range(KD):
                    pair = place.pair(n)
                    act.wait_ge(dense_ready.sem, place.ready(n))
                    g = gate_tile(n)
                    act.activation(half(g, 0), dense[2 * pair][:, :], ACT.Sigmoid).then_inc(p_gate.sem, 1)
                    act.activation(half(g, 1), dense[2 * pair + 1][:, :], ACT.Sigmoid).then_inc(taken[pair].sem, 1)
                for k in range(KP):
                    for h in range(2):
                        after(act, p_turned, i, 2 * k + h + 1)
                        act.activation(half(yh[:, k, :], h), work[2 * k + h][:, :], ACT.Copy).then_inc(p_high.sem, 1)

            ple(0, PLE0, 1)
            after(act, p_added, 0, KD)
            norm(2)
            for n in range(ODD_N):
                evac(("P", 0, n), n, PRE_ODD)

            def lru(u, turn, fill):
                uc = unit_cols[:, u, :]
                after(act, lz_ready[u], turn, 2)
                for i in range(2):
                    after(act, l_gates[u], turn, i + 1)
                    for h in range(2):
                        act.activation(half(cv[:, 1 + i, :], h), work[2 * i + h][:, :], ACT.Sigmoid,
                                       bias=uc[:, 5 + i:6 + i]).then_inc(l_sig[u].sem, 1)
                after(act, l_sig[u], turn, 2)
                act.activation(za[:, u, :], za[:, u, :], ACT.Silu).then_inc(l_silu[u].sem, 1)
                fill()
                after(act, l_sig[u], turn, 2)
                act.activation(za[:, 2, :], cv[:, 1, :], ACT.Tanh, scale=uc[:, 8:9]).then_inc(l_exp[u].sem, 1)
                after(act, l_exp[u], turn, 1)
                act.activation(cv[:, 1, :], cv[:, 1, :], ACT.Exp, scale=uc[:, 7:8]).then_inc(l_exp[u].sem, 1)
                fill()
                after(act, l_vec[u], turn, 2)
                act.activation(za[:, 2, :], za[:, 2, :], ACT.Sqrt).then_inc(l_root[u].sem, 1)
                fill()
                round_y(u, turn, za[:, 3, :], l_vec[u], l_high[u])
                fill()
                fill()

            def odd_turn(turn, last):
                place = ODD(turn)
                w = turn_steps(ODD_N, last)
                steps = sum(w, [])
                lru(0, turn, Filler(w[0], 0, place, steps, FILLS_L, None, evac))
                lru(1, turn, Filler(w[1], len(w[0]), place, steps, FILLS_L, None, evac))

            turns(act, TURNS, odd_turn)
            ple(1, PLE1, 3)
            after(act, p_added, 1, KD)
            norm(4, split=False)
            after(act, f_scaled, 0, KD)
            for i in range(2 * NC):
                c = i // 2
                act.wait_ge(f_turned.sem, i + 1)
                if c >= 2:
                    act.wait_ge(stored[c % 2].sem, 16 * (c // 2))
                act.activation(half((w1, w2)[c % 2], i % 2), work[i % 4][:, :], ACT.Copy).then_inc(f_kept.sem, 1)

        @block.vector
        def _(dve):
            def evac(what, local, place):
                kind, u, n = what
                if kind != "O":
                    return
                pair = place.pair(local)
                dve.wait_ge(dense_ready.sem, place.ready(local))
                dve.tensor_tensor(half(x[:, n, :], 0), dense[2 * pair][:, :], half(x[:, n, :], 0), ALU.add)
                dve.tensor_tensor(half(x[:, n, :], 1), dense[2 * pair + 1][:, :], half(x[:, n, :], 1), ALU.add)\
                    .then_inc(taken[pair].sem, 1)

            def norm_start(n):
                for h in range(2):
                    after(dve, norm_rooted, n, h + 1)
                    dve.reciprocal(half(w3, h), half(w3, h)).then_inc(norm_inverse.sem, 1)
                after(dve, norm_inverse, n, 2)

            def norm(n):
                norm_start(n)

                def low(k):
                    after(dve, norm_high, n, k + 1)
                    dve.tensor_tensor(xl[:, k, :], (w1, w2)[k % 2][:, :], xh[:, k, :].bitcast(F32), ALU.subtract)\
                        .then_inc(norm_low.sem, 1)

                for k in range(KD):
                    if k >= 2:
                        after(dve, norm_low, n, k - 1)
                    dve.scalar_tensor_tensor(out=(w1, w2)[k % 2][:, :], in0=x[:, k, :],
                                             scalar=cols[:, NORMS[n] + k:NORMS[n] + k + 1], in1=w3[:, :],
                                             op0=ALU.mult, op1=ALU.mult).then_inc(norm_scaled.sem, 1)
                    if k:
                        low(k - 1)
                low(KD - 1)

            build = zb[:, :, :].rearrange("p a b -> p (a b)")[:, 0:(2 * LEVELS + 1) * P].rearrange("p (a b) -> p a b", b=P)
            dve.wait_ge(made.sem, MADE)
            dve.tensor_copy(masks[:, :, :], build).then_inc(masks_ready.sem, 1)
            dve.wait_ge(masks_ready.sem, 1)
            dve.memset(zb[:, :, 0:PAD], 0.0).then_inc(masks_ready.sem, 1)
            dve.wait_ge(vec_kept.sem, 1)
            lb = cols[:, C_LB:C_LB + HEADS]
            dve.tensor_tensor(lows[:, 0, :], lb, lb, ALU.subtract).then_inc(vec_ready.sem, 1)
            dve.wait_ge(l_lam.sem, 1)
            dve.reciprocal(lows[:, 2, :], lows[:, 1, :]).then_inc(vec_ready.sem, 1)
            dve.wait_ge(vec_ready.sem, 2)
            dve.tensor_tensor(lows[:, 0, :], lows[:, 1, :], lows[:, 2, :], ALU.mult).then_inc(vec_ready.sem, 1)
            dve.wait_ge(vec_ready.sem, 3)
            dve.tensor_tensor(lows[:, 2, :], lows[:, 0, :], lows[:, 0, :], ALU.subtract).then_inc(vec_ready.sem, 1)
            dve.wait_ge(vec_ready.sem, 4)
            dve.tensor_scalar(lows[:, 3, :], lows[:, 2, :], -1.0, 1.0, ALU.mult, ALU.add).then_inc(vec_ready.sem, 1)
            dve.wait_ge(l_lam.sem, 5)
            t0 = pairs(0)
            lam = cols[:, C_ODD + 7 * BLOCKS:C_ODD + 8 * BLOCKS]
            dve.tensor_tensor(t0, t0, unit_cols[:, 0, :], ALU.add).then_inc(vec_ready.sem, 1)
            dve.wait_ge(vec_ready.sem, 6)
            dve.tensor_scalar(lam, t0, -8.0, None, ALU.mult).then_inc(vec_ready.sem, 1)
            dve.wait_ge(l_lam.sem, 6)
            dve.tensor_scalar(tiny[0:HEADS, 3:4], tiny[0:HEADS, 3:4], -1.0, None, ALU.mult).then_inc(vec_ready.sem, 1)
            dve.wait_ge(vec_ready.sem, 8)
            norm(0)

            dve.memset(w3[0:HEADS, :], 1.0).then_inc(row_vec.sem, 1)
            dve.wait_ge(row_vec.sem, 1)
            dve.memset(w3[0:HEADS, :].rearrange("p (c t) -> p c t", t=CHUNK)[:, :, 0:1], 0.0).then_inc(row_vec.sem, 1)
            dve.wait_ge(row_step.sem, 7)
            dve.tensor_tensor(w1[0:HEADS, :], w1[0:HEADS, :], w2[0:HEADS, :], ALU.add).then_inc(row_vec.sem, 1)
            dve.wait_ge(row_vec.sem, 3)
            dve.tensor_scalar(w1[0:HEADS, :], w1[0:HEADS, :], tiny[0:HEADS, 3:4], None, ALU.mult).then_inc(row_vec.sem, 1)
            dve.wait_ge(row_vec.sem, 4)
            dve.tensor_tensor_scan(out=rows[0:HEADS, :], data0=w3[0:HEADS, :], data1=w1[0:HEADS, :], initial=0.0,
                                   op0=ALU.mult, op1=ALU.add).then_inc(row_vec.sem, 1)

            def select(out_, mask, data):
                dve.sem_inc(select_begun.sem, 1)
                return dve.copy_predicated(out_, mask, data)

            def over_chunks(n_mask, n, b=None):
                m = masks[:, n_mask, :]
                if b is not None:
                    m = m.rearrange("p (n two b) -> p n two b", two=2, b=b)[:, :, 1, :]
                dims = [list(d) for d in m.ap]
                return bass.AP(m.tensor, m.offset, [dims[0], [0, n]] + dims[1:])

            def by_blocks(t, b):
                return t.rearrange("p (n two b) -> p n two b", two=2, b=b)

            def repeat(v, b):
                dims = [list(d) for d in v.ap]
                return bass.AP(v.tensor, v.offset, dims[:-1] + [[0, b]])

            def head_out(u, turn, o, sq, gate, g_col, fill):
                after(dve, o_rooted[u], turn, 2)
                dve.reciprocal(sq, sq).then_inc(o_scaled[u].sem, 1)
                after(dve, o_scaled[u], turn, 1)
                dve.scalar_tensor_tensor(out=o, in0=o, scalar=g_col, in1=sq, op0=ALU.mult, op1=ALU.mult)\
                    .then_inc(o_scaled[u].sem, 1)
                after(dve, o_scaled[u], turn, 2)
                dve.tensor_tensor(o, o, gate, ALU.mult).then_inc(o_scaled[u].sem, 1)
                fill()
                after(dve, y_high[u], turn, 1)
                dve.tensor_tensor(yl[:, u, :], o, yh[:, u, :].bitcast(F32), ALU.subtract).then_inc(y_ready[u].sem, 1)
                fill()

            def hgrn(turn, fill):
                uc = unit_cols[:, 0, :]
                after(dve, a_gates, turn, 3)
                dve.tensor_copy(uc[:, 0:2], lows[:, 2:4, bass.ds(turn, 1)].rearrange("p a b -> p (a b)"))\
                    .then_inc(a_bounded.sem, 1)
                dve.tensor_copy(uc[:, 2:3], cols[:, bass.ds(turn + C_HEAD, 1)]).then_inc(a_cols.sem, 1)
                after(dve, a_bounded, turn, 1)
                dve.tensor_scalar(k_a, k_a, uc[:, 1:2], None, ALU.mult).then_inc(a_bounded.sem, 1)
                dve.tensor_scalar(f_a, f_a, uc[:, 1:2], uc[:, 0:1], ALU.mult, ALU.add).then_inc(a_bounded.sem, 1)
                dve.memset(w1[:, :], 0.0)
                after(dve, a_bounded, turn, 3)
                after(dve, a_scores, turn, 1)
                dve.tensor_tensor(q_a, q_a, f_a, ALU.mult).then_inc(a_scaled.sem, 1)
                after(dve, a_scaled, turn, 1)
                for h in range(2):
                    select(half(w1, h).rearrange("p (c t) -> p c t", t=P), over_chunks(2 * LEVELS, HC),
                           work[h][:, :].rearrange("p (c t) -> p c t", t=P)).then_inc(a_kept.sem, 1)
                fill()
                for l in range(LEVELS):
                    b = 1 << l
                    after(dve, a_scores, turn, 2 + l)
                    q, k, f = by_blocks(q_a, b), by_blocks(k_a, b), by_blocks(f_a, b)
                    done = 1 + 3 * l
                    dve.tensor_tensor(q[:, :, 1, :], q[:, :, 1, :], repeat(f[:, :, 0, 0:1], b), ALU.mult)\
                        .then_inc(a_scaled.sem, 1)
                    dve.tensor_tensor(k[:, :, 0, :], k[:, :, 0, :], repeat(f[:, :, 1, 0:1], b), ALU.mult)\
                        .then_inc(a_scaled.sem, 1)
                    after(dve, a_scaled, turn, done + 2)
                    dve.tensor_tensor(f[:, :, 0, 0:1], f[:, :, 0, 0:1], f[:, :, 1, 0:1], ALU.mult)\
                        .then_inc(a_scaled.sem, 1)
                    kept = w1[:, :].rearrange("p (c n two b) -> p c n two b", c=NC, two=2, b=b)[:, :, :, 1, :]
                    after(dve, a_kept, turn, 2 + l)
                    select(kept, over_chunks(l, NC, b),
                           work[2 + l % 2][:, :].rearrange("p (c n b) -> p c n b", c=NC, b=b)).then_inc(a_kept.sem, 1)
                    after(dve, a_scaled, turn, done + 3)
                    fill()
                fill()
                for c in range(NC - 1):
                    if c % HC == 0:
                        after(dve, a_kv, turn, c // HC + 1)
                    kv, now = in_half(work[2 + c // HC], c), chunk(w2, c)
                    if c == 0:
                        dve.tensor_copy(now, kv).then_inc(a_state.sem, 1)
                    else:
                        after(dve, a_state, turn, c)
                        dve.scalar_tensor_tensor(out=now, in0=chunk(w2, c - 1), scalar=chunk(f_a, c)[:, 0:1],
                                                 in1=kv, op0=ALU.mult, op1=ALU.add).then_inc(a_state.sem, 1)
                fill()
                fill()
                head_out(0, turn, q_a, f_a, gate_a, unit_cols[:, 0, 2:3], fill)

            def gdn(turn, fill):
                uc = unit_cols[:, 1, :]
                after(dve, z_ready[1], turn, 4)
                taps = cols[:, C_CONV:C_CONV + TAPS * 3 * HEADS].rearrange("p (f j) -> p f j", j=HEADS)
                dve.tensor_copy(uc[:, 0:3 * TAPS], taps[:, :, bass.ds(turn, 1)].rearrange("p f j -> p (f j)"))\
                    .then_inc(b_cols.sem, 1)
                dve.tensor_copy(uc[:, 12:13], cols[:, bass.ds(turn + C_HEAD + HEADS, 1)]).then_inc(b_cols.sem, 1)
                dve.tensor_copy(head_cols[:, 0:2, :],
                                gcols[:, :, :, bass.ds(turn, 1)].rearrange("p a c h -> p a (c h)")).then_inc(b_cols.sem, 1)
                after(dve, b_cols, turn, 3)
                for i in range(TAPS):
                    tap = TAPS - 1 - i
                    for m in range(3):
                        src = zb[:, m, tap:tap + T]
                        w = uc[:, 3 * tap + m:3 * tap + m + 1]
                        if i == 0:
                            dve.tensor_scalar(cv[:, m, :], src, w, None, ALU.mult).then_inc(b_conv.sem, 1)
                        else:
                            after(dve, b_conv, turn, 3 * (i - 1) + m + 1)
                            dve.scalar_tensor_tensor(out=cv[:, m, :], in0=src, scalar=w, in1=cv[:, m, :],
                                                     op0=ALU.mult, op1=ALU.add).then_inc(b_conv.sem, 1)
                for at in (0, 32):
                    dve.tensor_scalar(w2[at:at + HEADS, :], rows[at:at + HEADS, :],
                                      ident[at:at + HEADS, bass.ds(turn + at, 1)], None, ALU.mult)\
                        .then_inc(b_rows.sem, 1)
                for i in range(2):
                    after(dve, b_rooted, turn, 2 * i + 2)
                    dve.reciprocal(raw[i], raw[i]).then_inc(b_normed.sem, 1)
                    after(dve, b_normed, turn, 2 * i + 1)
                    dve.scalar_tensor_tensor(out=cv[:, i, :], in0=cv[:, i, :], scalar=(P ** -0.5, 1.0)[i],
                                             in1=raw[i], op0=ALU.mult, op1=ALU.mult).then_inc(b_normed.sem, 1)
                fill()
                after(dve, b_normed, turn, 4)
                after(dve, b_spread, turn, 2)
                for h in range(2):
                    dve.scalar_tensor_tensor(out=half(raw[1], h), in0=half(k_b, h), scalar=-1.0,
                                             in1=work[2 + h][:, :], op0=ALU.mult, op1=ALU.mult)\
                        .then_inc(b_keyed.sem, 1)
                after(dve, b_decay, turn, 2)
                for c in range(NC):
                    dve.tensor_scalar(chunk(raw[2], c), in_half(work[c // HC], c), head_cols[:, 0, c:c + 1], 0.0,
                                      ALU.subtract, ALU.min).then_inc(b_diff.sem, 1)
                for h in range(2):
                    ends = work[h][:, :].rearrange("p (c t) -> p c t", t=P)[:, :, P - 1]
                    dve.tensor_tensor(head_cols[:, 3, h * HC:(h + 1) * HC], ends,
                                      head_cols[:, 0, h * HC:(h + 1) * HC], ALU.subtract).then_inc(b_diff.sem, 1)
                fill()
                after(dve, b_exp, turn, 3)
                up = upper[:, :]
                up = bass.AP(up.tensor, up.offset, [list(up.ap[0]), [0, NC], [1, P]])
                decays = raw[2].rearrange("p (c t) -> p c t", t=P)
                dve.tensor_tensor(decays, decays, up, ALU.mult).then_inc(b_masked.sem, 1)
                dve.scalar_tensor_tensor(out=head_cols[:, 2, :], in0=head_cols[:, 2, :], scalar=-1.0,
                                         in1=head_cols[:, 1, :], op0=ALU.mult, op1=ALU.mult).then_inc(b_cols.sem, 1)
                dve.tensor_copy(head_cols[:, 5, :], raw[0].rearrange("p (c t) -> p c t", t=P)[:, :, P - 1])\
                    .then_inc(b_cols.sem, 1)
                after(dve, b_cols, turn, 5)
                after(dve, b_masked, turn, 1)
                for i in range(2):
                    for h in range(2):
                        after(dve, b_prod, turn, 2 * i + h + 1)
                        dve.tensor_tensor(half(raw[1 + i], h), work[2 * i + h][:, :], half(raw[2], h), ALU.mult)\
                            .then_inc(b_scores.sem, 1)
                fill()
                dve.tensor_tensor(q_b, q_b, raw[0], ALU.mult).then_inc(b_qdec.sem, 1)
                for i, (dst, col) in enumerate(((v_b, 1), (raw[0], 3))):
                    for h in range(2):
                        after(dve, b_turned, turn, 2 * i + h + 1)
                        if i:
                            after(dve, b_qdec, turn, 1)
                        v = head_cols[:, col, h * HC:(h + 1) * HC]
                        v = bass.AP(v.tensor, v.offset, [list(v.ap[0]), list(v.ap[1]), [0, P]])
                        dve.tensor_tensor(half(dst, h).rearrange("p (c t) -> p c t", t=P),
                                          work[2 * i + h][:, :].rearrange("p (c t) -> p c t", t=P), v, ALU.mult)\
                            .then_inc(b_vk.sem, 1)
                fill()

                def grow(t, n_mask, h, data):
                    return select(half(t, h).rearrange("p (c t) -> p c t", t=P), over_chunks(n_mask, HC),
                                  data.rearrange("p (c t) -> p c t", t=P)).then_inc(b_inv.sem, 1)

                after(dve, b_ident, turn, 2)
                for l in range(LEVELS):
                    if l == 0:
                        for h in range(2):
                            after(dve, b_u, turn, h + 1)
                            grow(w1, LEVELS, h, work[2 * h][:, :])
                            grow(w3, 0, h, half(raw[1], h))
                    else:
                        fill()
                        n = 4 * (l - 1)
                        for h in range(2):
                            after(dve, b_inv, turn, 4 * l)
                            if l < LEVELS - 1:
                                after(dve, b_y, turn, n + 2 * h + 1)
                                grow(w1, LEVELS + l, h, work[2 * h + 1][:, :])
                                after(dve, b_y, turn, n + 2 * h + 2)
                            else:
                                after(dve, b_y, turn, n + h + 1)
                            grow(w3, l, h, work[2 * h][:, :])
                    fill()
                for c in range(NC):
                    if c:
                        after(dve, c_ks, turn, c)
                        dve.scalar_tensor_tensor(out=chunk(v_b, c), in0=work[0][:, 0:P], scalar=head_cols[:, 2, c:c + 1],
                                                 in1=chunk(v_b, c), op0=ALU.mult, op1=ALU.add).then_inc(c_r.sem, 1)
                    if c < NC - 1:
                        after(dve, c_kv, turn, c + 1)
                        if c == 0:
                            dve.tensor_copy(state[:, 1, :], work[0][:, 0:P]).then_inc(c_state.sem, 1)
                        else:
                            dve.scalar_tensor_tensor(out=state[:, (c + 1) % 2, :], in0=state[:, c % 2, :],
                                                     scalar=head_cols[:, 5, c:c + 1], in1=work[0][:, 0:P],
                                                     op0=ALU.mult, op1=ALU.add).then_inc(c_state.sem, 1)
                    if c % 2:
                        fill()
                head_out(1, turn, q_b, raw[0], zg[:, :], uc[:, 12:13], fill)
                fill()

            def even_turn(turn, last):
                place = EVEN(turn)
                w = turn_steps(EVEN_N, last)
                steps = sum(w, [])
                hgrn(turn, Filler(w[0], 0, place, steps, FILLS_A, None, evac))
                gdn(turn, Filler(w[1], len(w[0]), place, steps, FILLS_B, None, evac))
                Filler(w[2], len(w[0]) + len(w[1]), place, steps, 1, None, evac)()

            turns(dve, HEADS, even_turn)

            def ple(i, place, n_norm):
                norm(n_norm)
                for k in range(KP):
                    for h in range(2):
                        after(dve, p_high, i, 2 * k + h + 1)
                        dve.tensor_tensor(half(yl[:, k, :], h), work[2 * k + h][:, :],
                                          half(yh[:, k, :].bitcast(F32), h), ALU.subtract).then_inc(p_low.sem, 1)
                for n in range(KD):
                    local = KD + n
                    pair = place.pair(local)
                    g = gate_tile(n)
                    dve.wait_ge(dense_ready.sem, place.ready(local))
                    dve.tensor_tensor(half(g, 0), dense[2 * pair][:, :], half(g, 0), ALU.mult).then_inc(p_prod.sem, 1)
                    dve.tensor_tensor(half(g, 1), dense[2 * pair + 1][:, :], half(g, 1), ALU.mult)\
                        .then_inc(taken[pair].sem, 1)
                    dve.wait_ge(taken[pair].sem, place.taken(local))
                    dve.tensor_tensor(x[:, n, :], x[:, n, :], g, ALU.add).then_inc(p_added.sem, 1)

            ple(0, PLE0, 1)
            after(dve, p_added, 0, KD)
            norm(2)

            def lru(u, turn, fill):
                uc = unit_cols[:, u, :]
                xc, a, gx, th, h_t = cv[:, 0, :], cv[:, 1, :], cv[:, 2, :], za[:, 2, :], za[:, 3, :]
                after(dve, lz_ready[u], turn, 2)
                v = cols[:, C_ODD:C_ODD + 8 * BLOCKS].rearrange("p (f i u) -> p f i u", u=2, i=TURNS)
                dve.tensor_copy(uc[:, 0:8], v[:, :, bass.ds(turn, 1), u].rearrange("p f i -> p (f i)"))\
                    .then_inc(l_cols[u].sem, 1)
                after(dve, l_cols[u], turn, 1)
                for i in range(TAPS):
                    tap = TAPS - 1 - i
                    src = zb[:, u, tap:tap + T]
                    if i == 0:
                        dve.tensor_scalar(uc[:, 8:9], uc[:, 7:8], -1.0, None, ALU.mult)
                        dve.tensor_scalar(xc, src, uc[:, tap:tap + 1], uc[:, 4:5], ALU.mult, ALU.add)\
                            .then_inc(l_conv[u].sem, 1)
                    else:
                        after(dve, l_conv[u], turn, i)
                        dve.scalar_tensor_tensor(out=xc, in0=src, scalar=uc[:, tap:tap + 1], in1=xc,
                                                 op0=ALU.mult, op1=ALU.add).then_inc(l_conv[u].sem, 1)
                fill()
                after(dve, l_exp[u], turn, 2)
                dve.tensor_tensor(h_t, a, a, ALU.mult).then_inc(l_vec[u].sem, 1)
                after(dve, l_vec[u], turn, 1)
                dve.scalar_tensor_tensor(out=th, in0=h_t, scalar=1.0, in1=th, op0=ALU.add, op1=ALU.mult)\
                    .then_inc(l_vec[u].sem, 1)
                fill()
                after(dve, l_sig[u], turn, 4)
                dve.tensor_tensor(gx, gx, xc, ALU.mult).then_inc(l_vec[u].sem, 1)
                after(dve, l_root[u], turn, 1)
                dve.memset(th[:, 0:1], 1.0).then_inc(l_vec[u].sem, 1)
                after(dve, l_vec[u], turn, 4)
                dve.tensor_tensor(gx, gx, th, ALU.mult).then_inc(l_vec[u].sem, 1)
                after(dve, l_vec[u], turn, 5)
                dve.tensor_tensor_scan(out=h_t, data0=a, data1=gx, initial=0.0, op0=ALU.mult, op1=ALU.add)\
                    .then_inc(l_vec[u].sem, 1)
                fill()
                after(dve, l_vec[u], turn, 6)
                after(dve, l_silu[u], turn, 1)
                dve.tensor_tensor(h_t, h_t, za[:, u, :], ALU.mult).then_inc(l_vec[u].sem, 1)
                fill()
                after(dve, l_high[u], turn, 1)
                dve.tensor_tensor(yl[:, u, :], h_t, yh[:, u, :].bitcast(F32), ALU.subtract).then_inc(l_y[u].sem, 1)
                fill()

            def odd_turn(turn, last):
                place = ODD(turn)
                w = turn_steps(ODD_N, last)
                steps = sum(w, [])
                lru(0, turn, Filler(w[0], 0, place, steps, FILLS_L, None, evac))
                lru(1, turn, Filler(w[1], len(w[0]), place, steps, FILLS_L, None, evac))
                Filler(w[2], len(w[0]) + len(w[1]), place, steps, 1, None, evac)()

            turns(dve, TURNS, odd_turn)
            ple(1, PLE1, 3)
            after(dve, p_added, 1, KD)
            norm_start(4)
            for k in range(KD):
                dve.scalar_tensor_tensor(out=tiles8[k], in0=x[:, k, :], scalar=cols[:, NORMS[4] + k:NORMS[4] + k + 1],
                                         in1=w3[:, :], op0=ALU.mult, op1=ALU.mult).then_inc(f_scaled.sem, 1)


_INS = ["x", "p", "even_norm", "even_w_in", "hgrn_lb_logits", "gdn_conv_w", "gdn_a_log", "gdn_dt_bias",
        "even_head_norm", "even_w_out", "odd_norm", "odd_w_in", "lru_conv_w", "lru_conv_b", "lru_w_a",
        "lru_b_a", "lru_w_x", "lru_b_x", "lru_lambda", "odd_w_out", "ple_norm", "ple_gate_w", "ple_proj_w",
        "final_norm"]


def kernel(**inputs):
    import numpy as _np
    import concourse.bacc as _bacc
    from concourse import mybir as _mybir
    from concourse.bass_utils import run_bass_kernel_spmd as _run

    nc = _bacc.Bacc("TRN2", target_bir_lowering=False, num_devices=1)
    arrays, args = {}, []
    for name in _INS:
        a = _np.ascontiguousarray(inputs[name])
        arrays[f"in_{name}_dram"] = a
        args.append(nc.dram_tensor(f"in_{name}_dram", a.shape, _mybir.dt.from_np(a.dtype), kind="ExternalInput").ap())
    shape = inputs["x"].shape
    args.append(nc.dram_tensor("out_0_dram", shape, _mybir.dt.from_np(_np.dtype("float32")), kind="ExternalOutput").ap())
    build_trunk(nc, *args)
    r = _run(nc, [arrays], core_ids=[0])
    return r.results[0]["out_0_dram"]
```

```python
from contextlib import ExitStack

import concourse.bass as bass
from concourse import mybir

F32 = mybir.dt.float32
F32R = mybir.dt.float32r
U8 = mybir.dt.uint8
ACT = mybir.ActivationFunctionType
ALU = mybir.AluOpType

P = 128
HALF = 512
CHUNK = 128
LEVELS = 7
EPS = 1e-6
TAPS = 4
PAD = TAPS - 1


class Step:

    def __init__(self, sem, per_turn):
        self.sem, self.per_turn = sem, per_turn

    def at(self, turn, n):
        return turn * self.per_turn + n


def after(eng, step, turn, n):
    eng.wait_ge(step.sem, step.at(turn, n))


def spread(pieces, weights):
    total, sums = sum(weights), [sum(weights[:n + 1]) for n in range(len(weights))]
    return [int(pieces * s / total + 0.5) for s in sums]


def build_trunk(nc, x_in, p_in, even_norm, even_w_in, lb_logits, gdn_conv_w, gdn_a_log, gdn_dt_bias,
                even_head_norm, even_w_out, odd_norm, odd_w_in, lru_conv_w, lru_conv_b, lru_w_a,
                lru_b_a, lru_w_x, lru_b_x, lru_lambda, odd_w_out, ple_norm, ple_gate_w, ple_proj_w,
                final_norm, out):
    _, T, D = x_in.shape
    KD = D // P
    NC = T // CHUNK
    HC = NC // 2
    HEADS = D // P
    BLOCKS = lru_w_a.shape[1]
    KP = p_in.shape[3] // P
    AW = HEADS * P
    GATE0 = 6 * AW + 2 * HEADS
    assert T == 2 * HALF and KD == 8 and NC == 8 and HEADS == 8 and BLOCKS == 2 * HEADS and KP == 2

    with ExitStack() as ctx:
        def sb(name, shape, dt=F32):
            return ctx.enter_context(nc.sbuf_tensor(name, shape, dt))

        def sem(name):
            return ctx.enter_context(nc.semaphore(name))

        def step(name, per_turn):
            return Step(sem(name), per_turn)

        x = sb("x", [P, KD, T])
        xh = sb("xh", [P, KD, T], F32R)
        xl = sb("xl", [P, KD, T], F32R)
        yh = sb("yh", [P, 2, T], F32R)
        yl = sb("yl", [P, 2, T], F32R)
        w_stage = sb("w_stage", [P, T])
        w_high = sb("w_high", [P, 2, T], F32R)
        w_low = sb("w_low", [P, 2, T], F32R)
        za = sb("za", [P, 5, T])
        zb = sb("zb", [P, 3, PAD + T + 1])
        zg = sb("zg", [P, T])
        cv = sb("cv", [P, 3, T])
        w1 = sb("w1", [P, T])
        w2 = sb("w2", [P, T])
        w3 = sb("w3", [P, T])
        rows = sb("rows", [64, T])
        cols = sb("cols", [P, 2 * P + 32])
        lows = sb("lows", [P, 4, HEADS])
        unit_cols = sb("unit_cols", [P, 2, 16])
        gcols = sb("gcols", [P, 2, NC, HEADS])
        head_cols = sb("head_cols", [P, 6, NC])
        state = sb("state", [P, 2, P])
        ident = sb("ident", [P, P])
        upper = sb("upper", [P, P])
        ones = sb("ones", [P, P])
        masks = sb("masks", [P, 2 * LEVELS + 1, P], U8)
        tiny = sb("tiny", [P, 4])

        dense = [ctx.enter_context(nc.psum_tensor(f"dense{i}", [P, HALF], F32)) for i in range(4)]
        work = [ctx.enter_context(nc.psum_tensor(f"work{i}", [P, HALF], F32)) for i in range(4)]

        def half(t, h):
            return t[:, h * HALF:(h + 1) * HALF]

        def chunk(t, c):
            return t[:, c * CHUNK:(c + 1) * CHUNK]

        def in_half(bank, c):
            return bank[:, (c % HC) * CHUNK:(c % HC + 1) * CHUNK]

        q_a, f_a, v_a, gate_a, k_a = (za[:, n, :] for n in range(5))
        q_b, k_b, v_b = (cv[:, n, :] for n in range(3))
        raw = [zb[:, n, PAD:PAD + T] for n in range(3)]
        tiles8 = [za[:, n, :] for n in range(5)] + [cv[:, n, :] for n in range(3)]

        C_CONV, C_HEAD, C_NORM, C_LB = 0, TAPS * 3 * HEADS, TAPS * 3 * HEADS + 2 * HEADS, P - HEADS
        C_ODD = P
        C_TAIL = 2 * P
        NORMS = [C_NORM, C_TAIL + 8, C_TAIL, C_TAIL + 16, C_TAIL + 24]

        def pairs(i):
            return head_cols[:, :, :].rearrange("p a c -> p (a c)")[:, i * BLOCKS:(i + 1) * BLOCKS]

        def squares(n, k):
            return raw[k % 2] if n in (2, 4) else (w1, w2)[k % 2][:, :]

        MADE = 6 + 6 * LEVELS + 2

        made = step("constants_made", 0)
        cleared = step("padding_cleared", 0)
        small_in = step("small_inputs_loaded", 0)
        vec_in = step("vectors_loaded", 0)
        vec_turned = step("vectors_turned", 0)
        vec_kept = step("vectors_kept", 0)
        vec_ready = step("vector_work_done", 0)
        x_loaded = step("x_loaded", 0)
        x_turned = step("x_turned", 0)
        x_kept = [step(f"x_half{h}_kept", 0) for h in range(2)]
        masks_ready = step("masks_ready", 0)
        split_begun = step("split_begun", 0)
        select_begun = step("select_begun", 0)
        w_in = step("weights_loaded", 0)
        w_split_high = step("weights_split_high", 0)
        w_split = step("weights_split", 0)
        dense_ready = step("dense_ready", 0)
        taken = [step(f"dense_taken{n}", 0) for n in range(2)]
        norm_squared = step("norm_squared", KD)
        norm_summed = step("norm_summed", KD)
        norm_rooted = step("norm_rooted", 2)
        norm_inverse = step("norm_inverse", 2)
        norm_scaled = step("norm_scaled", KD)
        norm_high = step("norm_high", KD)
        norm_low = step("norm_low", KD)
        row_step = step("row_step_scalar", 0)
        row_vec = step("row_step_vector", 0)
        row_turned = step("rows_turned", 0)
        row_cols = step("row_columns_kept", 0)
        z_ready = [step("unit_a_projected", 4), step("unit_b_projected", 4)]
        a_gates = step("hgrn_gates", 3)
        a_cols = step("hgrn_columns", 1)
        a_bounded = step("hgrn_bounded", 3)
        a_scores = step("hgrn_scores", 1 + LEVELS)
        a_kept = step("hgrn_scores_kept", 2 + LEVELS)
        a_scaled = step("hgrn_scaled", 1 + 3 * LEVELS)
        a_turned = step("hgrn_turned", 4)
        a_values = step("hgrn_values_turned", 2)
        a_keys = step("hgrn_keys_turned", 2)
        a_kv = step("hgrn_key_values", 2)
        a_state = step("hgrn_states", NC - 1)
        mixed = [step("hgrn_mixed", 2), step("gdn_mixed", 2)]
        o_kept = [step("hgrn_output_kept", 4), step("gdn_output_kept", 4)]
        o_summed = [step("hgrn_output_summed", 2), step("gdn_output_summed", 2)]
        o_rooted = [step("hgrn_output_rooted", 2), step("gdn_output_rooted", 2)]
        o_scaled = [step("hgrn_output_scaled", 3), step("gdn_output_scaled", 3)]
        y_high = [step("hgrn_y_high", 1), step("gdn_y_high", 1)]
        y_ready = [step("hgrn_y_ready", 1), step("gdn_y_ready", 1)]
        b_cols = step("gdn_columns", 5)
        b_conv = step("gdn_convolved", 3 * TAPS)
        b_silu = step("gdn_silu", 4)
        b_squared = step("gdn_squared", 2)
        b_summed = step("gdn_summed", 4)
        b_rooted = step("gdn_rooted", 4)
        b_normed = step("gdn_normed", 4)
        b_rows = step("gdn_rows_picked", 2)
        b_spread = step("gdn_rows_spread", 2)
        b_decay = step("gdn_decay_rows", 2)
        b_keyed = step("gdn_keys_scaled", 2)
        b_diff = step("gdn_decay_differences", NC + 2)
        b_exp = step("gdn_decay_exponentials", 3)
        b_masked = step("gdn_decays_masked", 1)
        b_prod = step("gdn_products", 4)
        b_scores = step("gdn_scores", 4)
        b_qdec = step("gdn_queries_decayed", 1)
        b_turned = step("gdn_turned", 4)
        b_vk = step("gdn_values_and_keys_turned", 4)
        b_ident = step("inverse_started", 2)
        b_u = step("inverse_right_factor", 2 * LEVELS)
        b_ukept = step("inverse_right_factor_kept", 2 * (LEVELS - 1))
        b_y = step("inverse_products", 2 * (2 * (LEVELS - 1)) - 2)
        b_inv = step("inverse_grown", 4 * LEVELS - 2)
        c_ks = step("chain_read_state", NC - 1)
        c_r = step("chain_residue", NC - 1)
        c_v = step("chain_value", NC)
        c_vn = step("chain_value_kept", NC)
        c_kv = step("chain_state_change", NC - 1)
        c_state = step("chain_state", NC - 1)
        l_in = [step(f"lru{u}_weights_loaded", 32) for u in range(2)]
        l_cols = [step(f"lru{u}_columns", 1) for u in range(2)]
        l_silu = [step(f"lru{u}_gate_silu", 1) for u in range(2)]
        l_conv = [step(f"lru{u}_convolved", TAPS) for u in range(2)]
        l_gates = [step(f"lru{u}_gate_products", 2) for u in range(2)]
        l_sig = [step(f"lru{u}_gates", 4) for u in range(2)]
        l_exp = [step(f"lru{u}_decays", 2) for u in range(2)]
        l_vec = [step(f"lru{u}_vector_steps", 7) for u in range(2)]
        l_root = [step(f"lru{u}_rooted", 1) for u in range(2)]
        l_high = [step(f"lru{u}_y_high", 1) for u in range(2)]
        l_y = [step(f"lru{u}_y_ready", 1) for u in range(2)]
        lz_ready = [step(f"lru{u}_projected", 2) for u in range(2)]
        l_lam = step("lambda_steps", 0)
        p_loaded = step("ple_input_loaded", 0)
        p_turned = step("ple_input_turned", 4)
        p_high = step("ple_input_high", 4)
        p_low = step("ple_input_low", 4)
        p_proj = step("ple_projection_kept", KD)
        p_gate = step("ple_gates", KD)
        p_prod = step("ple_gated", KD)
        p_added = step("ple_added", KD)
        f_scaled = step("final_scaled", KD)
        f_turned = step("final_turned", 2 * NC)
        f_kept = step("final_kept", 2 * NC)
        stored = [step(f"output{n}_stored", 0) for n in range(2)]

        def proj(u, n):
            return [("P", u, i) for i in range(n)]

        def outp(u):
            return [("O", u, n) for n in range(KD)]

        def turn_steps(n, first, last):
            now, ahead = proj(1, n), [] if last else proj(0, n)
            late = [] if first else [("V", 1, r) for r in range(KD)]
            return [now[:n // 2] + late + now[n // 2:], ahead[:n // 2] + outp(0) + ahead[n // 2:]]

        def n_steps(n, first=False, last=False):
            return sum(len(w) for w in turn_steps(n, first, last))

        def n_tiles(n, first=False, last=False):
            return sum(kind == "P" or r == 0 for w in turn_steps(n, first, last) for kind, _, r in w)

        class Place:

            def __init__(self, step0, tile0, steps=0, tiles=0, turn=0):
                self.step0, self.tile0, self.steps, self.tiles, self.turn = step0, tile0, steps, tiles, turn

            def ready(self, local):
                return self.turn * self.steps + (self.step0 + local + 1)

            def pair(self, local):
                return (self.step0 + local) % 2

            def taken(self, local):
                s = self.step0 + local
                return self.turn * (self.steps // 2) + (s - s % 2) // 2 + 1

            def split(self, local):
                return self.turn * self.tiles + (self.tile0 + local + 1)

            def slot(self, local):
                return (self.tile0 + local) % 2

        def tile_of(steps, local):
            t = -1
            for kind, _, n in steps[:local + 1]:
                t += kind in "PG" or n == 0
                t += kind == "J" and n == 1
            return t

        EVEN_N, ODD_N = 4, 2
        TURNS = BLOCKS // 2

        def places(step0, tile0, n, count):
            def at(turn):
                return Place(step0 + n_steps(n, first=True) - n_steps(n), tile0 + n_tiles(n, first=True) - n_tiles(n),
                             n_steps(n), n_tiles(n), turn)

            def of_turn(turn):
                return Place(step0, tile0, n_steps(n), n_tiles(n), 0) if isinstance(turn, int) and turn == 0 else at(turn)

            last = at(count - 1)
            last.step0 += n_steps(n, last=True)
            last.tile0 += n_tiles(n, last=True)
            return of_turn, last

        PRE_EVEN = Place(0, 0)
        EVEN, EVEN_TAIL = places(1 + EVEN_N, 1 + EVEN_N, EVEN_N, HEADS)
        after_even = (EVEN_TAIL.ready(KD - 1), EVEN_TAIL.split(0))
        PLE_STEPS = [("J", 0, n) for n in range(KD)] + [("G", 0, n) for n in range(KD)]
        PLE_TILES = KD + KP
        PLE0 = Place(*after_even)
        after_ple0 = (after_even[0] + 2 * KD, after_even[1] + PLE_TILES)
        PRE_ODD = Place(*after_ple0)
        ODD, ODD_TAIL = places(after_ple0[0] + ODD_N, after_ple0[1] + ODD_N, ODD_N, TURNS)
        PLE1 = Place(ODD_TAIL.ready(KD - 1), ODD_TAIL.split(0))

        def turns(eng, count, body):
            body(0, True, False)
            with eng.Fori(1, count - 1) as turn:
                body(turn, False, False)
            body(count - 1, False, True)

        FILLS_A = [24] + [4.3] * 13
        FILLS_B = [20, 6, 16, 3, 2] + [0.6] * 13 + [1] * 15 + [3, 3, 4]
        FILLS_L = [9, 5, 5, 5, 4, 4]

        class Filler:

            def __init__(self, window, local0, place, steps, points, piece, done):
                self.pieces = [(i, k) for i, s in enumerate(window) for k in range(2 * KD if s[0] == "P" else 2)]
                self.upto = spread(len(self.pieces), points)
                self.at = self.point = 0
                self.window, self.local0, self.place, self.steps = window, local0, place, steps
                self.piece, self.done = piece, done

            def __call__(self):
                while self.at < self.upto[self.point]:
                    i, k = self.pieces[self.at]
                    last = k == (2 * KD - 1 if self.window[i][0] == "P" else 1)
                    if self.piece:
                        self.piece(self.window[i], self.local0 + i, k, last, self.place, self.steps)
                    if self.done and last:
                        self.done(self.window[i], self.local0 + i, self.place)
                    self.at += 1
                self.point += 1

            def finish(self):
                assert self.point == len(self.upto) and self.at == len(self.pieces)

        block = ctx.enter_context(nc.Block())

        @block.sync
        def _(sp):
            def load_rows(src, slot, at):
                n = src.shape[0]
                sp.dma_start(w1[at:at + n, slot * P:(slot + 1) * P], src).then_inc(vec_in.sem, 16)

            load_rows(gdn_conv_w[0].rearrange("t (m q) -> (t m) q", q=P), 0, C_CONV)
            load_rows(even_head_norm[0].rearrange("(m q) -> m q", q=P), 0, C_HEAD)
            load_rows(even_norm[0].rearrange("(m q) -> m q", q=P), 0, C_NORM)
            load_rows(lb_logits[0].rearrange("(m q) -> m q", q=P), 0, C_LB)
            load_rows(lru_conv_w[0].rearrange("t (m q) -> (t m) q", q=P), 1, 0)
            for i, v in enumerate((lru_conv_b, lru_b_a, lru_b_x, lru_lambda)):
                load_rows(v[0].rearrange("(m q) -> m q", q=P), 1, (TAPS + i) * BLOCKS)
            load_rows(odd_norm[0].rearrange("(m q) -> m q", q=P), 2, 0)
            load_rows(ple_norm.rearrange("d (m q) -> (d m) q", q=P), 2, 8)
            load_rows(final_norm.rearrange("(m q) -> m q", q=P), 2, 24)
            sp.dma_start(tiny[0:HEADS, 1:2], gdn_a_log.rearrange("a (h b) -> (a h) b", b=1)).then_inc(small_in.sem, 16)
            sp.dma_start(tiny[0:HEADS, 2:3], gdn_dt_bias.rearrange("a (h b) -> (a h) b", b=1)).then_inc(small_in.sem, 16)

            def load(src, before, width=P):
                if before is not None:
                    sp.wait_ge(w_split.sem, before)
                dst = w_stage[:, :] if len(src.shape) == 2 else w_stage[:, :].rearrange("p (k n) -> p k n", n=P)
                sp.dma_start(dst, src).then_inc(w_in.sem, 16)

            def columns(w, at):
                return w[:, at].rearrange("(k p) n -> p k n", p=P)

            w_even = even_w_in[0]
            sp.wait_ge(cleared.sem, 1)
            stage3 = w_stage[:, :].rearrange("p (k n) -> p k n", n=P)
            for i, at in enumerate((0, 32)):
                sp.dma_start(stage3[:, :, at:at + HEADS],
                             w_even[:, 6 * AW + i * HEADS:6 * AW + (i + 1) * HEADS].rearrange("(k p) n -> p k n", p=P))\
                    .then_inc(w_in.sem, 16)
            starts = ([0, AW, 2 * AW, GATE0], [3 * AW, 4 * AW, 5 * AW, GATE0 + AW])

            def even_columns(u, n, head):
                return w_even[:, bass.ds(starts[u][n] + head * P, P)].rearrange("(k p) n -> p k n", p=P)

            def odd_columns(u, n, turn):
                at = n * BLOCKS * P + u * P
                return odd_w_in[0][:, bass.ds(at + turn * (2 * P), P)].rearrange("(k p) n -> p k n", p=P)

            for n in range(EVEN_N):
                load(even_columns(0, n, 0), 1 + n)

            def even_turn(turn, first, last):
                place, tile = EVEN(turn), 0
                for kind, u, n in sum(turn_steps(EVEN_N, first, last), []):
                    if kind == "P":
                        load(even_columns(u, n, turn + 1 if u == 0 else turn), place.split(tile - 1))
                        tile += 1
                    elif n == 0:
                        load(even_w_out[0][bass.ds(turn * P + (AW - P if kind == "V" else 0), P), :],
                             place.split(tile - 1))
                        tile += 1

            turns(sp, HEADS, even_turn)
            load(even_w_out[0][AW + (HEADS - 1) * P:AW + HEADS * P, :], EVEN_TAIL.split(-1))

            def load_ple(i, place):
                sp.dma_start(cv[:, 0:2, :].rearrange("p a b -> p (a b)").rearrange("p (c q) -> p c q", q=KP * P),
                             p_in[i, 0].rearrange("(c t) q -> t c q", t=P)).then_inc(p_loaded.sem, 16)
                for n in range(KP):
                    load(ple_proj_w[i][n * P:(n + 1) * P, :], place.split(n - 1))
                for n in range(KD):
                    load(ple_gate_w[i][:, n * P:(n + 1) * P].rearrange("(k p) n -> p k n", p=P), place.split(KP + n - 1))

            sp.wait_ge(y_ready[1].sem, HEADS)
            load_ple(0, PLE0)

            def load_gates(turn, u):
                sp.dma_start(w1[:, :].rearrange("p (a b) -> p a b", b=P)[:, 2 * u, :],
                             lru_w_a[0][bass.ds(turn * 2 + u, 1)].rearrange("g i j -> i (g j)")).then_inc(l_in[u].sem, 16)
                sp.dma_start(w1[:, :].rearrange("p (a b) -> p a b", b=P)[:, 2 * u + 1, :],
                             lru_w_x[0][bass.ds(turn * 2 + u, 1)].rearrange("g i j -> i (g j)")).then_inc(l_in[u].sem, 16)

            for n in range(ODD_N):
                load(odd_columns(0, n, 0), PRE_ODD.split(n - 1))
            after(sp, norm_low, 2, KD)
            for u in range(2):
                load_gates(0, u)

            def odd_turn(turn, first, last):
                place, tile = ODD(turn), 0
                for kind, u, n in sum(turn_steps(ODD_N, first, last), []):
                    if kind == "P":
                        load(odd_columns(u, n, turn + 1 if u == 0 else turn), place.split(tile - 1))
                        tile += 1
                    elif n == 0:
                        load(odd_w_out[0][bass.ds(turn * (2 * P) - (P if kind == "V" else 0), P), :],
                             place.split(tile - 1))
                        tile += 1
                        if kind == "V":
                            after(sp, l_y[1], turn, 0)
                            load_gates(turn, 1)
                        elif not last:
                            after(sp, l_y[0], turn, 1)
                            load_gates(turn + 1, 0)

            turns(sp, TURNS, odd_turn)
            load(odd_w_out[0][(BLOCKS - 1) * P:BLOCKS * P, :], ODD_TAIL.split(-1))
            sp.wait_ge(l_y[1].sem, TURNS)
            load_ple(1, PLE1)

            for c in range(NC):
                sp.wait_ge(f_kept.sem, 2 * c + 2)
                sp.dma_start(out[0, c * P:(c + 1) * P, :], (w1, w2)[c % 2][:, :]).then_inc(stored[c % 2].sem, 16)
            for n in range(2):
                sp.wait_ge(stored[n].sem, 16 * NC // 2)

        @block.gpsimd
        def _(pool):
            build = zb[:, :, :].rearrange("p a b -> p (a b)")[:, 0:(2 * LEVELS + 1) * P].rearrange("p (a b) -> p a b", b=P)
            count = [0]

            def link(ins):
                count[0] += 1
                ins.then_inc(made.sem, 1)
                pool.wait_ge(made.sem, count[0])

            pool.memset(w_stage[:, :], 0.0).then_inc(cleared.sem, 1)
            link(pool.memset(ones[:, :], 1.0))
            link(pool.memset(ident[:, :], 0.0))
            link(pool.affine_select(out=ident[:, :], in_=ident[:, :], compare_op=ALU.not_equal, fill=1.0,
                                    base=0, pattern=[[-1, P]], channel_multiplier=1))
            link(pool.memset(upper[:, :], 1.0))
            link(pool.affine_select(out=upper[:, :], in_=upper[:, :], compare_op=ALU.is_ge, fill=0.0,
                                    base=0, pattern=[[1, P]], channel_multiplier=-1))
            link(pool.memset(build[:, :, :], 0.0))
            for l in range(LEVELS):
                b = 1 << l
                n = P // (2 * b)
                right = build[:, l, :].rearrange("p (n two b) -> p n two b", two=2, b=b)[:, :, 1, :]
                left = build[:, LEVELS + l, :].rearrange("p (n two b) -> p n two b", two=2, b=b)[:, :, 0, :]
                for v, off in ((right, 0), (left, b)):
                    link(pool.memset(v, 1.0))
                    link(pool.affine_select(out=v, in_=v, compare_op=ALU.is_ge, fill=0.0, base=-off,
                                            pattern=[[-2 * b, n], [0, b]], channel_multiplier=1))
                    link(pool.affine_select(out=v, in_=v, compare_op=ALU.is_ge, fill=0.0, base=off + b - 1,
                                            pattern=[[2 * b, n], [0, b]], channel_multiplier=-1))
            link(pool.tensor_copy(build[:, 2 * LEVELS, :], ident[:, :]))
            pool.memset(tiny[:, 0:1], EPS).then_inc(made.sem, 1)
            assert count[0] + 1 == MADE

            def split(slot, loaded, used):
                pool.wait_ge(w_in.sem, loaded)
                if used is not None:
                    pool.wait_ge(dense_ready.sem, used)
                pool.sem_inc(split_begun.sem, 1)
                pool.tensor_scalar(w_high[:, slot, :], w_stage[:, :], 1.0, 0.0, ALU.mult, ALU.add)\
                    .then_inc(w_split_high.sem, 1)

            def rest(slot, n):
                pool.wait_ge(w_split_high.sem, n)
                pool.tensor_tensor(w_low[:, slot, :], w_stage[:, :], w_high[:, slot, :].bitcast(F32),
                                   ALU.subtract).then_inc(w_split.sem, 1)

            def tile(place, local, used):
                slot = place.slot(local)
                n = place.split(local)
                split(slot, place.turn * (16 * place.tiles) + 16 * (place.tile0 + local + 2), used)
                rest(slot, n)

            tile(PRE_EVEN, 0, None)
            tile(PRE_EVEN, 1, None)
            for n in range(1, EVEN_N):
                tile(PRE_EVEN, 1 + n, n)

            def turn_tiles(place, n_cols, first, last):
                steps = sum(turn_steps(n_cols, first, last), [])
                final = [max(i for i in range(len(steps)) if tile_of(steps, i) == t)
                         for t in range(tile_of(steps, len(steps) - 1) + 1)]
                for t in range(len(final)):
                    tile(place, t, place.ready(final[t - 2] if t >= 2 else t - 2))

            turns(pool, HEADS, lambda turn, first, last: turn_tiles(EVEN(turn), EVEN_N, first, last))
            tile(EVEN_TAIL, 0, EVEN_TAIL.ready(-KD - 1))

            def ple_tiles(place):
                for n in range(KP + KD):
                    if n < KP:
                        used = place.ready((-9, -1)[n])
                    elif n < 2 * KP:
                        used = place.ready(KD - 1)
                    else:
                        used = place.ready(KD + n - 2 * KP)
                    tile(place, n, used)

            ple_tiles(PLE0)
            for n in range(ODD_N):
                tile(PRE_ODD, n, PRE_ODD.ready(n - 2))
            turns(pool, TURNS, lambda turn, first, last: turn_tiles(ODD(turn), ODD_N, first, last))
            tile(ODD_TAIL, 0, ODD_TAIL.ready(-KD - 1))
            ple_tiles(PLE1)

        @block.tensor
        def _(pe):
            def three(out_, wh, wl, xh_, xl_, first, last):
                pe.matmul(out_, wh, xh_, start=first, stop=False)
                pe.matmul(out_, wh, xl_, start=False, stop=False)
                return pe.matmul(out_, wl, xh_, start=False, stop=last)

            def piece(what, local, n_piece, last, place, steps):
                kind, u, n = what
                k, h = divmod(n_piece, 2)
                pair = place.pair(local)
                slot = place.slot(tile_of(steps, local))
                if n_piece == 0:
                    pe.wait_ge(w_split.sem, place.split(tile_of(steps, local)))
                    if not (isinstance(place.turn, int) and place.taken(local) < 2):
                        pe.wait_ge(taken[pair].sem, place.taken(local) - 1)
                    if kind in "OV" and n == 0:
                        y = y_ready if place.steps == n_steps(EVEN_N) else l_y
                        after(pe, y[u], place.turn, 0 if kind == "V" else 1)
                bank = dense[2 * pair + h]
                if kind in "PG":
                    w = slice(k * P, (k + 1) * P)
                    r = three(bank[:, :], w_high[:, slot, w], w_low[:, slot, w],
                              half(xh[:, k, :], h), half(xl[:, k, :], h), k == 0, k == KD - 1)
                else:
                    w = slice(n * P, (n + 1) * P)
                    r = three(bank[:, :], w_high[:, slot, w], w_low[:, slot, w],
                              half(yh[:, u, :], h), half(yl[:, u, :], h), True, True)
                if last:
                    r.then_inc(dense_ready.sem, 1)

            def norm_sum(n, k):
                after(pe, norm_squared, n, k + 1)
                for h in range(2):
                    r = pe.matmul(work[h][:, :], ones[:, :], half(squares(n, k), h), start=k == 0, stop=k == KD - 1)
                r.then_inc(norm_summed.sem, 1)

            def turn_all(src, banks, st):
                for c in range(NC):
                    r = pe.transpose(in_half(banks[c // HC], c), chunk(src, c), ident[:, :])
                    if c % HC == HC - 1:
                        r.then_inc(st.sem, 1)

            pe.wait_ge(vec_in.sem, 16 * 12)
            pe.wait_ge(made.sem, MADE)
            for i, n in enumerate((P, P, 32)):
                r = pe.transpose(work[0][:, i * P:i * P + n], w1[0:n, i * P:(i + 1) * P], ident[0:n, 0:n])
            r.then_inc(vec_turned.sem, 1)
            pe.wait_ge(x_loaded.sem, 16 * NC)
            for k in range(KD + 2):
                if k < KD:
                    for h in range(2):
                        if k >= 2:
                            pe.wait_ge(x_kept[h].sem, k - 1)
                        for c in range(HC):
                            r = pe.transpose(in_half(dense[2 * (k % 2) + h], c),
                                             tiles8[h * HC + c][:, k * P:(k + 1) * P], ident[:, :])
                        r.then_inc(x_turned.sem, 1)
                if k == 1:
                    pe.wait_ge(vec_kept.sem, 1)
                if k >= 2:
                    norm_sum(0, k - 2)

            first = [("P", 0, 0)] + proj(0, EVEN_N)
            pe.wait_ge(w_split.sem, 1)
            for h in range(2):
                pe.wait_ge(x_kept[h].sem, KD)
            for k in range(KD):
                after(pe, norm_low, 0, k + 1)
                for h in range(2):
                    r = three(dense[h][0:64, :], w_high[:, 0, k * P:k * P + 64], w_low[:, 0, k * P:k * P + 64],
                              half(xh[:, k, :], h), half(xl[:, k, :], h), k == 0, k == KD - 1)
                if k == KD - 1:
                    r.then_inc(dense_ready.sem, 1)
                for h in range(2):
                    piece(first[1], 1, 2 * k + h, k == KD - 1 and h == 1, PRE_EVEN, first)
            for n in range(1, EVEN_N):
                for k in range(2 * KD):
                    piece(first[1 + n], 1 + n, k, k == 2 * KD - 1, PRE_EVEN, first)
            pe.wait_ge(row_vec.sem, 5)
            after(pe, norm_rooted, 0, 2)
            for i in range(2):
                for c in range(NC):
                    at = 32 * i
                    r = pe.transpose(work[i][:, c * HEADS:(c + 1) * HEADS],
                                     rows[at:at + HEADS, c * CHUNK:(c + 1) * CHUNK],
                                     ident[at:at + HEADS, at:at + HEADS])
                r.then_inc(row_turned.sem, 1)

            def head_sum(u, turn, sq):
                for h in range(2):
                    after(pe, o_kept[u], turn, 2 * h + 2)
                    pe.matmul(work[2 + h][:, :], ones[:, :], half(sq, h), start=True, stop=True)\
                        .then_inc(o_summed[u].sem, 1)

            def hgrn(turn, fill):
                fill()
                after(pe, a_bounded, turn, 3)
                for c in range(NC):
                    r = pe.matmul(in_half(work[c // HC], c), chunk(k_a, c), chunk(q_a, c), start=True, stop=True)
                r.then_inc(a_scores.sem, 1)
                fill()
                for l in range(LEVELS):
                    b = 1 << l
                    after(pe, a_scaled, turn, 1 + 3 * l)
                    if l >= 2:
                        after(pe, a_kept, turn, 2 + l - 1)
                    for c in range(NC):
                        right = chunk(q_a, c).rearrange("p (n two b) -> p n two b", two=2, b=b)[:, :, 1, :]
                        r = pe.matmul(work[2 + l % 2][:, c * 64:(c + 1) * 64], chunk(k_a, c), right,
                                      start=True, stop=True)
                    r.then_inc(a_scores.sem, 1)
                    if l == 0:
                        after(pe, a_kept, turn, 2)
                        turn_all(v_a, work[0:2], a_turned)
                    fill()
                after(pe, a_values, turn, 2)
                after(pe, a_scaled, turn, 1 + 3 * LEVELS)
                turn_all(k_a, work[0:2], a_turned)
                fill()
                for h in range(2):
                    after(pe, a_keys, turn, h + 1)
                    after(pe, a_kept, turn, 2 + LEVELS)
                    for c in range(h * HC, min((h + 1) * HC, NC - 1)):
                        r = pe.matmul(in_half(work[2 + h], c), chunk(k_a, c), chunk(v_a, c), start=True, stop=True)
                    r.then_inc(a_kv.sem, 1)
                fill()
                for h in range(2):
                    for c in range(h * HC, (h + 1) * HC):
                        o = in_half(work[h], c)
                        r = pe.matmul(o, chunk(v_a, c), chunk(w1, c), start=True, stop=c == 0)
                        if c:
                            after(pe, a_state, turn, c)
                            r = pe.matmul(o, w2[:, (c - 1) * P:c * P], chunk(q_a, c), start=False, stop=True)
                    r.then_inc(mixed[0].sem, 1)
                fill()
                after(pe, a_state, turn, NC - 1)
                head_sum(0, turn, f_a)
                fill()
                fill()

            def gdn(turn, fill):
                fill()
                for i in range(2):
                    after(pe, b_squared, turn, i + 1)
                    for h in range(2):
                        pe.matmul(work[2 * i + h][:, :], ones[:, :], half(raw[i], h), start=True, stop=True)\
                            .then_inc(b_summed.sem, 1)
                fill()
                for i in range(2):
                    after(pe, b_rooted, turn, 2 * i + 2)
                    after(pe, b_rows, turn, 2)
                    at = 32 * i
                    for h in range(2):
                        r = pe.matmul(work[2 * i + h][:, :], ones[at:at + HEADS, :],
                                      w2[at:at + HEADS, h * HALF:(h + 1) * HALF], start=True, stop=True)
                    r.then_inc(b_spread.sem, 1)
                fill()
                after(pe, b_normed, turn, 4)
                after(pe, b_diff, turn, NC + 2)
                after(pe, b_keyed, turn, 2)
                for i, other in enumerate((raw[1], q_b)):
                    for c in range(NC):
                        r = pe.matmul(in_half(work[2 * i + c // HC], c), chunk(k_b, c), chunk(other, c),
                                      start=True, stop=True)
                        if c % HC == HC - 1:
                            r.then_inc(b_prod.sem, 1)
                fill()
                after(pe, b_scores, turn, 2)
                after(pe, b_silu, turn, 3)
                turn_all(v_b, work[0:2], b_turned)
                after(pe, b_scores, turn, 4)
                turn_all(k_b, work[2:4], b_turned)
                fill()
                after(pe, b_ident, turn, 2)
                for l in range(LEVELS):
                    for h in range(2):
                        right = work[2 * h]
                        if l == 0:
                            after(pe, b_vk, turn, 4)
                        else:
                            after(pe, b_inv, turn, 4 * l if h else 4 * l - 2)
                        for c in range(h * HC, (h + 1) * HC):
                            r = pe.matmul(in_half(right, c), chunk(raw[1], c),
                                          ident[:, :] if l == 0 else chunk(w1, c), start=True, stop=True)
                        r.then_inc(b_u.sem, 1)
                    if l:
                        fill()
                        for h in range(2):
                            after(pe, b_ukept, turn, 2 * (l - 1) + h + 1)
                            if l < LEVELS - 1:
                                for c in range(h * HC, (h + 1) * HC):
                                    r = pe.matmul(in_half(work[2 * h + 1], c), chunk(w3, c), chunk(w2, c),
                                                  start=True, stop=True)
                                r.then_inc(b_y.sem, 1)
                            for c in range(h * HC, (h + 1) * HC):
                                r = pe.matmul(in_half(work[2 * h], c), chunk(w2, c), chunk(w3, c),
                                              start=True, stop=True)
                            r.then_inc(b_y.sem, 1)
                    fill()
                for c in range(NC):
                    before = state[:, c % 2, :]
                    if c == 0:
                        after(pe, b_inv, turn, 4 * LEVELS - 2)
                    else:
                        after(pe, c_state, turn, c)
                        pe.matmul(work[0][:, 0:P], chunk(k_b, c), before, start=True, stop=True).then_inc(c_ks.sem, 1)
                        fill()
                        after(pe, c_r, turn, c)
                    pe.matmul(work[1][:, 0:P], chunk(w3, c), chunk(v_b, c), start=True, stop=True).then_inc(c_v.sem, 1)
                    fill()
                    after(pe, c_vn, turn, c + 1)
                    if c < NC - 1:
                        pe.matmul(work[0][:, 0:P], chunk(raw[0], c), chunk(w2, c), start=True, stop=True)\
                            .then_inc(c_kv.sem, 1)
                    o = in_half(work[2 + c // HC], c)
                    if c:
                        pe.matmul(o, before, chunk(q_b, c), start=True, stop=False)
                    r = pe.matmul(o, chunk(w2, c), chunk(raw[2], c), start=c == 0, stop=True)
                    if c % HC == HC - 1:
                        r.then_inc(mixed[1].sem, 1)
                after(pe, o_kept[1], turn, 4)
                head_sum(1, turn, raw[0])
                fill()
                fill()
                fill()

            def lru(u, turn, fill):
                fill()
                after(pe, l_in[u], turn, 32)
                after(pe, l_conv[u], turn, TAPS)
                blocks = w1[:, :].rearrange("p (a b) -> p a b", b=P)
                for i in range(2):
                    for h in range(2):
                        r = pe.matmul(work[2 * i + h][:, :], blocks[:, 2 * u + i, :], half(cv[:, 0, :], h),
                                      start=True, stop=True)
                    r.then_inc(l_gates[u].sem, 1)
                for _ in FILLS_L[1:]:
                    fill()

            def even_turn(turn, first, last):
                place = EVEN(turn)
                w = turn_steps(EVEN_N, first, last)
                steps = sum(w, [])
                f = Filler(w[0], 0, place, steps, FILLS_A, piece, None)
                hgrn(turn, f)
                f.finish()
                f = Filler(w[1], len(w[0]), place, steps, FILLS_B, piece, None)
                gdn(turn, f)
                f.finish()

            turns(pe, HEADS, even_turn)
            Filler(outp(1), 0, EVEN_TAIL, outp(1), [1], piece, None)()

            def ple(i, place, n_norm):
                pe.wait_ge(p_loaded.sem, 16 * (i + 1))
                src = cv[:, 0:2, :].rearrange("p a b -> p (a b)").rearrange("p (c q) -> p c q", q=KP * P)
                for k in range(KP):
                    for h in range(2):
                        for c in range(HC):
                            r = pe.transpose(in_half(work[2 * k + h], c), src[:, h * HC + c, k * P:(k + 1) * P],
                                             ident[:, :])
                        r.then_inc(p_turned.sem, 1)
                after(pe, p_low, i, 2)
                for k in range(KD):
                    norm_sum(n_norm, k)
                pe.wait_ge(w_split.sem, place.split(KP - 1))
                after(pe, p_low, i, 4)
                for n in range(KD):
                    pair = place.pair(n)
                    pe.wait_ge(taken[pair].sem, place.taken(n) - 1)
                    for k in range(KP):
                        slot = place.slot(k)
                        w = slice(n * P, (n + 1) * P)
                        for h in range(2):
                            r = three(dense[2 * pair + h][:, :], w_high[:, slot, w], w_low[:, slot, w],
                                      half(yh[:, k, :], h), half(yl[:, k, :], h), k == 0, k == KP - 1)
                    r.then_inc(dense_ready.sem, 1)
                after(pe, norm_rooted, n_norm, 2)
                for n in range(KD + 2):
                    if n < KD:
                        for k in range(2 * KD):
                            if n == 0 and k % 2 == 0:
                                after(pe, norm_low, n_norm, k // 2 + 1)
                            piece(("G", 0, n), KD + n, k, k == 2 * KD - 1, place, PLE_STEPS)
                    if n >= 2:
                        norm_sum(n_norm + 1, n - 2)

            ple(0, PLE0, 1)
            for k in range(KD):
                after(pe, norm_low, 2, k + 1)
                for n in range(ODD_N):
                    for h in range(2):
                        piece(("P", 0, n), n, 2 * k + h, k == KD - 1 and h == 1, PRE_ODD, proj(0, ODD_N))

            def odd_turn(turn, first, last):
                place = ODD(turn)
                w = turn_steps(ODD_N, first, last)
                steps = sum(w, [])
                f = Filler(w[0], 0, place, steps, FILLS_L, piece, None)
                lru(0, turn, f)
                f = Filler(w[1], len(w[0]), place, steps, FILLS_L, piece, None)
                lru(1, turn, f)

            turns(pe, TURNS, odd_turn)
            Filler(outp(1), 0, ODD_TAIL, outp(1), [1], piece, None)()
            ple(1, PLE1, 3)
            after(pe, f_scaled, 0, KD)
            after(pe, norm_rooted, 4, 2)
            for c in range(NC):
                for h in range(2):
                    i = 2 * c + h
                    if i >= 4:
                        pe.wait_ge(f_kept.sem, i - 3)
                    for k in range(KD // 2):
                        r = pe.transpose(in_half(work[i % 4], k), chunk(tiles8[h * (KD // 2) + k], c), ident[:, :])
                    r.then_inc(f_turned.sem, 1)

        @block.scalar
        def _(act):
            eps = tiny[:, 0:1]

            def evac(what, local, place):
                kind, u, n = what
                if kind != "P":
                    return
                pair = place.pair(local)
                odd = place.steps == n_steps(ODD_N) or place is PRE_ODD
                if odd:
                    dst = raw[u] if n == 0 else za[:, u, :]
                elif u == 0:
                    dst = za[:, n, :]
                else:
                    dst = raw[n] if n < 3 else zg[:, :]
                act.wait_ge(dense_ready.sem, place.ready(local))
                if place.steps == n_steps(EVEN_N) and u == 0 and n == 0:
                    after(act, y_ready[0], place.turn, 1)
                if place.steps == n_steps(EVEN_N) and u == 1 and n == 0 and not (
                        isinstance(place.turn, int) and place.turn == 0):
                    after(act, y_ready[1], place.turn, 0)
                act.activation(half(dst, 0), dense[2 * pair][:, :], ACT.Copy)\
                    .then_inc((lz_ready if odd else z_ready)[u].sem, 1)
                act.activation(half(dst, 1), dense[2 * pair + 1][:, :], ACT.Copy).then_inc(taken[pair].sem, 1)

            def norm_root(n):
                for h in range(2):
                    after(act, norm_summed, n, KD)
                    act.activation(half(w3, h), work[h][:, :], ACT.Sqrt, bias=eps, scale=1.0 / D)\
                        .then_inc(norm_rooted.sem, 1)

            def square(n, k):
                if k >= 2:
                    after(act, norm_summed, n, k - 1)
                act.activation(squares(n, k), x[:, k, :], ACT.Square).then_inc(norm_squared.sem, 1)

            def norm(n, split=True):
                norm_root(n)
                if split:
                    for k in range(KD):
                        after(act, norm_scaled, n, k + 1)
                        act.activation(xh[:, k, :], (w1, w2)[k % 2][:, :], ACT.Copy).then_inc(norm_high.sem, 1)

            for c in range(NC):
                act.dma_start(tiles8[c], x_in[0, c * P:(c + 1) * P, :]).then_inc(x_loaded.sem, 16)
            act.wait_ge(vec_turned.sem, 1)
            act.activation(cols[:, :], work[0][:, 0:2 * P + 32], ACT.Copy).then_inc(vec_kept.sem, 1)
            for k in range(KD):
                act.wait_ge(x_turned.sem, 2 * k + 1)
                act.activation(half(x[:, k, :], 0), dense[2 * (k % 2)][:, :], ACT.Copy).then_inc(x_kept[0].sem, 1)
                if k:
                    act.wait_ge(x_kept[0].sem, k)
                    act.wait_ge(x_kept[1].sem, k)
                    square(0, k - 1)
            for h in range(2):
                act.wait_ge(x_kept[h].sem, KD)
            square(0, KD - 1)
            norm(0)
            act.wait_ge(vec_ready.sem, 1)
            act.activation(lows[:, 1, :], lows[:, 0, :], ACT.Exp).then_inc(l_lam.sem, 1)
            lam = cols[:, C_ODD + 7 * BLOCKS:C_ODD + 8 * BLOCKS]
            t0, t1 = pairs(0), pairs(1)
            act.wait_ge(vec_kept.sem, 1)
            act.activation(t0, lam, ACT.Abs).then_inc(l_lam.sem, 1)
            act.wait_ge(l_lam.sem, 2)
            act.activation(t1, t0, ACT.Exp, scale=-1.0).then_inc(l_lam.sem, 1)
            act.wait_ge(l_lam.sem, 3)
            act.activation(t0, t1, ACT.Ln, bias=1.0).then_inc(l_lam.sem, 1)
            act.activation(unit_cols[:, 0, :], lam, ACT.Relu, scale=-1.0).then_inc(l_lam.sem, 1)
            act.wait_ge(small_in.sem, 32)
            act.activation(tiny[0:HEADS, 3:4], tiny[0:HEADS, 1:2], ACT.Exp).then_inc(l_lam.sem, 1)

            act.wait_ge(dense_ready.sem, 1)
            dt = tiny[0:HEADS, 2:3]
            for h in range(2):
                act.activation(rows[32:32 + HEADS, h * HALF:(h + 1) * HALF], dense[h][32:32 + HEADS, :], ACT.Sigmoid)\
                    .then_inc(row_step.sem, 1)
            for h in range(2):
                act.activation(w1[0:HEADS, h * HALF:(h + 1) * HALF], dense[h][0:HEADS, :], ACT.Abs, bias=dt)\
                    .then_inc(row_step.sem, 1)
                act.activation(w2[0:HEADS, h * HALF:(h + 1) * HALF], dense[h][0:HEADS, :], ACT.Relu, bias=dt)\
                    .then_inc(row_step.sem if h == 0 else taken[0].sem, 1)
            act.wait_ge(row_step.sem, 5)
            act.activation(w1[0:HEADS, :], w1[0:HEADS, :], ACT.Exp, scale=-1.0).then_inc(row_step.sem, 1)
            act.wait_ge(row_step.sem, 6)
            act.activation(w1[0:HEADS, :], w1[0:HEADS, :], ACT.Ln, bias=1.0).then_inc(row_step.sem, 1)
            for n in range(EVEN_N):
                evac(("P", 0, n), 1 + n, PRE_EVEN)
            for i in range(2):
                act.wait_ge(row_turned.sem, i + 1)
                act.activation(gcols[:, i, :, :].rearrange("p c h -> p (c h)"), work[i][:, 0:NC * HEADS], ACT.Copy)\
                    .then_inc(row_cols.sem, 1)

            def head_out(u, turn, o, sq):
                for h in range(2):
                    after(act, mixed[u], turn, h + 1)
                    bank = work[(0, 2)[u] + h]
                    act.activation(half(o, h), bank[:, :], ACT.Copy).then_inc(o_kept[u].sem, 1)
                    act.activation(half(sq, h), bank[:, :], ACT.Square).then_inc(o_kept[u].sem, 1)
                for h in range(2):
                    after(act, o_summed[u], turn, h + 1)
                    act.activation(half(sq, h), work[2 + h][:, :], ACT.Sqrt, bias=eps, scale=1.0 / P)\
                        .then_inc(o_rooted[u].sem, 1)

            def round_y(u, turn, o, st, high):
                after(act, st, turn, st.per_turn)
                act.activation(yh[:, u, :], o, ACT.Copy).then_inc(high.sem, 1)

            def hgrn(turn, fill):
                after(act, z_ready[0], turn, 4)
                act.activation(k_a, f_a, ACT.Sigmoid, scale=-1.0).then_inc(a_gates.sem, 1)
                after(act, a_gates, turn, 1)
                act.activation(f_a, f_a, ACT.Sigmoid).then_inc(a_gates.sem, 1)
                act.activation(gate_a, gate_a, ACT.Silu).then_inc(a_gates.sem, 1)
                fill()
                fill()
                for l in range(LEVELS):
                    if l == 0:
                        for h in range(2):
                            after(act, a_turned, turn, h + 1)
                            act.activation(half(v_a, h), work[h][:, :], ACT.Copy).then_inc(a_values.sem, 1)
                    fill()
                for h in range(2):
                    after(act, a_turned, turn, 2 + h + 1)
                    act.activation(half(k_a, h), work[h][:, :], ACT.Copy).then_inc(a_keys.sem, 1)
                fill()
                fill()
                fill()
                after(act, a_state, turn, HC)
                head_out(0, turn, q_a, f_a)
                fill()
                round_y(0, turn, q_a, o_scaled[0], y_high[0])
                fill()

            def gdn(turn, fill):
                for m in range(2):
                    after(act, b_conv, turn, TAPS * (m + 1))
                    act.activation(cv[:, m, :], cv[:, m, :], ACT.Silu).then_inc(b_silu.sem, 1)
                    after(act, b_silu, turn, m + 1)
                    act.activation(raw[m], cv[:, m, :], ACT.Square).then_inc(b_squared.sem, 1)
                for i in range(2):
                    for h in range(2):
                        after(act, b_summed, turn, 2 * i + h + 1)
                        act.activation(half(raw[i], h), work[2 * i + h][:, :], ACT.Sqrt, bias=eps)\
                            .then_inc(b_rooted.sem, 1)
                fill()
                fill()
                after(act, b_conv, turn, 3 * TAPS)
                act.activation(v_b, v_b, ACT.Silu).then_inc(b_silu.sem, 1)
                act.activation(zg[:, :], zg[:, :], ACT.Silu).then_inc(b_silu.sem, 1)
                after(act, b_normed, turn, 4)
                after(act, b_spread, turn, 1)
                for h in range(2):
                    act.activation(half(raw[0], h), work[h][:, :], ACT.Exp).then_inc(b_decay.sem, 1)
                act.activation(w1[:, :].rearrange("p (c t) -> p c t", t=P), wide(ident, NC), ACT.Copy)\
                    .then_inc(b_ident.sem, 1)
                act.activation(w3[:, :].rearrange("p (c t) -> p c t", t=P), wide(ident, NC), ACT.Copy)\
                    .then_inc(b_ident.sem, 1)
                fill()
                after(act, b_diff, turn, NC + 2)
                act.activation(raw[2], raw[2], ACT.Exp).then_inc(b_exp.sem, 1)
                act.activation(head_cols[:, 2, :], head_cols[:, 0, :], ACT.Exp).then_inc(b_exp.sem, 1)
                act.activation(head_cols[:, 3, :], head_cols[:, 3, :], ACT.Exp).then_inc(b_exp.sem, 1)
                fill()
                fill()
                for l in range(LEVELS):
                    if l:
                        for h in range(2):
                            after(act, b_u, turn, 2 * l + h + 1)
                            act.activation(half(w2, h), work[2 * h][:, :], ACT.Copy).then_inc(b_ukept.sem, 1)
                        fill()
                    fill()
                for c in range(NC):
                    if c:
                        fill()
                    after(act, c_v, turn, c + 1)
                    act.activation(chunk(w2, c), work[1][:, 0:P], ACT.Copy).then_inc(c_vn.sem, 1)
                    fill()
                head_out(1, turn, q_b, raw[0])
                fill()
                round_y(1, turn, q_b, o_scaled[1], y_high[1])
                fill()
                fill()

            def even_turn(turn, first, last):
                place = EVEN(turn)
                w = turn_steps(EVEN_N, first, last)
                steps = sum(w, [])
                hgrn(turn, Filler(w[0], 0, place, steps, FILLS_A, None, evac))
                gdn(turn, Filler(w[1], len(w[0]), place, steps, FILLS_B, None, evac))

            def wide(t, n):
                a = t[:, :]
                return bass.AP(a.tensor, a.offset, [list(a.ap[0]), [0, n], [1, P]])

            turns(act, HEADS, even_turn)

            def ple(i, place, n_norm):
                for k in range(KD):
                    act.wait_ge(taken[place.pair(k - KD)].sem, place.taken(k - KD))
                    square(n_norm, k)
                    if k == 1:
                        for j in range(2 * KP):
                            after(act, p_turned, i, j + 1)
                            act.activation(half(yh[:, j // 2, :], j % 2), work[j][:, :], ACT.Copy).then_inc(p_high.sem, 1)

                def keep(n):
                    pair = place.pair(n)
                    act.wait_ge(dense_ready.sem, place.ready(n))
                    act.activation(half(tiles8[n], 0), dense[2 * pair][:, :], ACT.Copy).then_inc(p_proj.sem, 1)
                    act.activation(half(tiles8[n], 1), dense[2 * pair + 1][:, :], ACT.Copy).then_inc(taken[pair].sem, 1)

                norm_root(n_norm)
                for k in range(KD):
                    keep(k)
                    after(act, norm_scaled, n_norm, k + 1)
                    act.activation(xh[:, k, :], (w1, w2)[k % 2][:, :], ACT.Copy).then_inc(norm_high.sem, 1)
                for n in range(KD + 1):
                    if n < KD:
                        local = KD + n
                        pair = place.pair(local)
                        act.wait_ge(dense_ready.sem, place.ready(local))
                        if n >= 2:
                            after(act, p_added, i, n - 1)
                        g = (w1, w2)[n % 2]
                        act.activation(half(g, 0), dense[2 * pair][:, :], ACT.Sigmoid).then_inc(p_gate.sem, 1)
                        act.activation(half(g, 1), dense[2 * pair + 1][:, :], ACT.Sigmoid).then_inc(taken[pair].sem, 1)
                    if n:
                        after(act, p_added, i, n)
                        square(n_norm + 1, n - 1)

            ple(0, PLE0, 1)
            norm(2)
            for n in range(ODD_N):
                evac(("P", 0, n), n, PRE_ODD)

            def lru(u, turn, fill):
                uc = unit_cols[:, u, :]
                after(act, lz_ready[u], turn, 2)
                fill()
                for i in range(2):
                    after(act, l_gates[u], turn, i + 1)
                    for h in range(2):
                        act.activation(half(cv[:, 1 + i, :], h), work[2 * i + h][:, :], ACT.Sigmoid,
                                       bias=uc[:, 5 + i:6 + i]).then_inc(l_sig[u].sem, 1)
                after(act, l_sig[u], turn, 2)
                act.activation(za[:, u, :], za[:, u, :], ACT.Silu).then_inc(l_silu[u].sem, 1)
                fill()
                after(act, l_sig[u], turn, 2)
                act.activation(za[:, 2, :], cv[:, 1, :], ACT.Tanh, scale=uc[:, 8:9]).then_inc(l_exp[u].sem, 1)
                after(act, l_exp[u], turn, 1)
                act.activation(cv[:, 1, :], cv[:, 1, :], ACT.Exp, scale=uc[:, 7:8]).then_inc(l_exp[u].sem, 1)
                fill()
                after(act, l_vec[u], turn, 2)
                act.activation(za[:, 2, :], za[:, 2, :], ACT.Sqrt).then_inc(l_root[u].sem, 1)
                fill()
                round_y(u, turn, za[:, 3, :], l_vec[u], l_high[u])
                fill()
                fill()

            def odd_turn(turn, first, last):
                place = ODD(turn)
                w = turn_steps(ODD_N, first, last)
                steps = sum(w, [])
                lru(0, turn, Filler(w[0], 0, place, steps, FILLS_L, None, evac))
                lru(1, turn, Filler(w[1], len(w[0]), place, steps, FILLS_L, None, evac))

            turns(act, TURNS, odd_turn)
            ple(1, PLE1, 3)
            norm(4, split=False)
            after(act, f_scaled, 0, KD)
            for i in range(2 * NC):
                c = i // 2
                act.wait_ge(f_turned.sem, i + 1)
                if c >= 2:
                    act.wait_ge(stored[c % 2].sem, 16 * (c // 2))
                act.activation(half((w1, w2)[c % 2], i % 2), work[i % 4][:, :], ACT.Copy).then_inc(f_kept.sem, 1)

        @block.vector
        def _(dve):
            def evac(what, local, place):
                kind, u, n = what
                if kind not in "OV":
                    return
                pair = place.pair(local)
                dve.wait_ge(dense_ready.sem, place.ready(local))
                dve.tensor_tensor(half(x[:, n, :], 0), dense[2 * pair][:, :], half(x[:, n, :], 0), ALU.add)
                dve.tensor_tensor(half(x[:, n, :], 1), dense[2 * pair + 1][:, :], half(x[:, n, :], 1), ALU.add)\
                    .then_inc(taken[pair].sem, 1)

            def norm_start(n):
                for h in range(2):
                    after(dve, norm_rooted, n, h + 1)
                    dve.reciprocal(half(w3, h), half(w3, h)).then_inc(norm_inverse.sem, 1)
                after(dve, norm_inverse, n, 2)

            def norm(n):
                norm_start(n)

                def low(k):
                    after(dve, norm_high, n, k + 1)
                    dve.tensor_tensor(xl[:, k, :], (w1, w2)[k % 2][:, :], xh[:, k, :].bitcast(F32), ALU.subtract)\
                        .then_inc(norm_low.sem, 1)

                for k in range(KD):
                    if k >= 2:
                        after(dve, norm_low, n, k - 1)
                    dve.scalar_tensor_tensor(out=(w1, w2)[k % 2][:, :], in0=x[:, k, :],
                                             scalar=cols[:, NORMS[n] + k:NORMS[n] + k + 1], in1=w3[:, :],
                                             op0=ALU.mult, op1=ALU.mult).then_inc(norm_scaled.sem, 1)
                    if k:
                        low(k - 1)
                low(KD - 1)

            build = zb[:, :, :].rearrange("p a b -> p (a b)")[:, 0:(2 * LEVELS + 1) * P].rearrange("p (a b) -> p a b", b=P)
            dve.wait_ge(made.sem, MADE)
            dve.tensor_copy(masks[:, :, :], build).then_inc(masks_ready.sem, 1)
            dve.wait_ge(masks_ready.sem, 1)
            dve.memset(zb[:, :, 0:PAD], 0.0).then_inc(masks_ready.sem, 1)
            for k in range(KD):
                dve.wait_ge(x_turned.sem, 2 * k + 2)
                dve.tensor_copy(half(x[:, k, :], 1), dense[2 * (k % 2) + 1][:, :]).then_inc(x_kept[1].sem, 1)
            for h in range(2):
                dve.wait_ge(x_kept[h].sem, KD)
            norm(0)
            dve.wait_ge(vec_kept.sem, 1)
            lb = cols[:, C_LB:C_LB + HEADS]
            dve.tensor_tensor(lows[:, 0, :], lb, lb, ALU.subtract).then_inc(vec_ready.sem, 1)
            dve.wait_ge(l_lam.sem, 1)
            dve.reciprocal(lows[:, 2, :], lows[:, 1, :]).then_inc(vec_ready.sem, 1)
            dve.wait_ge(vec_ready.sem, 2)
            dve.tensor_tensor(lows[:, 0, :], lows[:, 1, :], lows[:, 2, :], ALU.mult).then_inc(vec_ready.sem, 1)
            dve.wait_ge(vec_ready.sem, 3)
            dve.tensor_tensor(lows[:, 2, :], lows[:, 0, :], lows[:, 0, :], ALU.subtract).then_inc(vec_ready.sem, 1)
            dve.wait_ge(vec_ready.sem, 4)
            dve.tensor_scalar(lows[:, 3, :], lows[:, 2, :], -1.0, 1.0, ALU.mult, ALU.add).then_inc(vec_ready.sem, 1)
            dve.wait_ge(l_lam.sem, 5)
            t0 = pairs(0)
            lam = cols[:, C_ODD + 7 * BLOCKS:C_ODD + 8 * BLOCKS]
            dve.tensor_tensor(t0, t0, unit_cols[:, 0, :], ALU.add).then_inc(vec_ready.sem, 1)
            dve.wait_ge(vec_ready.sem, 6)
            dve.tensor_scalar(lam, t0, -8.0, None, ALU.mult).then_inc(vec_ready.sem, 1)
            dve.wait_ge(l_lam.sem, 6)
            dve.tensor_scalar(tiny[0:HEADS, 3:4], tiny[0:HEADS, 3:4], -1.0, None, ALU.mult).then_inc(vec_ready.sem, 1)
            dve.wait_ge(vec_ready.sem, 8)

            dve.memset(w3[0:HEADS, :], 1.0).then_inc(row_vec.sem, 1)
            dve.wait_ge(row_vec.sem, 1)
            dve.memset(w3[0:HEADS, :].rearrange("p (c t) -> p c t", t=CHUNK)[:, :, 0:1], 0.0).then_inc(row_vec.sem, 1)
            dve.wait_ge(row_step.sem, 7)
            dve.tensor_tensor(w1[0:HEADS, :], w1[0:HEADS, :], w2[0:HEADS, :], ALU.add).then_inc(row_vec.sem, 1)
            dve.wait_ge(row_vec.sem, 3)
            dve.tensor_scalar(w1[0:HEADS, :], w1[0:HEADS, :], tiny[0:HEADS, 3:4], None, ALU.mult).then_inc(row_vec.sem, 1)
            dve.wait_ge(row_vec.sem, 4)
            dve.tensor_tensor_scan(out=rows[0:HEADS, :], data0=w3[0:HEADS, :], data1=w1[0:HEADS, :], initial=0.0,
                                   op0=ALU.mult, op1=ALU.add).then_inc(row_vec.sem, 1)

            def select(out_, mask, data):
                dve.sem_inc(select_begun.sem, 1)
                return dve.copy_predicated(out_, mask, data)

            def over_chunks(n_mask, n, b=None):
                m = masks[:, n_mask, :]
                if b is not None:
                    m = m.rearrange("p (n two b) -> p n two b", two=2, b=b)[:, :, 1, :]
                dims = [list(d) for d in m.ap]
                return bass.AP(m.tensor, m.offset, [dims[0], [0, n]] + dims[1:])

            def by_blocks(t, b):
                return t.rearrange("p (n two b) -> p n two b", two=2, b=b)

            def repeat(v, b):
                dims = [list(d) for d in v.ap]
                return bass.AP(v.tensor, v.offset, dims[:-1] + [[0, b]])

            def head_out(u, turn, o, sq, gate, g_col, fill):
                after(dve, o_rooted[u], turn, 2)
                dve.reciprocal(sq, sq).then_inc(o_scaled[u].sem, 1)
                after(dve, o_scaled[u], turn, 1)
                dve.scalar_tensor_tensor(out=o, in0=o, scalar=g_col, in1=sq, op0=ALU.mult, op1=ALU.mult)\
                    .then_inc(o_scaled[u].sem, 1)
                after(dve, o_scaled[u], turn, 2)
                dve.tensor_tensor(o, o, gate, ALU.mult).then_inc(o_scaled[u].sem, 1)
                fill()
                after(dve, y_high[u], turn, 1)
                dve.tensor_tensor(yl[:, u, :], o, yh[:, u, :].bitcast(F32), ALU.subtract).then_inc(y_ready[u].sem, 1)
                fill()

            def hgrn(turn, fill):
                uc = unit_cols[:, 0, :]
                after(dve, a_gates, turn, 3)
                dve.tensor_copy(uc[:, 0:2], lows[:, 2:4, bass.ds(turn, 1)].rearrange("p a b -> p (a b)"))\
                    .then_inc(a_bounded.sem, 1)
                dve.tensor_copy(uc[:, 2:3], cols[:, bass.ds(turn + C_HEAD, 1)]).then_inc(a_cols.sem, 1)
                after(dve, a_bounded, turn, 1)
                dve.tensor_scalar(k_a, k_a, uc[:, 1:2], None, ALU.mult).then_inc(a_bounded.sem, 1)
                dve.tensor_scalar(f_a, f_a, uc[:, 1:2], uc[:, 0:1], ALU.mult, ALU.add).then_inc(a_bounded.sem, 1)
                dve.memset(w1[:, :], 0.0)
                after(dve, a_bounded, turn, 3)
                fill()
                after(dve, a_scores, turn, 1)
                dve.tensor_tensor(q_a, q_a, f_a, ALU.mult).then_inc(a_scaled.sem, 1)
                after(dve, a_scaled, turn, 1)
                for h in range(2):
                    select(half(w1, h).rearrange("p (c t) -> p c t", t=P), over_chunks(2 * LEVELS, HC),
                           work[h][:, :].rearrange("p (c t) -> p c t", t=P)).then_inc(a_kept.sem, 1)
                fill()
                for l in range(LEVELS):
                    b = 1 << l
                    after(dve, a_scores, turn, 2 + l)
                    q, k, f = by_blocks(q_a, b), by_blocks(k_a, b), by_blocks(f_a, b)
                    done = 1 + 3 * l
                    dve.tensor_tensor(q[:, :, 1, :], q[:, :, 1, :], repeat(f[:, :, 0, 0:1], b), ALU.mult)\
                        .then_inc(a_scaled.sem, 1)
                    dve.tensor_tensor(k[:, :, 0, :], k[:, :, 0, :], repeat(f[:, :, 1, 0:1], b), ALU.mult)\
                        .then_inc(a_scaled.sem, 1)
                    after(dve, a_scaled, turn, done + 2)
                    dve.tensor_tensor(f[:, :, 0, 0:1], f[:, :, 0, 0:1], f[:, :, 1, 0:1], ALU.mult)\
                        .then_inc(a_scaled.sem, 1)
                    kept = w1[:, :].rearrange("p (c n two b) -> p c n two b", c=NC, two=2, b=b)[:, :, :, 1, :]
                    after(dve, a_kept, turn, 2 + l)
                    select(kept, over_chunks(l, NC, b),
                           work[2 + l % 2][:, :].rearrange("p (c n b) -> p c n b", c=NC, b=b)).then_inc(a_kept.sem, 1)
                    after(dve, a_scaled, turn, done + 3)
                    fill()
                fill()
                for c in range(NC - 1):
                    if c % HC == 0:
                        after(dve, a_kv, turn, c // HC + 1)
                    kv, now = in_half(work[2 + c // HC], c), chunk(w2, c)
                    if c == 0:
                        dve.tensor_copy(now, kv).then_inc(a_state.sem, 1)
                    else:
                        after(dve, a_state, turn, c)
                        dve.scalar_tensor_tensor(out=now, in0=chunk(w2, c - 1), scalar=chunk(f_a, c)[:, 0:1],
                                                 in1=kv, op0=ALU.mult, op1=ALU.add).then_inc(a_state.sem, 1)
                fill()
                fill()
                head_out(0, turn, q_a, f_a, gate_a, unit_cols[:, 0, 2:3], fill)

            def gdn(turn, fill):
                uc = unit_cols[:, 1, :]
                taps = cols[:, C_CONV:C_CONV + TAPS * 3 * HEADS].rearrange("p (f j) -> p f j", j=HEADS)
                dve.tensor_copy(uc[:, 0:3 * TAPS], taps[:, :, bass.ds(turn, 1)].rearrange("p f j -> p (f j)"))\
                    .then_inc(b_cols.sem, 1)
                dve.tensor_copy(uc[:, 12:13], cols[:, bass.ds(turn + C_HEAD + HEADS, 1)]).then_inc(b_cols.sem, 1)
                dve.tensor_copy(head_cols[:, 0:2, :],
                                gcols[:, :, :, bass.ds(turn, 1)].rearrange("p a c h -> p a (c h)")).then_inc(b_cols.sem, 1)
                after(dve, b_cols, turn, 3)
                for m in range(3):
                    after(dve, z_ready[1], turn, m + 2)
                    for i in range(TAPS):
                        tap = TAPS - 1 - i
                        src = zb[:, m, tap:tap + T]
                        w = uc[:, 3 * tap + m:3 * tap + m + 1]
                        if i == 0:
                            dve.tensor_scalar(cv[:, m, :], src, w, None, ALU.mult).then_inc(b_conv.sem, 1)
                        else:
                            after(dve, b_conv, turn, TAPS * m + i)
                            dve.scalar_tensor_tensor(out=cv[:, m, :], in0=src, scalar=w, in1=cv[:, m, :],
                                                     op0=ALU.mult, op1=ALU.add).then_inc(b_conv.sem, 1)
                    if m == 1:
                        for at in (0, 32):
                            dve.tensor_scalar(w2[at:at + HEADS, :], rows[at:at + HEADS, :],
                                              ident[at:at + HEADS, bass.ds(turn + at, 1)], None, ALU.mult)\
                                .then_inc(b_rows.sem, 1)
                fill()
                fill()
                for i in range(2):
                    after(dve, b_rooted, turn, 2 * i + 2)
                    dve.reciprocal(raw[i], raw[i]).then_inc(b_normed.sem, 1)
                    after(dve, b_normed, turn, 2 * i + 1)
                    dve.scalar_tensor_tensor(out=cv[:, i, :], in0=cv[:, i, :], scalar=(P ** -0.5, 1.0)[i],
                                             in1=raw[i], op0=ALU.mult, op1=ALU.mult).then_inc(b_normed.sem, 1)
                after(dve, b_normed, turn, 4)
                after(dve, b_spread, turn, 2)
                for h in range(2):
                    dve.scalar_tensor_tensor(out=half(raw[1], h), in0=half(k_b, h), scalar=-1.0,
                                             in1=work[2 + h][:, :], op0=ALU.mult, op1=ALU.mult)\
                        .then_inc(b_keyed.sem, 1)
                after(dve, b_decay, turn, 2)
                for c in range(NC):
                    dve.tensor_scalar(chunk(raw[2], c), in_half(work[c // HC], c), head_cols[:, 0, c:c + 1], 0.0,
                                      ALU.subtract, ALU.min).then_inc(b_diff.sem, 1)
                for h in range(2):
                    ends = work[h][:, :].rearrange("p (c t) -> p c t", t=P)[:, :, P - 1]
                    dve.tensor_tensor(head_cols[:, 3, h * HC:(h + 1) * HC], ends,
                                      head_cols[:, 0, h * HC:(h + 1) * HC], ALU.subtract).then_inc(b_diff.sem, 1)
                fill()
                after(dve, b_exp, turn, 3)
                up = upper[:, :]
                up = bass.AP(up.tensor, up.offset, [list(up.ap[0]), [0, NC], [1, P]])
                decays = raw[2].rearrange("p (c t) -> p c t", t=P)
                dve.tensor_tensor(decays, decays, up, ALU.mult).then_inc(b_masked.sem, 1)
                dve.scalar_tensor_tensor(out=head_cols[:, 2, :], in0=head_cols[:, 2, :], scalar=-1.0,
                                         in1=head_cols[:, 1, :], op0=ALU.mult, op1=ALU.mult).then_inc(b_cols.sem, 1)
                dve.tensor_copy(head_cols[:, 5, :], raw[0].rearrange("p (c t) -> p c t", t=P)[:, :, P - 1])\
                    .then_inc(b_cols.sem, 1)
                after(dve, b_cols, turn, 5)
                after(dve, b_masked, turn, 1)
                for i in range(2):
                    for h in range(2):
                        after(dve, b_prod, turn, 2 * i + h + 1)
                        dve.tensor_tensor(half(raw[1 + i], h), work[2 * i + h][:, :], half(raw[2], h), ALU.mult)\
                            .then_inc(b_scores.sem, 1)
                fill()
                dve.tensor_tensor(q_b, q_b, raw[0], ALU.mult).then_inc(b_qdec.sem, 1)
                for i, (dst, col) in enumerate(((v_b, 1), (raw[0], 3))):
                    for h in range(2):
                        after(dve, b_turned, turn, 2 * i + h + 1)
                        if i:
                            after(dve, b_qdec, turn, 1)
                        v = head_cols[:, col, h * HC:(h + 1) * HC]
                        v = bass.AP(v.tensor, v.offset, [list(v.ap[0]), list(v.ap[1]), [0, P]])
                        dve.tensor_tensor(half(dst, h).rearrange("p (c t) -> p c t", t=P),
                                          work[2 * i + h][:, :].rearrange("p (c t) -> p c t", t=P), v, ALU.mult)\
                            .then_inc(b_vk.sem, 1)
                fill()

                def grow(t, n_mask, h, data):
                    return select(half(t, h).rearrange("p (c t) -> p c t", t=P), over_chunks(n_mask, HC),
                                  data.rearrange("p (c t) -> p c t", t=P)).then_inc(b_inv.sem, 1)

                after(dve, b_ident, turn, 2)
                for l in range(LEVELS):
                    if l == 0:
                        for h in range(2):
                            after(dve, b_u, turn, h + 1)
                            grow(w1, LEVELS, h, work[2 * h][:, :])
                            grow(w3, 0, h, half(raw[1], h))
                    else:
                        fill()
                        n = 4 * (l - 1)
                        for h in range(2):
                            after(dve, b_inv, turn, 4 * l)
                            if l < LEVELS - 1:
                                after(dve, b_y, turn, n + 2 * h + 1)
                                grow(w1, LEVELS + l, h, work[2 * h + 1][:, :])
                                after(dve, b_y, turn, n + 2 * h + 2)
                            else:
                                after(dve, b_y, turn, n + h + 1)
                            grow(w3, l, h, work[2 * h][:, :])
                    fill()
                for c in range(NC):
                    if c:
                        after(dve, c_ks, turn, c)
                        dve.scalar_tensor_tensor(out=chunk(v_b, c), in0=work[0][:, 0:P], scalar=head_cols[:, 2, c:c + 1],
                                                 in1=chunk(v_b, c), op0=ALU.mult, op1=ALU.add).then_inc(c_r.sem, 1)
                        fill()
                    if c < NC - 1:
                        after(dve, c_kv, turn, c + 1)
                        if c == 0:
                            dve.tensor_copy(state[:, 1, :], work[0][:, 0:P]).then_inc(c_state.sem, 1)
                        else:
                            dve.scalar_tensor_tensor(out=state[:, (c + 1) % 2, :], in0=state[:, c % 2, :],
                                                     scalar=head_cols[:, 5, c:c + 1], in1=work[0][:, 0:P],
                                                     op0=ALU.mult, op1=ALU.add).then_inc(c_state.sem, 1)
                    fill()
                head_out(1, turn, q_b, raw[0], zg[:, :], uc[:, 12:13], fill)
                fill()

            def even_turn(turn, first, last):
                place = EVEN(turn)
                w = turn_steps(EVEN_N, first, last)
                steps = sum(w, [])
                hgrn(turn, Filler(w[0], 0, place, steps, FILLS_A, None, evac))
                gdn(turn, Filler(w[1], len(w[0]), place, steps, FILLS_B, None, evac))

            turns(dve, HEADS, even_turn)
            Filler(outp(1), 0, EVEN_TAIL, outp(1), [1], None, evac)()

            def ple(i, place, n_norm):
                for k in range(KP):
                    for h in range(2):
                        after(dve, p_high, i, 2 * k + h + 1)
                        dve.tensor_tensor(half(yl[:, k, :], h), work[2 * k + h][:, :],
                                          half(yh[:, k, :].bitcast(F32), h), ALU.subtract).then_inc(p_low.sem, 1)
                norm(n_norm)
                for n in range(KD):
                    g, local = (w1, w2)[n % 2][:, :], KD + n
                    dve.wait_ge(taken[place.pair(local)].sem, place.taken(local))
                    dve.tensor_tensor(g, tiles8[n], g, ALU.mult).then_inc(p_prod.sem, 1)
                    after(dve, p_prod, i, n + 1)
                    dve.tensor_tensor(x[:, n, :], x[:, n, :], g, ALU.add).then_inc(p_added.sem, 1)

            ple(0, PLE0, 1)
            after(dve, p_added, 0, KD)
            norm(2)

            def lru(u, turn, fill):
                uc = unit_cols[:, u, :]
                xc, a, gx, th, h_t = cv[:, 0, :], cv[:, 1, :], cv[:, 2, :], za[:, 2, :], za[:, 3, :]
                after(dve, lz_ready[u], turn, 2)
                v = cols[:, C_ODD:C_ODD + 8 * BLOCKS].rearrange("p (f i u) -> p f i u", u=2, i=TURNS)
                dve.tensor_copy(uc[:, 0:8], v[:, :, bass.ds(turn, 1), u].rearrange("p f i -> p (f i)"))\
                    .then_inc(l_cols[u].sem, 1)
                after(dve, l_cols[u], turn, 1)
                for i in range(TAPS):
                    tap = TAPS - 1 - i
                    src = zb[:, u, tap:tap + T]
                    if i == 0:
                        dve.tensor_scalar(uc[:, 8:9], uc[:, 7:8], -1.0, None, ALU.mult)
                        dve.tensor_scalar(xc, src, uc[:, tap:tap + 1], uc[:, 4:5], ALU.mult, ALU.add)\
                            .then_inc(l_conv[u].sem, 1)
                    else:
                        after(dve, l_conv[u], turn, i)
                        dve.scalar_tensor_tensor(out=xc, in0=src, scalar=uc[:, tap:tap + 1], in1=xc,
                                                 op0=ALU.mult, op1=ALU.add).then_inc(l_conv[u].sem, 1)
                fill()
                fill()
                after(dve, l_exp[u], turn, 2)
                dve.tensor_tensor(h_t, a, a, ALU.mult).then_inc(l_vec[u].sem, 1)
                after(dve, l_vec[u], turn, 1)
                dve.scalar_tensor_tensor(out=th, in0=h_t, scalar=1.0, in1=th, op0=ALU.add, op1=ALU.mult)\
                    .then_inc(l_vec[u].sem, 1)
                fill()
                after(dve, l_sig[u], turn, 4)
                dve.tensor_tensor(gx, gx, xc, ALU.mult).then_inc(l_vec[u].sem, 1)
                after(dve, l_root[u], turn, 1)
                dve.memset(th[:, 0:1], 1.0).then_inc(l_vec[u].sem, 1)
                after(dve, l_vec[u], turn, 4)
                dve.tensor_tensor(gx, gx, th, ALU.mult).then_inc(l_vec[u].sem, 1)
                after(dve, l_vec[u], turn, 5)
                dve.tensor_tensor_scan(out=h_t, data0=a, data1=gx, initial=0.0, op0=ALU.mult, op1=ALU.add)\
                    .then_inc(l_vec[u].sem, 1)
                fill()
                after(dve, l_vec[u], turn, 6)
                after(dve, l_silu[u], turn, 1)
                dve.tensor_tensor(h_t, h_t, za[:, u, :], ALU.mult).then_inc(l_vec[u].sem, 1)
                fill()
                after(dve, l_high[u], turn, 1)
                dve.tensor_tensor(yl[:, u, :], h_t, yh[:, u, :].bitcast(F32), ALU.subtract).then_inc(l_y[u].sem, 1)
                fill()

            def odd_turn(turn, first, last):
                place = ODD(turn)
                w = turn_steps(ODD_N, first, last)
                steps = sum(w, [])
                lru(0, turn, Filler(w[0], 0, place, steps, FILLS_L, None, evac))
                lru(1, turn, Filler(w[1], len(w[0]), place, steps, FILLS_L, None, evac))

            turns(dve, TURNS, odd_turn)
            Filler(outp(1), 0, ODD_TAIL, outp(1), [1], None, evac)()
            ple(1, PLE1, 3)
            after(dve, p_added, 1, KD)
            norm_start(4)
            for k in range(KD):
                dve.scalar_tensor_tensor(out=tiles8[k], in0=x[:, k, :], scalar=cols[:, NORMS[4] + k:NORMS[4] + k + 1],
                                         in1=w3[:, :], op0=ALU.mult, op1=ALU.mult).then_inc(f_scaled.sem, 1)


_INS = ["x", "p", "even_norm", "even_w_in", "hgrn_lb_logits", "gdn_conv_w", "gdn_a_log", "gdn_dt_bias",
        "even_head_norm", "even_w_out", "odd_norm", "odd_w_in", "lru_conv_w", "lru_conv_b", "lru_w_a",
        "lru_b_a", "lru_w_x", "lru_b_x", "lru_lambda", "odd_w_out", "ple_norm", "ple_gate_w", "ple_proj_w",
        "final_norm"]


def kernel(**inputs):
    import numpy as _np
    import concourse.bacc as _bacc
    from concourse import mybir as _mybir
    from concourse.bass_utils import run_bass_kernel_spmd as _run

    nc = _bacc.Bacc("TRN2", target_bir_lowering=False, num_devices=1)
    arrays, args = {}, []
    for name in _INS:
        a = _np.ascontiguousarray(inputs[name])
        arrays[f"in_{name}_dram"] = a
        args.append(nc.dram_tensor(f"in_{name}_dram", a.shape, _mybir.dt.from_np(a.dtype), kind="ExternalInput").ap())
    shape = inputs["x"].shape
    args.append(nc.dram_tensor("out_0_dram", shape, _mybir.dt.from_np(_np.dtype("float32")), kind="ExternalOutput").ap())
    build_trunk(nc, *args)
    r = _run(nc, [arrays], core_ids=[0])
    return r.results[0]["out_0_dram"]
```

```python
from contextlib import ExitStack

import concourse.bass as bass
from concourse import mybir

F32 = mybir.dt.float32
F32R = mybir.dt.float32r
U8 = mybir.dt.uint8
ACT = mybir.ActivationFunctionType
ALU = mybir.AluOpType

P = 128
HALF = 512
CHUNK = 128
LEVELS = 7
EPS = 1e-6
TAPS = 4
PAD = TAPS - 1


class Step:

    def __init__(self, sem, per_turn):
        self.sem, self.per_turn = sem, per_turn

    def at(self, turn, n):
        return turn * self.per_turn + n


def after(eng, step, turn, n):
    eng.wait_ge(step.sem, step.at(turn, n))


def spread(pieces, amounts):
    sums = [min(sum(amounts[:n + 1]), pieces) for n in range(len(amounts))]
    return sums[:-1] + [pieces]


def build_trunk(nc, x_in, p_in, even_norm, even_w_in, lb_logits, gdn_conv_w, gdn_a_log, gdn_dt_bias,
                even_head_norm, even_w_out, odd_norm, odd_w_in, lru_conv_w, lru_conv_b, lru_w_a,
                lru_b_a, lru_w_x, lru_b_x, lru_lambda, odd_w_out, ple_norm, ple_gate_w, ple_proj_w,
                final_norm, out):
    _, T, D = x_in.shape
    KD = D // P
    NC = T // CHUNK
    HC = NC // 2
    HEADS = D // P
    BLOCKS = lru_w_a.shape[1]
    KP = p_in.shape[3] // P
    AW = HEADS * P
    GATE0 = 6 * AW + 2 * HEADS
    assert T == 2 * HALF and KD == 8 and NC == 8 and HEADS == 8 and BLOCKS == 2 * HEADS and KP == 2

    with ExitStack() as ctx:
        def sb(name, shape, dt=F32):
            return ctx.enter_context(nc.sbuf_tensor(name, shape, dt))

        def sem(name):
            return ctx.enter_context(nc.semaphore(name))

        def step(name, per_turn):
            return Step(sem(name), per_turn)

        x = sb("x", [P, KD, T])
        xh = sb("xh", [P, KD, T], F32R)
        xl = sb("xl", [P, KD, T], F32R)
        yh = sb("yh", [P, 2, T], F32R)
        yl = sb("yl", [P, 2, T], F32R)
        w_stage = sb("w_stage", [P, T])
        w_high = sb("w_high", [P, 2, T], F32R)
        w_low = sb("w_low", [P, 2, T], F32R)
        za = sb("za", [P, 5, T])
        zb = sb("zb", [P, 3, PAD + T + 1])
        zg = sb("zg", [P, T])
        cv = sb("cv", [P, 3, T])
        w1 = sb("w1", [P, T])
        w2 = sb("w2", [P, T])
        w3 = sb("w3", [P, T])
        rows = sb("rows", [64, T])
        cols = sb("cols", [P, 2 * P + 32])
        lows = sb("lows", [P, 4, HEADS])
        unit_cols = sb("unit_cols", [P, 2, 16])
        gcols = sb("gcols", [P, 2, NC, HEADS])
        head_cols = sb("head_cols", [P, 6, NC])
        state = sb("state", [P, 2, P])
        ident = sb("ident", [P, P])
        upper = sb("upper", [P, P])
        ones = sb("ones", [P, P])
        masks = sb("masks", [P, 2 * LEVELS + 1, P], U8)
        tiny = sb("tiny", [P, 4])

        dense = [ctx.enter_context(nc.psum_tensor(f"dense{i}", [P, HALF], F32)) for i in range(4)]
        work = [ctx.enter_context(nc.psum_tensor(f"work{i}", [P, HALF], F32)) for i in range(4)]

        def half(t, h):
            return t[:, h * HALF:(h + 1) * HALF]

        def chunk(t, c):
            return t[:, c * CHUNK:(c + 1) * CHUNK]

        def in_half(bank, c):
            return bank[:, (c % HC) * CHUNK:(c % HC + 1) * CHUNK]

        q_a, f_a, v_a, gate_a, k_a = (za[:, n, :] for n in range(5))
        q_b, k_b, v_b = (cv[:, n, :] for n in range(3))
        raw = [zb[:, n, PAD:PAD + T] for n in range(3)]
        tiles8 = [za[:, n, :] for n in range(5)] + [cv[:, n, :] for n in range(3)]

        C_CONV, C_HEAD, C_NORM, C_LB = 0, TAPS * 3 * HEADS, TAPS * 3 * HEADS + 2 * HEADS, P - HEADS
        C_ODD = P
        C_TAIL = 2 * P
        NORMS = [C_NORM, C_TAIL + 8, C_TAIL, C_TAIL + 16, C_TAIL + 24]

        def pairs(i):
            return head_cols[:, :, :].rearrange("p a c -> p (a c)")[:, i * BLOCKS:(i + 1) * BLOCKS]

        def squares(n, k):
            return raw[k % 2] if n in (2, 4) else (w1, w2)[k % 2][:, :]

        IDENT_MADE = 4
        MADE = 6 + 6 * LEVELS + 2

        made = step("constants_made", 0)
        cleared = step("padding_cleared", 0)
        small_in = step("small_inputs_loaded", 0)
        vec_in = step("vectors_loaded", 0)
        vec_turned = step("vectors_turned", 0)
        vec_kept = step("vectors_kept", 0)
        vec_ready = step("vector_work_done", 0)
        x_loaded = step("x_loaded", 0)
        x_turned = step("x_turned", 0)
        x_kept = [step(f"x_half{h}_kept", 0) for h in range(2)]
        masks_ready = step("masks_ready", 0)
        split_begun = step("split_begun", 0)
        select_begun = step("select_begun", 0)
        w_in = step("weights_loaded", 0)
        w_split_high = step("weights_split_high", 0)
        w_split = step("weights_split", 0)
        dense_ready = step("dense_ready", 0)
        taken = [step(f"dense_taken{n}", 0) for n in range(2)]
        norm_squared = step("norm_squared", KD)
        norm_summed = step("norm_summed", KD)
        norm_rooted = step("norm_rooted", 2)
        norm_inverse = step("norm_inverse", 2)
        norm_scaled = step("norm_scaled", KD)
        norm_high = step("norm_high", KD)
        norm_low = step("norm_low", KD)
        row_step = step("row_step_scalar", 0)
        row_vec = step("row_step_vector", 0)
        row_turned = step("rows_turned", 0)
        row_cols = step("row_columns_kept", 0)
        z_ready = [step("unit_a_projected", 4), step("unit_b_projected", 4)]
        a_gates = step("hgrn_gates", 3)
        a_cols = step("hgrn_columns", 1)
        a_bounded = step("hgrn_bounded", 3)
        a_scores = step("hgrn_scores", 1 + LEVELS)
        a_kept = step("hgrn_scores_kept", 2 + LEVELS)
        a_scaled = step("hgrn_scaled", 1 + 3 * LEVELS)
        a_turned = step("hgrn_turned", 4)
        a_values = step("hgrn_values_turned", 2)
        a_keys = step("hgrn_keys_turned", 2)
        a_kv = step("hgrn_key_values", 2)
        a_state = step("hgrn_states", NC - 1)
        mixed = [step("hgrn_mixed", 2), step("gdn_mixed", 2)]
        o_kept = [step("hgrn_output_kept", 4), step("gdn_output_kept", 4)]
        o_summed = [step("hgrn_output_summed", 2), step("gdn_output_summed", 2)]
        o_rooted = [step("hgrn_output_rooted", 2), step("gdn_output_rooted", 2)]
        o_scaled = [step("hgrn_output_scaled", 3), step("gdn_output_scaled", 3)]
        y_high = [step("hgrn_y_high", 1), step("gdn_y_high", 1)]
        y_ready = [step("hgrn_y_ready", 1), step("gdn_y_ready", 1)]
        b_cols = step("gdn_columns", 5)
        b_conv = step("gdn_convolved", 3 * TAPS)
        b_silu = step("gdn_silu", 4)
        b_squared = step("gdn_squared", 2)
        b_summed = step("gdn_summed", 4)
        b_rooted = step("gdn_rooted", 4)
        b_normed = step("gdn_normed", 4)
        b_rows = step("gdn_rows_picked", 2)
        b_spread = step("gdn_rows_spread", 2)
        b_decay = step("gdn_decay_rows", 2)
        b_keyed = step("gdn_keys_scaled", 2)
        b_diff = step("gdn_decay_differences", NC + 2)
        b_exp = step("gdn_decay_exponentials", 3)
        b_masked = step("gdn_decays_masked", 1)
        b_prod = step("gdn_products", 4)
        b_scores = step("gdn_scores", 4)
        b_qdec = step("gdn_queries_decayed", 1)
        b_turned = step("gdn_turned", 4)
        b_vk = step("gdn_values_and_keys_turned", 4)
        b_ident = step("inverse_started", 2)
        b_u = step("inverse_right_factor", 2 * LEVELS)
        b_ukept = step("inverse_right_factor_kept", 2 * (LEVELS - 1))
        b_y = step("inverse_products", 2 * (2 * (LEVELS - 1)) - 2)
        b_inv = step("inverse_grown", 4 * LEVELS - 2)
        c_ks = step("chain_read_state", NC - 1)
        c_r = step("chain_residue", NC - 1)
        c_v = step("chain_value", NC)
        c_vn = step("chain_value_kept", NC)
        c_kv = step("chain_state_change", NC - 1)
        c_state = step("chain_state", NC - 1)
        l_in = [step(f"lru{u}_weights_loaded", 32) for u in range(2)]
        l_cols = [step(f"lru{u}_columns", 1) for u in range(2)]
        l_silu = [step(f"lru{u}_gate_silu", 1) for u in range(2)]
        l_conv = [step(f"lru{u}_convolved", TAPS) for u in range(2)]
        l_gates = [step(f"lru{u}_gate_products", 2) for u in range(2)]
        l_sig = [step(f"lru{u}_gates", 4) for u in range(2)]
        l_exp = [step(f"lru{u}_decays", 2) for u in range(2)]
        l_vec = [step(f"lru{u}_vector_steps", 7) for u in range(2)]
        l_root = [step(f"lru{u}_rooted", 1) for u in range(2)]
        l_high = [step(f"lru{u}_y_high", 1) for u in range(2)]
        l_y = [step(f"lru{u}_y_ready", 1) for u in range(2)]
        lz_ready = [step(f"lru{u}_projected", 2) for u in range(2)]
        l_lam = step("lambda_steps", 0)
        p_loaded = step("ple_input_loaded", 0)
        p_turned = step("ple_input_turned", 4)
        p_high = step("ple_input_high", 4)
        p_low = step("ple_input_low", 4)
        p_proj = step("ple_projection_kept", KD)
        p_gate = step("ple_gates", KD)
        p_prod = step("ple_gated", KD)
        p_added = step("ple_added", KD)
        f_scaled = step("final_scaled", KD)
        f_turned = step("final_turned", 2 * NC)
        f_kept = step("final_kept", 2 * NC)
        stored = [step(f"output{n}_stored", 0) for n in range(2)]

        def proj(u, n):
            return [("P", u, i) for i in range(n)]

        def outp(u, kind="O"):
            return [(kind, u, n) for n in range(KD)]

        class DenseStep:

            def __init__(self, what, pair, tile, nth, rank):
                self.what, self.pair, self.tile, self.nth, self.rank = what, pair, tile, nth, rank
                self.pieces = 2 if what[0] in "OV" else 2 * KD

        class Plan:

            def __init__(self, pair, *windows):
                self.steps, self.tiles, self.final, self.uses, self.windows = [], [], [], [0, 0], []
                for window in windows:
                    pieces = []
                    for what in window:
                        s = self.add(what, pair)
                        pieces += [(s, k) for k in range(s.pieces)]
                        pair = 1 - pair
                    self.windows.append(pieces)
                self.pair = pair

            def add(self, what, pair):
                kind, _, n = what
                for _ in range(KP if kind == "J" and n == 0 else 1 if n == 0 or kind in "PG" else 0):
                    self.tiles.append(what)
                    self.final.append(0)
                s = DenseStep(what, pair, len(self.tiles) - 1, self.uses[pair], len(self.steps))
                self.uses[pair] += 1
                self.steps.append(s)
                for t in range(KP if kind == "J" else 1):
                    self.final[s.tile - t] = s.rank
                return s

        def before(*plans):
            found, off = [], 0
            for plan in reversed(plans):
                off += len(plan.steps)
                found += [f - off for f in reversed(plan.final)]
            return found[1], found[0]

        class Place:

            def __init__(self, plan, step0, tile0, use0, turn=0, looped=False, layer=None):
                self.plan, self.step0, self.tile0, self.use0, self.turn = plan, step0, tile0, use0, turn
                self.looped, self.layer = looped, layer

            def ready(self, rank):
                return self.turn * (len(self.plan.steps) if self.looped else 0) + (self.step0 + rank + 1)

            def taken(self, s):
                return self.turn * (self.plan.uses[s.pair] if self.looped else 0) + (self.use0[s.pair] + s.nth + 1)

            def split(self, tile):
                return self.turn * self.loop_tiles() + (self.tile0 + tile + 1)

            def loop_tiles(self):
                return len(self.plan.tiles) if self.looped else 0

            def slot(self, tile):
                return (self.tile0 + tile) % 2

            def end(self):
                p = self.plan
                return (self.step0 + len(p.steps), self.tile0 + len(p.tiles),
                        [self.use0[i] + p.uses[i] for i in range(2)])

        EVEN_N, ODD_N = 4, 2
        TURNS = BLOCKS // 2

        def turns_of(place, n, count, layer):
            def windows(first, last):
                ahead, m = [] if last else proj(0, n), n - n // 4
                now, late = proj(1, n), [] if first else outp(1, "V")
                return [now[:m] + late + now[m:], ahead[:m] + outp(0) + ahead[m:]]

            first, loop, last = (Plan(place.plan.pair, *windows(f, l)) for f, l in ((True, False), (False, False), (False, True)))
            assert first.pair == loop.pair == place.plan.pair and not len(loop.tiles) % 2
            start = place.end()
            after = Place(first, *start).end()
            step0, tile0, use0 = (after[0] - len(loop.steps), after[1] - len(loop.tiles),
                                  [after[2][i] - loop.uses[i] for i in range(2)])

            def at(turn):
                if isinstance(turn, int) and turn == 0:
                    return Place(first, *start, layer=layer)
                if isinstance(turn, int):
                    k = turn
                    return Place(last, step0 + k * len(loop.steps), tile0 + k * len(loop.tiles),
                                 [use0[i] + k * loop.uses[i] for i in range(2)], layer=layer)
                return Place(loop, step0, tile0, use0, turn, looped=True, layer=layer)

            tail = Place(Plan(last.pair, outp(1)), *at(count - 1).end(), layer=layer)
            return at, tail, (first, loop, last)

        PRE_EVEN = Place(Plan(0, [("R", 0, 0)] + proj(0, EVEN_N)), 0, 0, [0, 0], layer="even")
        EVEN, EVEN_TAIL, EVEN_PLANS = turns_of(PRE_EVEN, EVEN_N, HEADS, "even")

        def behind(place, steps, layer=None):
            return Place(Plan(place.plan.pair, steps), *place.end(), layer=layer)

        PLE_STEPS = [("J", 0, n) for n in range(KD)] + [("G", 0, n) for n in range(KD)]
        PLE0 = behind(EVEN_TAIL, PLE_STEPS)
        PRE_ODD = behind(PLE0, proj(0, ODD_N), "odd")
        ODD, ODD_TAIL, ODD_PLANS = turns_of(PRE_ODD, ODD_N, TURNS, "odd")
        PLE1 = behind(ODD_TAIL, PLE_STEPS)

        def turns(eng, count, body):
            body(0)
            with eng.Fori(1, count - 1) as turn:
                body(turn)
            body(count - 1)

        FILLS_A = [28] + [4] * 8 + [3, 4, 3, 5, 5]
        FILLS_B = [2, 16, 24, 2, 1] + [1] * 13 + [1] + [2, 1] * 7 + [0, 0, 0]
        FILLS_L = [16, 16, 12, 4, 0, 0, 0]

        LAST_B = [0, 0, 4, 3, 3] + [1] * 13 + [0] * 18
        LAST_L = [0, 16, 0, 0, 0, 0, 0]

        class Filler:

            def __init__(self, place, window, weights, piece, done):
                self.pieces = place.plan.windows[window]
                if len(self.pieces) == 2 * KD and len(weights) > 1:
                    weights = {len(LAST_B): LAST_B, len(LAST_L): LAST_L}[len(weights)]
                self.upto = spread(len(self.pieces), weights)
                self.at = self.point = 0
                self.place, self.piece, self.done = place, piece, done

            def __call__(self):
                while self.at < self.upto[self.point]:
                    s, k = self.pieces[self.at]
                    if self.piece:
                        self.piece(s, k, self.place)
                    if self.done and k == s.pieces - 1:
                        self.done(s, self.place)
                    self.at += 1
                self.point += 1

            def finish(self):
                assert self.point == len(self.upto) and self.at == len(self.pieces)

        block = ctx.enter_context(nc.Block())

        @block.sync
        def _(sp):
            def load_rows(src, slot, at):
                n = src.shape[0]
                sp.dma_start(w1[at:at + n, slot * P:(slot + 1) * P], src).then_inc(vec_in.sem, 16)

            load_rows(gdn_conv_w[0].rearrange("t (m q) -> (t m) q", q=P), 0, C_CONV)
            load_rows(even_head_norm[0].rearrange("(m q) -> m q", q=P), 0, C_HEAD)
            load_rows(even_norm[0].rearrange("(m q) -> m q", q=P), 0, C_NORM)
            load_rows(lb_logits[0].rearrange("(m q) -> m q", q=P), 0, C_LB)
            load_rows(lru_conv_w[0].rearrange("t (m q) -> (t m) q", q=P), 1, 0)
            for i, v in enumerate((lru_conv_b, lru_b_a, lru_b_x, lru_lambda)):
                load_rows(v[0].rearrange("(m q) -> m q", q=P), 1, (TAPS + i) * BLOCKS)
            load_rows(odd_norm[0].rearrange("(m q) -> m q", q=P), 2, 0)
            load_rows(ple_norm.rearrange("d (m q) -> (d m) q", q=P), 2, 8)
            load_rows(final_norm.rearrange("(m q) -> m q", q=P), 2, 24)
            sp.dma_start(tiny[0:HEADS, 1:2], gdn_a_log.rearrange("a (h b) -> (a h) b", b=1)).then_inc(small_in.sem, 16)
            sp.dma_start(tiny[0:HEADS, 2:3], gdn_dt_bias.rearrange("a (h b) -> (a h) b", b=1)).then_inc(small_in.sem, 16)

            def load(src, before, width=P):
                if before is not None:
                    sp.wait_ge(w_split.sem, before)
                dst = w_stage[:, :] if len(src.shape) == 2 else w_stage[:, :].rearrange("p (k n) -> p k n", n=P)
                sp.dma_start(dst, src).then_inc(w_in.sem, 16)

            def columns(w, at):
                return w[:, at].rearrange("(k p) n -> p k n", p=P)

            w_even = even_w_in[0]
            sp.wait_ge(cleared.sem, 1)
            stage3 = w_stage[:, :].rearrange("p (k n) -> p k n", n=P)
            for i, at in enumerate((0, 32)):
                sp.dma_start(stage3[:, :, at:at + HEADS],
                             w_even[:, 6 * AW + i * HEADS:6 * AW + (i + 1) * HEADS].rearrange("(k p) n -> p k n", p=P))\
                    .then_inc(w_in.sem, 16)
            starts = ([0, AW, 2 * AW, GATE0], [3 * AW, 4 * AW, 5 * AW, GATE0 + AW])

            def even_columns(u, n, head):
                return w_even[:, bass.ds(starts[u][n] + head * P, P)].rearrange("(k p) n -> p k n", p=P)

            def odd_columns(u, n, turn):
                at = n * BLOCKS * P + u * P
                return odd_w_in[0][:, bass.ds(at + turn * (2 * P), P)].rearrange("(k p) n -> p k n", p=P)

            for n in range(EVEN_N):
                load(even_columns(0, n, 0), 1 + n)

            def even_turn(turn):
                place = EVEN(turn)
                for t, (kind, u, n) in enumerate(place.plan.tiles):
                    if kind == "P":
                        load(even_columns(u, n, turn + 1 if u == 0 else turn), place.split(t - 1))
                    else:
                        load(even_w_out[0][bass.ds(turn * P + (AW - P if kind == "V" else 0), P), :],
                             place.split(t - 1))

            turns(sp, HEADS, even_turn)
            load(even_w_out[0][AW + (HEADS - 1) * P:AW + HEADS * P, :], EVEN_TAIL.split(-1))

            def load_ple(i, place):
                sp.dma_start(cv[:, 0:2, :].rearrange("p a b -> p (a b)").rearrange("p (c q) -> p c q", q=KP * P),
                             p_in[i, 0].rearrange("(c t) q -> t c q", t=P)).then_inc(p_loaded.sem, 16)
                for n in range(KP):
                    load(ple_proj_w[i][n * P:(n + 1) * P, :], place.split(n - 1))
                for n in range(KD):
                    load(ple_gate_w[i][:, n * P:(n + 1) * P].rearrange("(k p) n -> p k n", p=P), place.split(KP + n - 1))

            sp.wait_ge(y_ready[1].sem, HEADS)
            load_ple(0, PLE0)

            def load_gates(turn, u):
                sp.dma_start(w1[:, :].rearrange("p (a b) -> p a b", b=P)[:, 2 * u, :],
                             lru_w_a[0][bass.ds(turn * 2 + u, 1)].rearrange("g i j -> i (g j)")).then_inc(l_in[u].sem, 16)
                sp.dma_start(w1[:, :].rearrange("p (a b) -> p a b", b=P)[:, 2 * u + 1, :],
                             lru_w_x[0][bass.ds(turn * 2 + u, 1)].rearrange("g i j -> i (g j)")).then_inc(l_in[u].sem, 16)

            for n in range(ODD_N):
                load(odd_columns(0, n, 0), PRE_ODD.split(n - 1))
            after(sp, norm_low, 2, KD)
            for u in range(2):
                load_gates(0, u)

            def odd_turn(turn):
                place = ODD(turn)
                for t, (kind, u, n) in enumerate(place.plan.tiles):
                    if kind == "P":
                        load(odd_columns(u, n, turn + 1 if u == 0 else turn), place.split(t - 1))
                        continue
                    load(odd_w_out[0][bass.ds(turn * (2 * P) - (P if kind == "V" else 0), P), :], place.split(t - 1))
                    if kind == "V":
                        after(sp, l_y[1], turn, 0)
                        load_gates(turn, 1)
                    elif not (isinstance(turn, int) and turn == TURNS - 1):
                        after(sp, l_y[0], turn, 1)
                        load_gates(turn + 1, 0)

            turns(sp, TURNS, odd_turn)
            load(odd_w_out[0][(BLOCKS - 1) * P:BLOCKS * P, :], ODD_TAIL.split(-1))
            sp.wait_ge(l_y[1].sem, TURNS)
            load_ple(1, PLE1)

            for c in range(NC):
                sp.wait_ge(f_kept.sem, 2 * c + 2)
                sp.dma_start(out[0, c * P:(c + 1) * P, :], (w1, w2)[c % 2][:, :]).then_inc(stored[c % 2].sem, 16)
            for n in range(2):
                sp.wait_ge(stored[n].sem, 16 * NC // 2)

        @block.gpsimd
        def _(pool):
            build = zb[:, :, :].rearrange("p a b -> p (a b)")[:, 0:(2 * LEVELS + 1) * P].rearrange("p (a b) -> p a b", b=P)
            count = [0]

            def link(ins):
                count[0] += 1
                ins.then_inc(made.sem, 1)
                pool.wait_ge(made.sem, count[0])

            pool.memset(w_stage[:, :], 0.0).then_inc(cleared.sem, 1)
            link(pool.memset(tiny[:, 0:1], EPS))
            link(pool.memset(ones[:, :], 1.0))
            link(pool.memset(ident[:, :], 0.0))
            link(pool.affine_select(out=ident[:, :], in_=ident[:, :], compare_op=ALU.not_equal, fill=1.0,
                                    base=0, pattern=[[-1, P]], channel_multiplier=1))
            link(pool.memset(upper[:, :], 1.0))
            link(pool.affine_select(out=upper[:, :], in_=upper[:, :], compare_op=ALU.is_ge, fill=0.0,
                                    base=0, pattern=[[1, P]], channel_multiplier=-1))
            link(pool.memset(build[:, :, :], 0.0))
            for l in range(LEVELS):
                b = 1 << l
                n = P // (2 * b)
                right = build[:, l, :].rearrange("p (n two b) -> p n two b", two=2, b=b)[:, :, 1, :]
                left = build[:, LEVELS + l, :].rearrange("p (n two b) -> p n two b", two=2, b=b)[:, :, 0, :]
                for v, off in ((right, 0), (left, b)):
                    link(pool.memset(v, 1.0))
                    link(pool.affine_select(out=v, in_=v, compare_op=ALU.is_ge, fill=0.0, base=-off,
                                            pattern=[[-2 * b, n], [0, b]], channel_multiplier=1))
                    link(pool.affine_select(out=v, in_=v, compare_op=ALU.is_ge, fill=0.0, base=off + b - 1,
                                            pattern=[[2 * b, n], [0, b]], channel_multiplier=-1))
            link(pool.tensor_copy(build[:, 2 * LEVELS, :], ident[:, :]))
            assert count[0] == MADE

            def split(slot, loaded, used):
                pool.wait_ge(w_in.sem, loaded)
                if used is not None:
                    pool.wait_ge(dense_ready.sem, used)
                pool.sem_inc(split_begun.sem, 1)
                pool.tensor_scalar(w_high[:, slot, :], w_stage[:, :], 1.0, 0.0, ALU.mult, ALU.add)\
                    .then_inc(w_split_high.sem, 1)

            def rest(slot, n):
                pool.wait_ge(w_split_high.sem, n)
                pool.tensor_tensor(w_low[:, slot, :], w_stage[:, :], w_high[:, slot, :].bitcast(F32),
                                   ALU.subtract).then_inc(w_split.sem, 1)

            def tile(place, t, used):
                slot = place.slot(t)
                split(slot, place.turn * (16 * place.loop_tiles()) + 16 * (place.tile0 + t + 2), used)
                rest(slot, place.split(t))

            def tiles(place, *plans):
                back, final = before(*plans), place.plan.final
                for t in range(len(final)):
                    tile(place, t, place.ready(final[t - 2] if t >= 2 else back[t]))

            tile(PRE_EVEN, 0, None)
            tile(PRE_EVEN, 1, None)
            for n in range(1, EVEN_N):
                tile(PRE_EVEN, 1 + n, n)

            def all_tiles(pre, count, at, plans, tail):
                first, loop, last = plans
                assert before(first) == before(loop)
                turns(pool, count, lambda turn: tiles(at(turn), pre if isinstance(turn, int) and turn == 0 else loop))
                tiles(tail, last)

            all_tiles(PRE_EVEN.plan, HEADS, EVEN, EVEN_PLANS, EVEN_TAIL)
            tiles(PLE0, EVEN_PLANS[2], EVEN_TAIL.plan)
            tiles(PRE_ODD, PLE0.plan)
            all_tiles(PRE_ODD.plan, TURNS, ODD, ODD_PLANS, ODD_TAIL)
            tiles(PLE1, ODD_PLANS[2], ODD_TAIL.plan)

        @block.tensor
        def _(pe):
            def three(out_, wh, wl, xh_, xl_, first, last):
                pe.matmul(out_, wh, xh_, start=first, stop=False)
                pe.matmul(out_, wh, xl_, start=False, stop=False)
                return pe.matmul(out_, wl, xh_, start=False, stop=last)

            turn_now = [0]

            def free(s, place):
                if isinstance(place.turn, int) and place.taken(s) < 2:
                    return
                pe.wait_ge(taken[s.pair].sem, place.taken(s) - 1)

            def piece(s, n_piece, place):
                kind, u, n = s.what
                k, h = divmod(n_piece, 2)
                pair, slot = s.pair, place.slot(s.tile)
                last = n_piece == s.pieces - 1
                if n_piece == 0:
                    pe.wait_ge(w_split.sem, place.split(s.tile))
                    free(s, place)
                    if kind in "OV" and n == 0:
                        y = y_ready if place.layer == "even" else l_y
                        now = turn_now[0]
                        pe.wait_ge(y[u].sem, now if kind == "V" else now + 1)
                bank = dense[2 * pair + h]
                if kind in "PG":
                    w = slice(k * P, (k + 1) * P)
                    r = three(bank[:, :], w_high[:, slot, w], w_low[:, slot, w],
                              half(xh[:, k, :], h), half(xl[:, k, :], h), k == 0, k == KD - 1)
                else:
                    w = slice(n * P, (n + 1) * P)
                    r = three(bank[:, :], w_high[:, slot, w], w_low[:, slot, w],
                              half(yh[:, u, :], h), half(yl[:, u, :], h), True, True)
                if last:
                    r.then_inc(dense_ready.sem, 1)

            def norm_sum(n, k):
                after(pe, norm_squared, n, k + 1)
                for h in range(2):
                    r = pe.matmul(work[h][:, :], ones[:, :], half(squares(n, k), h), start=k == 0, stop=k == KD - 1)
                r.then_inc(norm_summed.sem, 1)

            def turn_all(src, banks, st):
                for c in range(NC):
                    r = pe.transpose(in_half(banks[c // HC], c), chunk(src, c), ident[:, :])
                    if c % HC == HC - 1:
                        r.then_inc(st.sem, 1)

            pe.wait_ge(vec_in.sem, 16 * 12)
            pe.wait_ge(made.sem, IDENT_MADE)
            for i, n in enumerate((P, P, 32)):
                r = pe.transpose(work[0][:, i * P:i * P + n], w1[0:n, i * P:(i + 1) * P], ident[0:n, 0:n])
            r.then_inc(vec_turned.sem, 1)
            pe.wait_ge(x_loaded.sem, 16 * NC)
            for k in range(KD + 2):
                if k < KD:
                    for h in range(2):
                        if k >= 2:
                            pe.wait_ge(x_kept[h].sem, k - 1)
                        for c in range(HC):
                            r = pe.transpose(in_half(dense[2 * (k % 2) + h], c),
                                             tiles8[h * HC + c][:, k * P:(k + 1) * P], ident[:, :])
                        r.then_inc(x_turned.sem, 1)
                if k == 1:
                    pe.wait_ge(vec_kept.sem, 1)
                if k >= 2:
                    norm_sum(0, k - 2)

            pre = PRE_EVEN.plan.steps
            pe.wait_ge(w_split.sem, 1)
            for h in range(2):
                pe.wait_ge(x_kept[h].sem, KD)
            for k in range(KD):
                after(pe, norm_low, 0, k + 1)
                for h in range(2):
                    r = three(dense[h][0:64, :], w_high[:, 0, k * P:k * P + 64], w_low[:, 0, k * P:k * P + 64],
                              half(xh[:, k, :], h), half(xl[:, k, :], h), k == 0, k == KD - 1)
                if k == KD - 1:
                    r.then_inc(dense_ready.sem, 1)
                for h in range(2):
                    piece(pre[1], 2 * k + h, PRE_EVEN)
            for s in pre[2:]:
                for k in range(2 * KD):
                    piece(s, k, PRE_EVEN)
            pe.wait_ge(row_vec.sem, 5)
            after(pe, norm_rooted, 0, 2)
            for i in range(2):
                for c in range(NC):
                    at = 32 * i
                    r = pe.transpose(work[i][:, c * HEADS:(c + 1) * HEADS],
                                     rows[at:at + HEADS, c * CHUNK:(c + 1) * CHUNK],
                                     ident[at:at + HEADS, at:at + HEADS])
                r.then_inc(row_turned.sem, 1)

            def head_sum(u, turn, sq):
                for h in range(2):
                    after(pe, o_kept[u], turn, 2 * h + 2)
                    pe.matmul(work[2 + h][:, :], ones[:, :], half(sq, h), start=True, stop=True)\
                        .then_inc(o_summed[u].sem, 1)

            def hgrn(turn, fill):
                fill()
                after(pe, a_bounded, turn, 3)
                for c in range(NC):
                    r = pe.matmul(in_half(work[c // HC], c), chunk(k_a, c), chunk(q_a, c), start=True, stop=True)
                r.then_inc(a_scores.sem, 1)
                fill()
                for l in range(LEVELS):
                    b = 1 << l
                    after(pe, a_scaled, turn, 1 + 3 * l)
                    if l >= 2:
                        after(pe, a_kept, turn, 2 + l - 1)
                    for c in range(NC):
                        right = chunk(q_a, c).rearrange("p (n two b) -> p n two b", two=2, b=b)[:, :, 1, :]
                        r = pe.matmul(work[2 + l % 2][:, c * 64:(c + 1) * 64], chunk(k_a, c), right,
                                      start=True, stop=True)
                    r.then_inc(a_scores.sem, 1)
                    if l == 0:
                        after(pe, a_kept, turn, 2)
                        turn_all(v_a, work[0:2], a_turned)
                    fill()
                after(pe, a_values, turn, 2)
                after(pe, a_scaled, turn, 1 + 3 * LEVELS)
                turn_all(k_a, work[0:2], a_turned)
                fill()
                for h in range(2):
                    after(pe, a_keys, turn, h + 1)
                    after(pe, a_kept, turn, 2 + LEVELS)
                    for c in range(h * HC, min((h + 1) * HC, NC - 1)):
                        r = pe.matmul(in_half(work[2 + h], c), chunk(k_a, c), chunk(v_a, c), start=True, stop=True)
                    r.then_inc(a_kv.sem, 1)
                fill()
                for h in range(2):
                    for c in range(h * HC, (h + 1) * HC):
                        o = in_half(work[h], c)
                        r = pe.matmul(o, chunk(v_a, c), chunk(w1, c), start=True, stop=c == 0)
                        if c:
                            after(pe, a_state, turn, c)
                            r = pe.matmul(o, w2[:, (c - 1) * P:c * P], chunk(q_a, c), start=False, stop=True)
                    r.then_inc(mixed[0].sem, 1)
                fill()
                after(pe, a_state, turn, NC - 1)
                head_sum(0, turn, f_a)
                fill()
                fill()

            def gdn(turn, fill):
                fill()
                for i in range(2):
                    after(pe, b_squared, turn, i + 1)
                    for h in range(2):
                        pe.matmul(work[2 * i + h][:, :], ones[:, :], half(raw[i], h), start=True, stop=True)\
                            .then_inc(b_summed.sem, 1)
                fill()
                for i in range(2):
                    after(pe, b_rooted, turn, 2 * i + 2)
                    after(pe, b_rows, turn, 2)
                    at = 32 * i
                    for h in range(2):
                        r = pe.matmul(work[2 * i + h][:, :], ones[at:at + HEADS, :],
                                      w2[at:at + HEADS, h * HALF:(h + 1) * HALF], start=True, stop=True)
                    r.then_inc(b_spread.sem, 1)
                fill()
                after(pe, b_normed, turn, 4)
                after(pe, b_diff, turn, NC + 2)
                after(pe, b_keyed, turn, 2)
                for i, other in enumerate((raw[1], q_b)):
                    for c in range(NC):
                        r = pe.matmul(in_half(work[2 * i + c // HC], c), chunk(k_b, c), chunk(other, c),
                                      start=True, stop=True)
                        if c % HC == HC - 1:
                            r.then_inc(b_prod.sem, 1)
                fill()
                after(pe, b_scores, turn, 2)
                after(pe, b_silu, turn, 3)
                turn_all(v_b, work[0:2], b_turned)
                after(pe, b_scores, turn, 4)
                turn_all(k_b, work[2:4], b_turned)
                fill()
                after(pe, b_ident, turn, 2)
                for l in range(LEVELS):
                    for h in range(2):
                        right = work[2 * h]
                        if l == 0:
                            after(pe, b_vk, turn, 4)
                        else:
                            after(pe, b_inv, turn, 4 * l if h else 4 * l - 2)
                        for c in range(h * HC, (h + 1) * HC):
                            r = pe.matmul(in_half(right, c), chunk(raw[1], c),
                                          ident[:, :] if l == 0 else chunk(w1, c), start=True, stop=True)
                        r.then_inc(b_u.sem, 1)
                    if l:
                        fill()
                        for h in range(2):
                            after(pe, b_ukept, turn, 2 * (l - 1) + h + 1)
                            if l < LEVELS - 1:
                                for c in range(h * HC, (h + 1) * HC):
                                    r = pe.matmul(in_half(work[2 * h + 1], c), chunk(w3, c), chunk(w2, c),
                                                  start=True, stop=True)
                                r.then_inc(b_y.sem, 1)
                            for c in range(h * HC, (h + 1) * HC):
                                r = pe.matmul(in_half(work[2 * h], c), chunk(w2, c), chunk(w3, c),
                                              start=True, stop=True)
                            r.then_inc(b_y.sem, 1)
                    fill()
                for c in range(NC):
                    before = state[:, c % 2, :]
                    if c == 0:
                        after(pe, b_inv, turn, 4 * LEVELS - 2)
                    else:
                        after(pe, c_state, turn, c)
                        pe.matmul(work[0][:, 0:P], chunk(k_b, c), before, start=True, stop=True).then_inc(c_ks.sem, 1)
                        fill()
                        after(pe, c_r, turn, c)
                    pe.matmul(work[1][:, 0:P], chunk(w3, c), chunk(v_b, c), start=True, stop=True).then_inc(c_v.sem, 1)
                    fill()
                    after(pe, c_vn, turn, c + 1)
                    if c < NC - 1:
                        pe.matmul(work[0][:, 0:P], chunk(raw[0], c), chunk(w2, c), start=True, stop=True)\
                            .then_inc(c_kv.sem, 1)
                    o = in_half(work[2 + c // HC], c)
                    if c:
                        pe.matmul(o, before, chunk(q_b, c), start=True, stop=False)
                    r = pe.matmul(o, chunk(w2, c), chunk(raw[2], c), start=c == 0, stop=True)
                    if c % HC == HC - 1:
                        r.then_inc(mixed[1].sem, 1)
                after(pe, o_kept[1], turn, 4)
                head_sum(1, turn, raw[0])
                fill()
                fill()
                fill()

            def lru(u, turn, fill):
                fill()
                after(pe, l_in[u], turn, 32)
                after(pe, l_conv[u], turn, TAPS)
                blocks = w1[:, :].rearrange("p (a b) -> p a b", b=P)
                for i in range(2):
                    for h in range(2):
                        r = pe.matmul(work[2 * i + h][:, :], blocks[:, 2 * u + i, :], half(cv[:, 0, :], h),
                                      start=True, stop=True)
                    r.then_inc(l_gates[u].sem, 1)
                for _ in FILLS_L[1:]:
                    fill()

            def even_turn(turn):
                turn_now[0] = turn
                f = Filler(EVEN(turn), 0, FILLS_A, piece, None)
                hgrn(turn, f)
                f.finish()
                f = Filler(EVEN(turn), 1, FILLS_B, piece, None)
                gdn(turn, f)
                f.finish()

            turns(pe, HEADS, even_turn)
            Filler(EVEN_TAIL, 0, [1], piece, None)()

            def ple(i, place, n_norm):
                pe.wait_ge(p_loaded.sem, 16 * (i + 1))
                src = cv[:, 0:2, :].rearrange("p a b -> p (a b)").rearrange("p (c q) -> p c q", q=KP * P)
                for k in range(KP):
                    for h in range(2):
                        for c in range(HC):
                            r = pe.transpose(in_half(work[2 * k + h], c), src[:, h * HC + c, k * P:(k + 1) * P],
                                             ident[:, :])
                        r.then_inc(p_turned.sem, 1)
                after(pe, p_low, i, 2)
                for k in range(KD):
                    norm_sum(n_norm, k)
                pe.wait_ge(w_split.sem, place.split(KP - 1))
                after(pe, p_low, i, 4)
                for n in range(KD):
                    s = place.plan.steps[n]
                    pair = s.pair
                    free(s, place)
                    for k in range(KP):
                        slot = place.slot(k)
                        w = slice(n * P, (n + 1) * P)
                        for h in range(2):
                            r = three(dense[2 * pair + h][:, :], w_high[:, slot, w], w_low[:, slot, w],
                                      half(yh[:, k, :], h), half(yl[:, k, :], h), k == 0, k == KP - 1)
                    r.then_inc(dense_ready.sem, 1)
                after(pe, norm_rooted, n_norm, 2)
                for n in range(KD + 2):
                    if n < KD:
                        for k in range(2 * KD):
                            if n == 0 and k % 2 == 0:
                                after(pe, norm_low, n_norm, k // 2 + 1)
                            piece(place.plan.steps[KD + n], k, place)
                    if n >= 2:
                        norm_sum(n_norm + 1, n - 2)

            ple(0, PLE0, 1)
            for k in range(KD):
                after(pe, norm_low, 2, k + 1)
                for n in range(ODD_N):
                    for h in range(2):
                        piece(PRE_ODD.plan.steps[n], 2 * k + h, PRE_ODD)

            def odd_turn(turn):
                turn_now[0] = turn
                for u in range(2):
                    f = Filler(ODD(turn), u, FILLS_L, piece, None)
                    lru(u, turn, f)
                    f.finish()

            turns(pe, TURNS, odd_turn)
            Filler(ODD_TAIL, 0, [1], piece, None)()

            ple(1, PLE1, 3)
            after(pe, f_scaled, 0, KD)
            after(pe, norm_rooted, 4, 2)
            for c in range(NC):
                for h in range(2):
                    i = 2 * c + h
                    if i >= 4:
                        pe.wait_ge(f_kept.sem, i - 3)
                    for k in range(KD // 2):
                        r = pe.transpose(in_half(work[i % 4], k), chunk(tiles8[h * (KD // 2) + k], c), ident[:, :])
                    r.then_inc(f_turned.sem, 1)

        @block.scalar
        def _(act):
            eps = tiny[:, 0:1]

            turn_now = [0]

            def evac(s, place):
                kind, u, n = s.what
                if kind != "P":
                    return
                pair, odd = s.pair, place.layer == "odd"
                if odd:
                    dst = raw[u] if n == 0 else za[:, u, :]
                elif u == 0:
                    dst = za[:, n, :]
                else:
                    dst = raw[n] if n < 3 else zg[:, :]
                act.wait_ge(dense_ready.sem, place.ready(s.rank))
                if n == 0 and not odd and place is not PRE_EVEN:
                    if u == 0:
                        act.wait_ge(y_ready[0].sem, turn_now[0] + 1)
                    elif not (isinstance(turn_now[0], int) and turn_now[0] == 0):
                        act.wait_ge(y_ready[1].sem, turn_now[0])
                act.activation(half(dst, 0), dense[2 * pair][:, :], ACT.Copy)\
                    .then_inc((lz_ready if odd else z_ready)[u].sem, 1)
                act.activation(half(dst, 1), dense[2 * pair + 1][:, :], ACT.Copy).then_inc(taken[pair].sem, 1)

            def norm_root(n):
                for h in range(2):
                    after(act, norm_summed, n, KD)
                    act.activation(half(w3, h), work[h][:, :], ACT.Sqrt, bias=eps, scale=1.0 / D)\
                        .then_inc(norm_rooted.sem, 1)

            def square(n, k):
                if k >= 2:
                    after(act, norm_summed, n, k - 1)
                act.activation(squares(n, k), x[:, k, :], ACT.Square).then_inc(norm_squared.sem, 1)

            def norm(n, split=True):
                norm_root(n)
                if split:
                    for k in range(KD):
                        after(act, norm_scaled, n, k + 1)
                        act.activation(xh[:, k, :], (w1, w2)[k % 2][:, :], ACT.Copy).then_inc(norm_high.sem, 1)

            for c in range(NC):
                act.dma_start(tiles8[c], x_in[0, c * P:(c + 1) * P, :]).then_inc(x_loaded.sem, 16)
            act.wait_ge(vec_turned.sem, 1)
            act.activation(cols[:, :], work[0][:, 0:2 * P + 32], ACT.Copy).then_inc(vec_kept.sem, 1)
            for k in range(KD):
                act.wait_ge(x_turned.sem, 2 * k + 1)
                act.activation(half(x[:, k, :], 0), dense[2 * (k % 2)][:, :], ACT.Copy).then_inc(x_kept[0].sem, 1)
                if k:
                    act.wait_ge(x_kept[0].sem, k)
                    act.wait_ge(x_kept[1].sem, k)
                    square(0, k - 1)
            for h in range(2):
                act.wait_ge(x_kept[h].sem, KD)
            square(0, KD - 1)
            norm(0)
            act.wait_ge(vec_ready.sem, 1)
            act.activation(lows[:, 1, :], lows[:, 0, :], ACT.Exp).then_inc(l_lam.sem, 1)
            lam = cols[:, C_ODD + 7 * BLOCKS:C_ODD + 8 * BLOCKS]
            t0, t1 = pairs(0), pairs(1)
            act.wait_ge(vec_kept.sem, 1)
            act.activation(t0, lam, ACT.Abs).then_inc(l_lam.sem, 1)
            act.wait_ge(l_lam.sem, 2)
            act.activation(t1, t0, ACT.Exp, scale=-1.0).then_inc(l_lam.sem, 1)
            act.wait_ge(l_lam.sem, 3)
            act.activation(t0, t1, ACT.Ln, bias=1.0).then_inc(l_lam.sem, 1)
            act.activation(unit_cols[:, 0, :], lam, ACT.Relu, scale=-1.0).then_inc(l_lam.sem, 1)
            act.wait_ge(small_in.sem, 32)
            act.activation(tiny[0:HEADS, 3:4], tiny[0:HEADS, 1:2], ACT.Exp).then_inc(l_lam.sem, 1)

            act.wait_ge(dense_ready.sem, 1)
            dt = tiny[0:HEADS, 2:3]
            for h in range(2):
                act.activation(rows[32:32 + HEADS, h * HALF:(h + 1) * HALF], dense[h][32:32 + HEADS, :], ACT.Sigmoid)\
                    .then_inc(row_step.sem, 1)
            for h in range(2):
                act.activation(w1[0:HEADS, h * HALF:(h + 1) * HALF], dense[h][0:HEADS, :], ACT.Abs, bias=dt)\
                    .then_inc(row_step.sem, 1)
                act.activation(w2[0:HEADS, h * HALF:(h + 1) * HALF], dense[h][0:HEADS, :], ACT.Relu, bias=dt)\
                    .then_inc(row_step.sem if h == 0 else taken[0].sem, 1)
            act.wait_ge(row_step.sem, 5)
            act.activation(w1[0:HEADS, :], w1[0:HEADS, :], ACT.Exp, scale=-1.0).then_inc(row_step.sem, 1)
            act.wait_ge(row_step.sem, 6)
            act.activation(w1[0:HEADS, :], w1[0:HEADS, :], ACT.Ln, bias=1.0).then_inc(row_step.sem, 1)
            for s in PRE_EVEN.plan.steps[1:]:
                evac(s, PRE_EVEN)
            for i in range(2):
                act.wait_ge(row_turned.sem, i + 1)
                act.activation(gcols[:, i, :, :].rearrange("p c h -> p (c h)"), work[i][:, 0:NC * HEADS], ACT.Copy)\
                    .then_inc(row_cols.sem, 1)

            def head_out(u, turn, o, sq):
                for h in range(2):
                    after(act, mixed[u], turn, h + 1)
                    bank = work[(0, 2)[u] + h]
                    act.activation(half(o, h), bank[:, :], ACT.Copy).then_inc(o_kept[u].sem, 1)
                    act.activation(half(sq, h), bank[:, :], ACT.Square).then_inc(o_kept[u].sem, 1)
                for h in range(2):
                    after(act, o_summed[u], turn, h + 1)
                    act.activation(half(sq, h), work[2 + h][:, :], ACT.Sqrt, bias=eps, scale=1.0 / P)\
                        .then_inc(o_rooted[u].sem, 1)

            def round_y(u, turn, o, st, high):
                after(act, st, turn, st.per_turn)
                act.activation(yh[:, u, :], o, ACT.Copy).then_inc(high.sem, 1)

            def hgrn(turn, fill):
                after(act, z_ready[0], turn, 4)
                act.activation(k_a, f_a, ACT.Sigmoid, scale=-1.0).then_inc(a_gates.sem, 1)
                after(act, a_gates, turn, 1)
                act.activation(f_a, f_a, ACT.Sigmoid).then_inc(a_gates.sem, 1)
                act.activation(gate_a, gate_a, ACT.Silu).then_inc(a_gates.sem, 1)
                fill()
                fill()
                for l in range(LEVELS):
                    if l == 0:
                        for h in range(2):
                            after(act, a_turned, turn, h + 1)
                            act.activation(half(v_a, h), work[h][:, :], ACT.Copy).then_inc(a_values.sem, 1)
                    fill()
                for h in range(2):
                    after(act, a_turned, turn, 2 + h + 1)
                    act.activation(half(k_a, h), work[h][:, :], ACT.Copy).then_inc(a_keys.sem, 1)
                fill()
                fill()
                fill()
                after(act, a_state, turn, HC)
                head_out(0, turn, q_a, f_a)
                fill()
                for m in range(2):
                    after(act, b_conv, turn, TAPS * (m + 1))
                    act.activation(cv[:, m, :], cv[:, m, :], ACT.Silu).then_inc(b_silu.sem, 1)
                    after(act, b_silu, turn, m + 1)
                    act.activation(raw[m], cv[:, m, :], ACT.Square).then_inc(b_squared.sem, 1)
                after(act, b_conv, turn, 3 * TAPS)
                act.activation(v_b, v_b, ACT.Silu).then_inc(b_silu.sem, 1)
                round_y(0, turn, q_a, o_scaled[0], y_high[0])
                fill()

            def gdn(turn, fill):
                for i in range(2):
                    for h in range(2):
                        after(act, b_summed, turn, 2 * i + h + 1)
                        act.activation(half(raw[i], h), work[2 * i + h][:, :], ACT.Sqrt, bias=eps)\
                            .then_inc(b_rooted.sem, 1)
                fill()
                fill()
                s = next(s for s in EVEN(turn).plan.steps if s.what == ("P", 1, 3))
                act.wait_ge(taken[s.pair].sem, EVEN(turn).taken(s))
                act.activation(zg[:, :], zg[:, :], ACT.Silu).then_inc(b_silu.sem, 1)
                fill()
                after(act, b_normed, turn, 4)
                after(act, b_spread, turn, 1)
                for h in range(2):
                    act.activation(half(raw[0], h), work[h][:, :], ACT.Exp).then_inc(b_decay.sem, 1)
                act.activation(w1[:, :].rearrange("p (c t) -> p c t", t=P), wide(ident, NC), ACT.Copy)\
                    .then_inc(b_ident.sem, 1)
                act.activation(w3[:, :].rearrange("p (c t) -> p c t", t=P), wide(ident, NC), ACT.Copy)\
                    .then_inc(b_ident.sem, 1)
                after(act, b_diff, turn, NC + 2)
                act.activation(raw[2], raw[2], ACT.Exp).then_inc(b_exp.sem, 1)
                act.activation(head_cols[:, 2, :], head_cols[:, 0, :], ACT.Exp).then_inc(b_exp.sem, 1)
                act.activation(head_cols[:, 3, :], head_cols[:, 3, :], ACT.Exp).then_inc(b_exp.sem, 1)
                fill()
                fill()
                for l in range(LEVELS):
                    if l:
                        for h in range(2):
                            after(act, b_u, turn, 2 * l + h + 1)
                            act.activation(half(w2, h), work[2 * h][:, :], ACT.Copy).then_inc(b_ukept.sem, 1)
                        fill()
                    fill()
                for c in range(NC):
                    if c:
                        fill()
                    after(act, c_v, turn, c + 1)
                    act.activation(chunk(w2, c), work[1][:, 0:P], ACT.Copy).then_inc(c_vn.sem, 1)
                    fill()
                head_out(1, turn, q_b, raw[0])
                fill()
                round_y(1, turn, q_b, o_scaled[1], y_high[1])
                fill()
                fill()

            def even_turn(turn):
                turn_now[0] = turn
                for w, (unit, weights) in enumerate(((hgrn, FILLS_A), (gdn, FILLS_B))):
                    f = Filler(EVEN(turn), w, weights, None, evac)
                    unit(turn, f)
                    f.finish()

            def wide(t, n):
                a = t[:, :]
                return bass.AP(a.tensor, a.offset, [list(a.ap[0]), [0, n], [1, P]])

            turns(act, HEADS, even_turn)

            def ple(i, tail, place, n_norm):
                for k in range(KD):
                    row = tail.plan.steps[k]
                    act.wait_ge(taken[row.pair].sem, tail.taken(row))
                    square(n_norm, k)
                    if k == 1:
                        for j in range(2 * KP):
                            after(act, p_turned, i, j + 1)
                            act.activation(half(yh[:, j // 2, :], j % 2), work[j][:, :], ACT.Copy).then_inc(p_high.sem, 1)

                def keep(n):
                    pair = place.plan.steps[n].pair
                    act.wait_ge(dense_ready.sem, place.ready(n))
                    act.activation(half(tiles8[n], 0), dense[2 * pair][:, :], ACT.Copy).then_inc(p_proj.sem, 1)
                    act.activation(half(tiles8[n], 1), dense[2 * pair + 1][:, :], ACT.Copy).then_inc(taken[pair].sem, 1)

                norm_root(n_norm)
                for k in range(KD):
                    keep(k)
                    after(act, norm_scaled, n_norm, k + 1)
                    act.activation(xh[:, k, :], (w1, w2)[k % 2][:, :], ACT.Copy).then_inc(norm_high.sem, 1)
                for n in range(KD + 1):
                    if n < KD:
                        local = KD + n
                        pair = place.plan.steps[local].pair
                        act.wait_ge(dense_ready.sem, place.ready(local))
                        if n >= 2:
                            after(act, p_added, i, n - 1)
                        g = (w1, w2)[n % 2]
                        act.activation(half(g, 0), dense[2 * pair][:, :], ACT.Sigmoid).then_inc(p_gate.sem, 1)
                        act.activation(half(g, 1), dense[2 * pair + 1][:, :], ACT.Sigmoid).then_inc(taken[pair].sem, 1)
                    if n:
                        after(act, p_added, i, n)
                        square(n_norm + 1, n - 1)

            ple(0, EVEN_TAIL, PLE0, 1)
            norm(2)
            for s in PRE_ODD.plan.steps:
                evac(s, PRE_ODD)

            def lru(u, turn, fill):
                uc = unit_cols[:, u, :]
                after(act, lz_ready[u], turn, 2)
                fill()
                for i in range(2):
                    after(act, l_gates[u], turn, i + 1)
                    for h in range(2):
                        act.activation(half(cv[:, 1 + i, :], h), work[2 * i + h][:, :], ACT.Sigmoid,
                                       bias=uc[:, 5 + i:6 + i]).then_inc(l_sig[u].sem, 1)
                after(act, l_sig[u], turn, 2)
                act.activation(za[:, 2, :], cv[:, 1, :], ACT.Tanh, scale=uc[:, 8:9]).then_inc(l_exp[u].sem, 1)
                after(act, l_exp[u], turn, 1)
                act.activation(cv[:, 1, :], cv[:, 1, :], ACT.Exp, scale=uc[:, 7:8]).then_inc(l_exp[u].sem, 1)
                fill()
                after(act, l_vec[u], turn, 2)
                act.activation(za[:, 2, :], za[:, 2, :], ACT.Sqrt).then_inc(l_root[u].sem, 1)
                act.activation(za[:, u, :], za[:, u, :], ACT.Silu).then_inc(l_silu[u].sem, 1)
                for _ in range(4):
                    fill()
                round_y(u, turn, za[:, 3, :], l_vec[u], l_high[u])
                fill()

            def odd_turn(turn):
                for u in range(2):
                    f = Filler(ODD(turn), u, FILLS_L, None, evac)
                    lru(u, turn, f)
                    f.finish()

            turns(act, TURNS, odd_turn)
            ple(1, ODD_TAIL, PLE1, 3)
            norm(4, split=False)
            after(act, f_scaled, 0, KD)
            for i in range(2 * NC):
                c = i // 2
                act.wait_ge(f_turned.sem, i + 1)
                if c >= 2:
                    act.wait_ge(stored[c % 2].sem, 16 * (c // 2))
                act.activation(half((w1, w2)[c % 2], i % 2), work[i % 4][:, :], ACT.Copy).then_inc(f_kept.sem, 1)

        @block.vector
        def _(dve):
            def evac(s, place):
                kind, u, n = s.what
                if kind not in "OV":
                    return
                pair = s.pair
                dve.wait_ge(dense_ready.sem, place.ready(s.rank))
                dve.tensor_tensor(half(x[:, n, :], 0), dense[2 * pair][:, :], half(x[:, n, :], 0), ALU.add)
                dve.tensor_tensor(half(x[:, n, :], 1), dense[2 * pair + 1][:, :], half(x[:, n, :], 1), ALU.add)\
                    .then_inc(taken[pair].sem, 1)

            def norm_start(n):
                for h in range(2):
                    after(dve, norm_rooted, n, h + 1)
                    dve.reciprocal(half(w3, h), half(w3, h)).then_inc(norm_inverse.sem, 1)
                after(dve, norm_inverse, n, 2)

            def norm(n):
                norm_start(n)

                def low(k):
                    after(dve, norm_high, n, k + 1)
                    dve.tensor_tensor(xl[:, k, :], (w1, w2)[k % 2][:, :], xh[:, k, :].bitcast(F32), ALU.subtract)\
                        .then_inc(norm_low.sem, 1)

                for k in range(KD):
                    if k >= 2:
                        after(dve, norm_low, n, k - 1)
                    dve.scalar_tensor_tensor(out=(w1, w2)[k % 2][:, :], in0=x[:, k, :],
                                             scalar=cols[:, NORMS[n] + k:NORMS[n] + k + 1], in1=w3[:, :],
                                             op0=ALU.mult, op1=ALU.mult).then_inc(norm_scaled.sem, 1)
                    if k:
                        low(k - 1)
                low(KD - 1)

            build = zb[:, :, :].rearrange("p a b -> p (a b)")[:, 0:(2 * LEVELS + 1) * P].rearrange("p (a b) -> p a b", b=P)
            for k in range(KD):
                dve.wait_ge(x_turned.sem, 2 * k + 2)
                dve.tensor_copy(half(x[:, k, :], 1), dense[2 * (k % 2) + 1][:, :]).then_inc(x_kept[1].sem, 1)
            for h in range(2):
                dve.wait_ge(x_kept[h].sem, KD)
            dve.wait_ge(made.sem, MADE)
            dve.tensor_copy(masks[:, :, :], build).then_inc(masks_ready.sem, 1)
            dve.wait_ge(masks_ready.sem, 1)
            dve.memset(zb[:, :, 0:PAD], 0.0).then_inc(masks_ready.sem, 1)
            norm(0)
            dve.wait_ge(vec_kept.sem, 1)
            lb = cols[:, C_LB:C_LB + HEADS]
            dve.tensor_tensor(lows[:, 0, :], lb, lb, ALU.subtract).then_inc(vec_ready.sem, 1)
            dve.wait_ge(l_lam.sem, 1)
            dve.reciprocal(lows[:, 2, :], lows[:, 1, :]).then_inc(vec_ready.sem, 1)
            dve.wait_ge(vec_ready.sem, 2)
            dve.tensor_tensor(lows[:, 0, :], lows[:, 1, :], lows[:, 2, :], ALU.mult).then_inc(vec_ready.sem, 1)
            dve.wait_ge(vec_ready.sem, 3)
            dve.tensor_tensor(lows[:, 2, :], lows[:, 0, :], lows[:, 0, :], ALU.subtract).then_inc(vec_ready.sem, 1)
            dve.wait_ge(vec_ready.sem, 4)
            dve.tensor_scalar(lows[:, 3, :], lows[:, 2, :], -1.0, 1.0, ALU.mult, ALU.add).then_inc(vec_ready.sem, 1)
            dve.wait_ge(l_lam.sem, 5)
            t0 = pairs(0)
            lam = cols[:, C_ODD + 7 * BLOCKS:C_ODD + 8 * BLOCKS]
            dve.tensor_tensor(t0, t0, unit_cols[:, 0, :], ALU.add).then_inc(vec_ready.sem, 1)
            dve.wait_ge(vec_ready.sem, 6)
            dve.tensor_scalar(lam, t0, -8.0, None, ALU.mult).then_inc(vec_ready.sem, 1)
            dve.wait_ge(l_lam.sem, 6)
            dve.tensor_scalar(tiny[0:HEADS, 3:4], tiny[0:HEADS, 3:4], -1.0, None, ALU.mult).then_inc(vec_ready.sem, 1)
            dve.wait_ge(vec_ready.sem, 8)

            dve.memset(w3[0:HEADS, :], 1.0).then_inc(row_vec.sem, 1)
            dve.wait_ge(row_vec.sem, 1)
            dve.memset(w3[0:HEADS, :].rearrange("p (c t) -> p c t", t=CHUNK)[:, :, 0:1], 0.0).then_inc(row_vec.sem, 1)
            dve.wait_ge(row_step.sem, 7)
            dve.tensor_tensor(w1[0:HEADS, :], w1[0:HEADS, :], w2[0:HEADS, :], ALU.add).then_inc(row_vec.sem, 1)
            dve.wait_ge(row_vec.sem, 3)
            dve.tensor_scalar(w1[0:HEADS, :], w1[0:HEADS, :], tiny[0:HEADS, 3:4], None, ALU.mult).then_inc(row_vec.sem, 1)
            dve.wait_ge(row_vec.sem, 4)
            dve.tensor_tensor_scan(out=rows[0:HEADS, :], data0=w3[0:HEADS, :], data1=w1[0:HEADS, :], initial=0.0,
                                   op0=ALU.mult, op1=ALU.add).then_inc(row_vec.sem, 1)

            def select(out_, mask, data):
                dve.sem_inc(select_begun.sem, 1)
                return dve.copy_predicated(out_, mask, data)

            def over_chunks(n_mask, n, b=None):
                m = masks[:, n_mask, :]
                if b is not None:
                    m = m.rearrange("p (n two b) -> p n two b", two=2, b=b)[:, :, 1, :]
                dims = [list(d) for d in m.ap]
                return bass.AP(m.tensor, m.offset, [dims[0], [0, n]] + dims[1:])

            def by_blocks(t, b):
                return t.rearrange("p (n two b) -> p n two b", two=2, b=b)

            def repeat(v, b):
                dims = [list(d) for d in v.ap]
                return bass.AP(v.tensor, v.offset, dims[:-1] + [[0, b]])

            def head_out(u, turn, o, sq, gate, g_col, fill):
                after(dve, o_rooted[u], turn, 2)
                dve.reciprocal(sq, sq).then_inc(o_scaled[u].sem, 1)
                after(dve, o_scaled[u], turn, 1)
                dve.scalar_tensor_tensor(out=o, in0=o, scalar=g_col, in1=sq, op0=ALU.mult, op1=ALU.mult)\
                    .then_inc(o_scaled[u].sem, 1)
                after(dve, o_scaled[u], turn, 2)
                dve.tensor_tensor(o, o, gate, ALU.mult).then_inc(o_scaled[u].sem, 1)
                fill()
                after(dve, y_high[u], turn, 1)
                dve.tensor_tensor(yl[:, u, :], o, yh[:, u, :].bitcast(F32), ALU.subtract).then_inc(y_ready[u].sem, 1)
                fill()

            def convolve_start(turn):
                uc = unit_cols[:, 1, :]
                taps = cols[:, C_CONV:C_CONV + TAPS * 3 * HEADS].rearrange("p (f j) -> p f j", j=HEADS)
                dve.tensor_copy(uc[:, 0:3 * TAPS], taps[:, :, bass.ds(turn, 1)].rearrange("p f j -> p (f j)"))\
                    .then_inc(b_cols.sem, 1)
                dve.tensor_copy(uc[:, 12:13], cols[:, bass.ds(turn + C_HEAD + HEADS, 1)]).then_inc(b_cols.sem, 1)
                dve.tensor_copy(head_cols[:, 0:2, :],
                                gcols[:, :, :, bass.ds(turn, 1)].rearrange("p a c h -> p a (c h)")).then_inc(b_cols.sem, 1)
                after(dve, b_cols, turn, 3)

            def convolve(turn, m):
                uc = unit_cols[:, 1, :]
                s = next(s for s in EVEN(turn).plan.steps if s.what == ("P", 1, m))
                dve.wait_ge(taken[s.pair].sem, EVEN(turn).taken(s))
                for i in range(TAPS):
                    tap = TAPS - 1 - i
                    src = zb[:, m, tap:tap + T]
                    w = uc[:, 3 * tap + m:3 * tap + m + 1]
                    if i == 0:
                        dve.tensor_scalar(cv[:, m, :], src, w, None, ALU.mult).then_inc(b_conv.sem, 1)
                    else:
                        after(dve, b_conv, turn, TAPS * m + i)
                        dve.scalar_tensor_tensor(out=cv[:, m, :], in0=src, scalar=w, in1=cv[:, m, :],
                                                 op0=ALU.mult, op1=ALU.add).then_inc(b_conv.sem, 1)

            def hgrn(turn, fill):
                uc = unit_cols[:, 0, :]
                after(dve, a_gates, turn, 3)
                dve.tensor_copy(uc[:, 0:2], lows[:, 2:4, bass.ds(turn, 1)].rearrange("p a b -> p (a b)"))\
                    .then_inc(a_bounded.sem, 1)
                dve.tensor_copy(uc[:, 2:3], cols[:, bass.ds(turn + C_HEAD, 1)]).then_inc(a_cols.sem, 1)
                after(dve, a_bounded, turn, 1)
                dve.tensor_scalar(k_a, k_a, uc[:, 1:2], None, ALU.mult).then_inc(a_bounded.sem, 1)
                dve.tensor_scalar(f_a, f_a, uc[:, 1:2], uc[:, 0:1], ALU.mult, ALU.add).then_inc(a_bounded.sem, 1)
                dve.memset(w1[:, :], 0.0)
                after(dve, a_bounded, turn, 3)
                fill()
                after(dve, a_scores, turn, 1)
                dve.tensor_tensor(q_a, q_a, f_a, ALU.mult).then_inc(a_scaled.sem, 1)
                after(dve, a_scaled, turn, 1)
                for h in range(2):
                    select(half(w1, h).rearrange("p (c t) -> p c t", t=P), over_chunks(2 * LEVELS, HC),
                           work[h][:, :].rearrange("p (c t) -> p c t", t=P)).then_inc(a_kept.sem, 1)
                fill()
                for l in range(LEVELS):
                    b = 1 << l
                    after(dve, a_scores, turn, 2 + l)
                    q, k, f = by_blocks(q_a, b), by_blocks(k_a, b), by_blocks(f_a, b)
                    done = 1 + 3 * l
                    dve.tensor_tensor(q[:, :, 1, :], q[:, :, 1, :], repeat(f[:, :, 0, 0:1], b), ALU.mult)\
                        .then_inc(a_scaled.sem, 1)
                    dve.tensor_tensor(k[:, :, 0, :], k[:, :, 0, :], repeat(f[:, :, 1, 0:1], b), ALU.mult)\
                        .then_inc(a_scaled.sem, 1)
                    after(dve, a_scaled, turn, done + 2)
                    dve.tensor_tensor(f[:, :, 0, 0:1], f[:, :, 0, 0:1], f[:, :, 1, 0:1], ALU.mult)\
                        .then_inc(a_scaled.sem, 1)
                    kept = w1[:, :].rearrange("p (c n two b) -> p c n two b", c=NC, two=2, b=b)[:, :, :, 1, :]
                    after(dve, a_kept, turn, 2 + l)
                    select(kept, over_chunks(l, NC, b),
                           work[2 + l % 2][:, :].rearrange("p (c n b) -> p c n b", c=NC, b=b)).then_inc(a_kept.sem, 1)
                    after(dve, a_scaled, turn, done + 3)
                    fill()
                fill()
                for c in range(NC - 1):
                    if c % HC == 0:
                        after(dve, a_kv, turn, c // HC + 1)
                    kv, now = in_half(work[2 + c // HC], c), chunk(w2, c)
                    if c == 0:
                        dve.tensor_copy(now, kv).then_inc(a_state.sem, 1)
                    else:
                        after(dve, a_state, turn, c)
                        dve.scalar_tensor_tensor(out=now, in0=chunk(w2, c - 1), scalar=chunk(f_a, c)[:, 0:1],
                                                 in1=kv, op0=ALU.mult, op1=ALU.add).then_inc(a_state.sem, 1)
                fill()
                convolve_start(turn)
                convolve(turn, 0)
                convolve(turn, 1)
                fill()
                convolve(turn, 2)
                head_out(0, turn, q_a, f_a, gate_a, unit_cols[:, 0, 2:3], fill)

            def gdn(turn, fill):
                uc = unit_cols[:, 1, :]
                for at in (0, 32):
                    dve.tensor_scalar(w2[at:at + HEADS, :], rows[at:at + HEADS, :],
                                      ident[at:at + HEADS, bass.ds(turn + at, 1)], None, ALU.mult)\
                        .then_inc(b_rows.sem, 1)
                fill()
                fill()
                for i in range(2):
                    after(dve, b_rooted, turn, 2 * i + 2)
                    dve.reciprocal(raw[i], raw[i]).then_inc(b_normed.sem, 1)
                    after(dve, b_normed, turn, 2 * i + 1)
                    dve.scalar_tensor_tensor(out=cv[:, i, :], in0=cv[:, i, :], scalar=(P ** -0.5, 1.0)[i],
                                             in1=raw[i], op0=ALU.mult, op1=ALU.mult).then_inc(b_normed.sem, 1)
                after(dve, b_normed, turn, 4)
                after(dve, b_spread, turn, 2)
                for h in range(2):
                    dve.scalar_tensor_tensor(out=half(raw[1], h), in0=half(k_b, h), scalar=-1.0,
                                             in1=work[2 + h][:, :], op0=ALU.mult, op1=ALU.mult)\
                        .then_inc(b_keyed.sem, 1)
                after(dve, b_decay, turn, 2)
                for c in range(NC):
                    dve.tensor_scalar(chunk(raw[2], c), in_half(work[c // HC], c), head_cols[:, 0, c:c + 1], 0.0,
                                      ALU.subtract, ALU.min).then_inc(b_diff.sem, 1)
                for h in range(2):
                    ends = work[h][:, :].rearrange("p (c t) -> p c t", t=P)[:, :, P - 1]
                    dve.tensor_tensor(head_cols[:, 3, h * HC:(h + 1) * HC], ends,
                                      head_cols[:, 0, h * HC:(h + 1) * HC], ALU.subtract).then_inc(b_diff.sem, 1)
                fill()
                after(dve, b_exp, turn, 3)
                up = upper[:, :]
                up = bass.AP(up.tensor, up.offset, [list(up.ap[0]), [0, NC], [1, P]])
                decays = raw[2].rearrange("p (c t) -> p c t", t=P)
                dve.tensor_tensor(decays, decays, up, ALU.mult).then_inc(b_masked.sem, 1)
                dve.scalar_tensor_tensor(out=head_cols[:, 2, :], in0=head_cols[:, 2, :], scalar=-1.0,
                                         in1=head_cols[:, 1, :], op0=ALU.mult, op1=ALU.mult).then_inc(b_cols.sem, 1)
                dve.tensor_copy(head_cols[:, 5, :], raw[0].rearrange("p (c t) -> p c t", t=P)[:, :, P - 1])\
                    .then_inc(b_cols.sem, 1)
                after(dve, b_cols, turn, 5)
                after(dve, b_masked, turn, 1)
                for i in range(2):
                    for h in range(2):
                        after(dve, b_prod, turn, 2 * i + h + 1)
                        dve.tensor_tensor(half(raw[1 + i], h), work[2 * i + h][:, :], half(raw[2], h), ALU.mult)\
                            .then_inc(b_scores.sem, 1)
                fill()
                dve.tensor_tensor(q_b, q_b, raw[0], ALU.mult).then_inc(b_qdec.sem, 1)
                for i, (dst, col) in enumerate(((v_b, 1), (raw[0], 3))):
                    for h in range(2):
                        after(dve, b_turned, turn, 2 * i + h + 1)
                        if i:
                            after(dve, b_qdec, turn, 1)
                        v = head_cols[:, col, h * HC:(h + 1) * HC]
                        v = bass.AP(v.tensor, v.offset, [list(v.ap[0]), list(v.ap[1]), [0, P]])
                        dve.tensor_tensor(half(dst, h).rearrange("p (c t) -> p c t", t=P),
                                          work[2 * i + h][:, :].rearrange("p (c t) -> p c t", t=P), v, ALU.mult)\
                            .then_inc(b_vk.sem, 1)
                fill()

                def grow(t, n_mask, h, data):
                    return select(half(t, h).rearrange("p (c t) -> p c t", t=P), over_chunks(n_mask, HC),
                                  data.rearrange("p (c t) -> p c t", t=P)).then_inc(b_inv.sem, 1)

                after(dve, b_ident, turn, 2)
                for l in range(LEVELS):
                    if l == 0:
                        for h in range(2):
                            after(dve, b_u, turn, h + 1)
                            grow(w1, LEVELS, h, work[2 * h][:, :])
                            grow(w3, 0, h, half(raw[1], h))
                    else:
                        fill()
                        n = 4 * (l - 1)
                        for h in range(2):
                            after(dve, b_inv, turn, 4 * l)
                            if l < LEVELS - 1:
                                after(dve, b_y, turn, n + 2 * h + 1)
                                grow(w1, LEVELS + l, h, work[2 * h + 1][:, :])
                                after(dve, b_y, turn, n + 2 * h + 2)
                            else:
                                after(dve, b_y, turn, n + h + 1)
                            grow(w3, l, h, work[2 * h][:, :])
                    fill()
                for c in range(NC):
                    if c:
                        after(dve, c_ks, turn, c)
                        dve.scalar_tensor_tensor(out=chunk(v_b, c), in0=work[0][:, 0:P], scalar=head_cols[:, 2, c:c + 1],
                                                 in1=chunk(v_b, c), op0=ALU.mult, op1=ALU.add).then_inc(c_r.sem, 1)
                        fill()
                    if c < NC - 1:
                        after(dve, c_kv, turn, c + 1)
                        if c == 0:
                            dve.tensor_copy(state[:, 1, :], work[0][:, 0:P]).then_inc(c_state.sem, 1)
                        else:
                            dve.scalar_tensor_tensor(out=state[:, (c + 1) % 2, :], in0=state[:, c % 2, :],
                                                     scalar=head_cols[:, 5, c:c + 1], in1=work[0][:, 0:P],
                                                     op0=ALU.mult, op1=ALU.add).then_inc(c_state.sem, 1)
                    fill()
                head_out(1, turn, q_b, raw[0], zg[:, :], uc[:, 12:13], fill)
                fill()

            def even_turn(turn):
                for w, (unit, weights) in enumerate(((hgrn, FILLS_A), (gdn, FILLS_B))):
                    f = Filler(EVEN(turn), w, weights, None, evac)
                    unit(turn, f)
                    f.finish()

            turns(dve, HEADS, even_turn)
            Filler(EVEN_TAIL, 0, [1], None, evac)()

            def ple(i, place, n_norm):
                for k in range(KP):
                    for h in range(2):
                        after(dve, p_high, i, 2 * k + h + 1)
                        dve.tensor_tensor(half(yl[:, k, :], h), work[2 * k + h][:, :],
                                          half(yh[:, k, :].bitcast(F32), h), ALU.subtract).then_inc(p_low.sem, 1)
                norm(n_norm)
                for n in range(KD):
                    g, s = (w1, w2)[n % 2][:, :], place.plan.steps[KD + n]
                    dve.wait_ge(taken[s.pair].sem, place.taken(s))
                    dve.tensor_tensor(g, tiles8[n], g, ALU.mult).then_inc(p_prod.sem, 1)
                    after(dve, p_prod, i, n + 1)
                    dve.tensor_tensor(x[:, n, :], x[:, n, :], g, ALU.add).then_inc(p_added.sem, 1)

            ple(0, PLE0, 1)
            after(dve, p_added, 0, KD)
            norm(2)

            def lru(u, turn, fill):
                uc = unit_cols[:, u, :]
                xc, a, gx, th, h_t = cv[:, 0, :], cv[:, 1, :], cv[:, 2, :], za[:, 2, :], za[:, 3, :]
                after(dve, lz_ready[u], turn, 2)
                v = cols[:, C_ODD:C_ODD + 8 * BLOCKS].rearrange("p (f i u) -> p f i u", u=2, i=TURNS)
                dve.tensor_copy(uc[:, 0:8], v[:, :, bass.ds(turn, 1), u].rearrange("p f i -> p (f i)"))\
                    .then_inc(l_cols[u].sem, 1)
                after(dve, l_cols[u], turn, 1)
                for i in range(TAPS):
                    tap = TAPS - 1 - i
                    src = zb[:, u, tap:tap + T]
                    if i == 0:
                        dve.tensor_scalar(uc[:, 8:9], uc[:, 7:8], -1.0, None, ALU.mult)
                        dve.tensor_scalar(xc, src, uc[:, tap:tap + 1], uc[:, 4:5], ALU.mult, ALU.add)\
                            .then_inc(l_conv[u].sem, 1)
                    else:
                        after(dve, l_conv[u], turn, i)
                        dve.scalar_tensor_tensor(out=xc, in0=src, scalar=uc[:, tap:tap + 1], in1=xc,
                                                 op0=ALU.mult, op1=ALU.add).then_inc(l_conv[u].sem, 1)
                fill()
                fill()
                after(dve, l_exp[u], turn, 2)
                dve.tensor_tensor(h_t, a, a, ALU.mult).then_inc(l_vec[u].sem, 1)
                after(dve, l_vec[u], turn, 1)
                dve.scalar_tensor_tensor(out=th, in0=h_t, scalar=1.0, in1=th, op0=ALU.add, op1=ALU.mult)\
                    .then_inc(l_vec[u].sem, 1)
                after(dve, l_sig[u], turn, 4)
                dve.tensor_tensor(gx, gx, xc, ALU.mult).then_inc(l_vec[u].sem, 1)
                fill()
                after(dve, l_root[u], turn, 1)
                dve.memset(th[:, 0:1], 1.0).then_inc(l_vec[u].sem, 1)
                after(dve, l_vec[u], turn, 4)
                dve.tensor_tensor(gx, gx, th, ALU.mult).then_inc(l_vec[u].sem, 1)
                fill()
                after(dve, l_vec[u], turn, 5)
                dve.tensor_tensor_scan(out=h_t, data0=a, data1=gx, initial=0.0, op0=ALU.mult, op1=ALU.add)\
                    .then_inc(l_vec[u].sem, 1)
                fill()
                after(dve, l_vec[u], turn, 6)
                after(dve, l_silu[u], turn, 1)
                dve.tensor_tensor(h_t, h_t, za[:, u, :], ALU.mult).then_inc(l_vec[u].sem, 1)
                fill()
                after(dve, l_high[u], turn, 1)
                dve.tensor_tensor(yl[:, u, :], h_t, yh[:, u, :].bitcast(F32), ALU.subtract).then_inc(l_y[u].sem, 1)
                fill()

            def odd_turn(turn):
                for u in range(2):
                    f = Filler(ODD(turn), u, FILLS_L, None, evac)
                    lru(u, turn, f)
                    f.finish()

            turns(dve, TURNS, odd_turn)
            Filler(ODD_TAIL, 0, [1], None, evac)()
            ple(1, PLE1, 3)
            after(dve, p_added, 1, KD)
            norm_start(4)
            for k in range(KD):
                dve.scalar_tensor_tensor(out=tiles8[k], in0=x[:, k, :], scalar=cols[:, NORMS[4] + k:NORMS[4] + k + 1],
                                         in1=w3[:, :], op0=ALU.mult, op1=ALU.mult).then_inc(f_scaled.sem, 1)


_INS = ["x", "p", "even_norm", "even_w_in", "hgrn_lb_logits", "gdn_conv_w", "gdn_a_log", "gdn_dt_bias",
        "even_head_norm", "even_w_out", "odd_norm", "odd_w_in", "lru_conv_w", "lru_conv_b", "lru_w_a",
        "lru_b_a", "lru_w_x", "lru_b_x", "lru_lambda", "odd_w_out", "ple_norm", "ple_gate_w", "ple_proj_w",
        "final_norm"]


def kernel(**inputs):
    import numpy as _np
    import concourse.bacc as _bacc
    from concourse import mybir as _mybir
    from concourse.bass_utils import run_bass_kernel_spmd as _run

    nc = _bacc.Bacc("TRN2", target_bir_lowering=False, num_devices=1)
    arrays, args = {}, []
    for name in _INS:
        a = _np.ascontiguousarray(inputs[name])
        arrays[f"in_{name}_dram"] = a
        args.append(nc.dram_tensor(f"in_{name}_dram", a.shape, _mybir.dt.from_np(a.dtype), kind="ExternalInput").ap())
    shape = inputs["x"].shape
    args.append(nc.dram_tensor("out_0_dram", shape, _mybir.dt.from_np(_np.dtype("float32")), kind="ExternalOutput").ap())
    build_trunk(nc, *args)
    r = _run(nc, [arrays], core_ids=[0])
    return r.results[0]["out_0_dram"]
```
